# Optimizing a Trainium2 kernel written in Bass

```python
import math
import jax
import jax.numpy as jnp
from jax import lax
import numpy as np

D_MODEL = 1024
BATCH = 1
SEQ = 512
DEPTH = 1

GRID_W = 64
CTX_LEN = 256
EPS = 1e-6
N_MOD = 6
F32 = jnp.float32

GLA_HEADS = 4
GLA_DK = 128
GLA_DV = 256
GLA_QK = GLA_HEADS * GLA_DK
GLA_V = GLA_HEADS * GLA_DV
GLA_RANK = 16
GLA_TAU = 16.0
GLA_CHUNK = 64

FNET_GROUPS = 4
FNET_WIDTH = D_MODEL
FNET_GROUP_DIM = FNET_WIDTH // FNET_GROUPS

SSD_INNER = 2 * D_MODEL
SSD_HEADDIM = 64
SSD_HEADS = SSD_INNER // SSD_HEADDIM
SSD_GROUPS = 4
SSD_STATE = 128
SSD_CONV = 5
SSD_CONV_DIM = SSD_INNER + 2 * SSD_GROUPS * SSD_STATE
SSD_CHUNK = 64

N_EXPERTS = 16
N_EXPERT_GROUPS = 4
EXPERTS_PER_GROUP = N_EXPERTS // N_EXPERT_GROUPS
TOP_K = 2
D_FF_EXPERT = 512

PROJ_SIZES = (
    GLA_QK,
    GLA_QK,
    GLA_V,
    GLA_V,
    GLA_RANK,
    GLA_RANK,
    FNET_WIDTH,
    SSD_INNER,
    SSD_CONV_DIM,
    SSD_HEADS,
    SSD_HEADS,
    D_MODEL,
    D_MODEL,
    D_MODEL,
)
D_IN_PROJ = sum(PROJ_SIZES)

kernel_name = 'hybrid_gla_fnet_ssd_moe_diffusion_trunk'

def rms_norm(x, g):
    xf = x.astype(F32)
    y = xf * lax.rsqrt(jnp.mean(xf * xf, axis=-1, keepdims=True) + EPS)
    return (y * g.astype(F32)).astype(x.dtype)

def modulate(x, g, shift, scale):
    return rms_norm(x, g) * (1.0 + scale) + shift

def grid_sincos(n_tokens, dim):
    rows = n_tokens // GRID_W
    row = jnp.broadcast_to(jnp.arange(rows)[:, None], (rows, GRID_W)).reshape(-1).astype(F32)
    col = jnp.broadcast_to(jnp.arange(GRID_W)[None, :], (rows, GRID_W)).reshape(-1).astype(F32)
    quarter = dim // 4
    freqs = jnp.exp(-math.log(10000.0) * jnp.arange(quarter, dtype=F32) / quarter)
    ar = row[:, None] * freqs
    ac = col[:, None] * freqs
    return jnp.concatenate([jnp.sin(ar), jnp.cos(ar), jnp.sin(ac), jnp.cos(ac)], axis=-1)

def project(h, w_in):
    parts, start = [], 0
    for size in PROJ_SIZES:
        parts.append(h @ w_in[:, start:start + size])
        start += size
    return parts

def gla_prepare(q, k, v, a_lr_f, a_lr_b, a_w, a_b):
    B, T, _ = q.shape

    def heads(t, d):
        return t.reshape(B, T, GLA_HEADS, d).transpose(0, 2, 1, 3)

    q = heads(q, GLA_DK) * (GLA_DK ** -0.5)
    k = heads(k, GLA_DK)
    v = heads(v, GLA_DV)
    la_f = heads(jax.nn.log_sigmoid((a_lr_f @ a_w[0] + a_b[0]).astype(F32)) / GLA_TAU, GLA_DK)
    la_b = heads(jax.nn.log_sigmoid((a_lr_b @ a_w[1] + a_b[1]).astype(F32)) / GLA_TAU, GLA_DK)
    return q, k, v, la_f, la_b

def gla_chunked(q, k, v, log_a, s0):
    B, H, T, dk = q.shape
    dv = v.shape[-1]
    L = GLA_CHUNK
    n = T // L
    q = q.astype(F32).reshape(B, H, n, L, dk)
    k = k.astype(F32).reshape(B, H, n, L, dk)
    v = v.astype(F32).reshape(B, H, n, L, dv)
    b = jnp.cumsum(log_a.astype(F32).reshape(B, H, n, L, dk), axis=3)
    b_ref = b[:, :, :, L // 2 - 1:L // 2]
    b_last = b[:, :, :, L - 1:]
    causal = jnp.tril(jnp.ones((L, L), dtype=bool))
    scores = jnp.einsum('bhnld,bhnsd->bhnls', q * jnp.exp(b - b_ref), k * jnp.exp(b_ref - b))
    scores = jnp.where(causal, scores, 0.0)
    o_intra = jnp.einsum('bhnls,bhnsv->bhnlv', scores, v)
    chunk_kv = jnp.einsum('bhnsd,bhnsv->bhndv', k * jnp.exp(b_last - b), v)
    chunk_decay = jnp.exp(b_last[:, :, :, 0])

    def step(s, inp):
        dec, kv = inp
        return dec[..., None] * s + kv, s

    s_final, s_prev = lax.scan(step, s0.astype(F32),
                               (jnp.moveaxis(chunk_decay, 2, 0), jnp.moveaxis(chunk_kv, 2, 0)))
    s_prev = jnp.moveaxis(s_prev, 0, 2)
    o_inter = jnp.einsum('bhnld,bhndv->bhnlv', q * jnp.exp(b), s_prev)
    return (o_intra + o_inter).reshape(B, H, T, dv), s_final

def gla_output(o, r, norm_g, proj):
    B, H, T, dv = o.shape
    o = rms_norm(o, norm_g).transpose(0, 2, 1, 3).reshape(B, T, GLA_V).astype(r.dtype)
    return (o * jax.nn.silu(r)) @ proj

def fourier_mix(u):
    B, T, _ = u.shape
    ug = u.astype(F32).reshape(B, T, FNET_GROUPS, FNET_GROUP_DIM)
    y = jnp.fft.fft2(ug, axes=(1, 3), norm='ortho').real
    return y.reshape(B, T, FNET_WIDTH).astype(u.dtype)

def centred_dwconv(x, w, b):
    pad = w.shape[0] // 2
    y = lax.conv_general_dilated(x, w[:, None, :], window_strides=(1,), padding=((pad, pad),),
                                 dimension_numbers=('NWC', 'WIO', 'NWC'), feature_group_count=x.shape[-1])
    return y + b

def ssd_prepare(xbc, dtf_raw, dtb_raw, conv_w, conv_b, dt_bias):
    B, T, _ = xbc.shape
    xbc = jax.nn.silu(centred_dwconv(xbc, conv_w, conv_b))
    gn = SSD_GROUPS * SSD_STATE
    xs = xbc[..., :SSD_INNER].reshape(B, T, SSD_HEADS, SSD_HEADDIM)
    bm = xbc[..., SSD_INNER:SSD_INNER + gn].reshape(B, T, SSD_GROUPS, SSD_STATE)
    cm = xbc[..., SSD_INNER + gn:].reshape(B, T, SSD_GROUPS, SSD_STATE)
    dt_f = jax.nn.softplus(dtf_raw.astype(F32) + dt_bias[0].astype(F32))
    dt_b = jax.nn.softplus(dtb_raw.astype(F32) + dt_bias[1].astype(F32))
    return xs, bm, cm, dt_f, dt_b

def ssd_chunked(x, dt, a, bm, cm, s0):
    B, T, H, P = x.shape
    G, N = bm.shape[2], bm.shape[3]
    J = H // G
    L = SSD_CHUNK
    n = T // L
    xdt = (x.astype(F32) * dt[..., None]).reshape(B, n, L, G, J, P)
    a_cs = jnp.cumsum((dt * a).reshape(B, n, L, G, J), axis=2).transpose(0, 1, 3, 4, 2)
    bm = bm.astype(F32).reshape(B, n, L, G, N)
    cm = cm.astype(F32).reshape(B, n, L, G, N)
    causal = jnp.tril(jnp.ones((L, L), dtype=bool))
    seg = a_cs[..., :, None] - a_cs[..., None, :]
    decay = jnp.exp(jnp.where(causal, seg, -jnp.inf))
    cb = jnp.einsum('bclgn,bcsgn->bcgls', cm, bm)
    y_diag = jnp.einsum('bcgls,bcgjls,bcsgjp->bclgjp', cb, decay, xdt)
    decay_to_end = jnp.exp(a_cs[..., -1:] - a_cs)
    states = jnp.einsum('bcsgn,bcgjs,bcsgjp->bcgjpn', bm, decay_to_end, xdt)
    chunk_decay = jnp.exp(a_cs[..., -1])

    def step(s, inp):
        dec, st = inp
        return dec[..., None, None] * s + st, s

    s_final, s_prev = lax.scan(step, s0.astype(F32).reshape(B, G, J, P, N),
                               (jnp.moveaxis(chunk_decay, 1, 0), jnp.moveaxis(states, 1, 0)))
    s_prev = jnp.moveaxis(s_prev, 0, 1)
    y_off = jnp.einsum('bclgn,bcgjpn,bcgjl->bclgjp', cm, s_prev, jnp.exp(a_cs))
    y = (y_diag + y_off).reshape(B, T, H, P)
    return y, s_final.reshape(B, H, P, N)

def ssd_output(y, xs, z, d_skip, norm_g, proj):
    B, T = z.shape[:2]
    y = y + d_skip.astype(F32)[:, None] * xs.astype(F32)
    y = y.reshape(B, T, SSD_INNER).astype(z.dtype)
    return rms_norm(y * jax.nn.silu(z), norm_g) @ proj

def merge_branches(g_a, g_b, g_c, y_a, y_b, y_c, w_out):
    y = jax.nn.sigmoid(g_a) * y_a + jax.nn.sigmoid(g_b) * y_b + jax.nn.sigmoid(g_c) * y_c
    return y @ w_out

def token_mixers(hc, hl, ctx_out, w_in, gla_a_w, gla_a_b, gla_norm_g, gla_proj, fnet_proj,
                 ssd_conv_w, ssd_conv_b, ssd_dt_bias, ssd_a_log, ssd_d, ssd_norm_g, ssd_proj, w_out):
    B = hl.shape[0]
    pc = project(hc, w_in)
    pl = project(hl, w_in)

    gc = gla_prepare(pc[0], pc[1], pc[2], pc[4], pc[5], gla_a_w, gla_a_b)
    gl = gla_prepare(pl[0], pl[1], pl[2], pl[4], pl[5], gla_a_w, gla_a_b)
    zero_gla = jnp.zeros((B, GLA_HEADS, GLA_DK, GLA_DV), F32)
    oc_f, gst_f = gla_chunked(gc[0], gc[1], gc[2], gc[3], zero_gla)
    oc_b, gst_b = gla_chunked(jnp.flip(gc[0], 2), jnp.flip(gc[1], 2), jnp.flip(gc[2], 2),
                              jnp.flip(gc[4], 2), zero_gla)
    ol_f, _ = gla_chunked(gl[0], gl[1], gl[2], gl[3], gst_f)
    ol_b, _ = gla_chunked(jnp.flip(gl[0], 2), jnp.flip(gl[1], 2), jnp.flip(gl[2], 2),
                          jnp.flip(gl[4], 2), gst_b)
    ya_l = gla_output(ol_f + jnp.flip(ol_b, 2), pl[3], gla_norm_g, gla_proj)

    yb_l = fourier_mix(pl[6]) @ fnet_proj

    a_f = -jnp.exp(ssd_a_log[0].astype(F32))
    a_b = -jnp.exp(ssd_a_log[1].astype(F32))
    sc = ssd_prepare(pc[8], pc[9], pc[10], ssd_conv_w, ssd_conv_b, ssd_dt_bias)
    sl = ssd_prepare(pl[8], pl[9], pl[10], ssd_conv_w, ssd_conv_b, ssd_dt_bias)
    zero_ssd = jnp.zeros((B, SSD_HEADS, SSD_HEADDIM, SSD_STATE), F32)
    yc_f, sst_f = ssd_chunked(sc[0], sc[3], a_f, sc[1], sc[2], zero_ssd)
    yc_b, sst_b = ssd_chunked(jnp.flip(sc[0], 1), jnp.flip(sc[4], 1), a_b,
                              jnp.flip(sc[1], 1), jnp.flip(sc[2], 1), zero_ssd)
    yl_f, _ = ssd_chunked(sl[0], sl[3], a_f, sl[1], sl[2], sst_f)
    yl_b, _ = ssd_chunked(jnp.flip(sl[0], 1), jnp.flip(sl[4], 1), a_b,
                          jnp.flip(sl[1], 1), jnp.flip(sl[2], 1), sst_b)
    yc_l = ssd_output(yl_f + jnp.flip(yl_b, 1), sl[0], pl[7], ssd_d, ssd_norm_g, ssd_proj)

    out_l = merge_branches(pl[11], pl[12], pl[13], ya_l, yb_l, yc_l, w_out)
    if not ctx_out:
        return None, out_l
    ya_c = gla_output(oc_f + jnp.flip(oc_b, 2), pc[3], gla_norm_g, gla_proj)
    yb_c = fourier_mix(pc[6]) @ fnet_proj
    yc_c = ssd_output(yc_f + jnp.flip(yc_b, 1), sc[0], pc[7], ssd_d, ssd_norm_g, ssd_proj)
    out_c = merge_branches(pc[11], pc[12], pc[13], ya_c, yb_c, yc_c, w_out)
    return out_c, out_l

def routed_moe(h, router_w, router_b, w1, w3, w2):
    scores = jax.nn.sigmoid((h @ router_w).astype(F32))
    sel = (scores + router_b.astype(F32)).reshape(-1, N_EXPERT_GROUPS, EXPERTS_PER_GROUP)
    grp_score = jnp.sum(lax.top_k(sel, TOP_K)[0], axis=-1)
    best = jnp.argmax(grp_score, axis=-1)
    in_group = jnp.arange(N_EXPERT_GROUPS)[None, :, None] == best[:, None, None]
    masked = jnp.where(in_group, sel, -jnp.inf).reshape(-1, N_EXPERTS)
    _, idx = lax.top_k(masked, TOP_K)
    w = jnp.take_along_axis(scores, idx, axis=-1)
    w = w / jnp.sum(w, axis=-1, keepdims=True)
    gate = jnp.sum(jax.nn.one_hot(idx, N_EXPERTS, dtype=F32) * w[..., None], axis=1).astype(h.dtype)
    out = jnp.zeros_like(h)
    for e in range(N_EXPERTS):
        he = jax.nn.silu(h @ w1[e]) * (h @ w3[e])
        out = out + gate[:, e:e + 1] * (he @ w2[e])
    return out

def setup_inputs(seed: int = 0) -> dict:
    key = jax.random.key(seed)
    keys = jax.random.split(key, 32)
    counter = [0]

    def nk():
        counter[0] += 1
        return keys[counter[0] - 1]

    def nrm(shape, scale):
        return scale * jax.random.normal(nk(), shape, F32)

    def gain(shape):
        return 1.0 + 0.1 * jax.random.normal(nk(), shape, F32)

    D = D_MODEL
    dt0 = jnp.exp(jax.random.uniform(nk(), (DEPTH, 2, SSD_HEADS), F32,
                                     minval=math.log(1e-3), maxval=math.log(1e-1)))
    return {
        'x': nrm((BATCH, SEQ, D), 1.0),
        'c': nrm((BATCH, D), 1.0),
        'ctx': nrm((BATCH, CTX_LEN, D), 1.0),
        'c_ctx': nrm((D,), 1.0),
        'ada_w': nrm((DEPTH, D, N_MOD * D), 0.5 * D ** -0.5),
        'ada_b': nrm((DEPTH, N_MOD * D), 0.01),
        'norm1_g': gain((DEPTH, D)),
        'norm2_g': gain((DEPTH, D)),
        'w_in': nrm((DEPTH, D, D_IN_PROJ), D ** -0.5),
        'gla_a_w': nrm((DEPTH, 2, GLA_RANK, GLA_QK), GLA_RANK ** -0.5),
        'gla_a_b': nrm((DEPTH, 2, GLA_QK), 0.1),
        'gla_norm_g': gain((DEPTH, GLA_DV)),
        'gla_proj': nrm((DEPTH, GLA_V, D), GLA_V ** -0.5),
        'fnet_proj': nrm((DEPTH, FNET_WIDTH, D), FNET_WIDTH ** -0.5),
        'ssd_conv_w': nrm((DEPTH, SSD_CONV, SSD_CONV_DIM), SSD_CONV ** -0.5),
        'ssd_conv_b': nrm((DEPTH, SSD_CONV_DIM), 0.01),
        'ssd_dt_bias': dt0 + jnp.log(-jnp.expm1(-dt0)),
        'ssd_a_log': jnp.log(jax.random.uniform(nk(), (DEPTH, 2, SSD_HEADS), F32, minval=1.0, maxval=16.0)),
        'ssd_d': gain((DEPTH, SSD_HEADS)),
        'ssd_norm_g': gain((DEPTH, SSD_INNER)),
        'ssd_proj': nrm((DEPTH, SSD_INNER, D), SSD_INNER ** -0.5),
        'w_out': nrm((DEPTH, D, D), D ** -0.5),
        'router_w': nrm((D, N_EXPERTS), D ** -0.5),
        'router_b': nrm((N_EXPERTS,), 0.01),
        'exp_w1': nrm((DEPTH, N_EXPERTS, D, D_FF_EXPERT), D ** -0.5),
        'exp_w3': nrm((DEPTH, N_EXPERTS, D, D_FF_EXPERT), D ** -0.5),
        'exp_w2': nrm((DEPTH, N_EXPERTS, D_FF_EXPERT, D), D_FF_EXPERT ** -0.5),
        'final_g': gain((D,)),
    }

def reference(x, c, ctx, c_ctx, ada_w, ada_b, norm1_g, norm2_g, w_in, gla_a_w, gla_a_b, gla_norm_g,
              gla_proj, fnet_proj, ssd_conv_w, ssd_conv_b, ssd_dt_bias, ssd_a_log, ssd_d, ssd_norm_g,
              ssd_proj, w_out, router_w, router_b, exp_w1, exp_w3, exp_w2, final_g):
    B, T, D = x.shape
    xl = x + grid_sincos(T, D).astype(x.dtype)
    xc = ctx
    c_act = jax.nn.silu(c)
    cc_act = jax.nn.silu(c_ctx)[None]
    for l in range(DEPTH):
        ctx_out = l < DEPTH - 1
        mod_l = jnp.split((c_act @ ada_w[l] + ada_b[l])[:, None, :], N_MOD, axis=-1)
        mod_c = jnp.split((cc_act @ ada_w[l] + ada_b[l])[:, None, :], N_MOD, axis=-1)
        hl = modulate(xl, norm1_g[l], mod_l[0], mod_l[1])
        hc = modulate(xc, norm1_g[l], mod_c[0], mod_c[1])
        yc, yl = token_mixers(hc, hl, ctx_out, w_in[l], gla_a_w[l], gla_a_b[l], gla_norm_g[l], gla_proj[l],
                              fnet_proj[l], ssd_conv_w[l], ssd_conv_b[l], ssd_dt_bias[l], ssd_a_log[l],
                              ssd_d[l], ssd_norm_g[l], ssd_proj[l], w_out[l])
        xl = xl + mod_l[2] * yl
        hl = modulate(xl, norm2_g[l], mod_l[3], mod_l[4])
        if ctx_out:
            xc = xc + mod_c[2] * yc
            hc = modulate(xc, norm2_g[l], mod_c[3], mod_c[4])
            n_c = hc.shape[0] * hc.shape[1]
            y = routed_moe(jnp.concatenate([hc.reshape(-1, D), hl.reshape(-1, D)], axis=0),
                           router_w, router_b, exp_w1[l], exp_w3[l], exp_w2[l])
            xc = xc + mod_c[5] * y[:n_c].reshape(hc.shape)
            xl = xl + mod_l[5] * y[n_c:].reshape(hl.shape)
        else:
            y = routed_moe(hl.reshape(-1, D), router_w, router_b, exp_w1[l], exp_w3[l], exp_w2[l])
            xl = xl + mod_l[5] * y.reshape(hl.shape)
    return rms_norm(xl, final_g)


_drawn_inputs = setup_inputs


def setup_inputs(seed=0):
    import zlib

    import numpy as np

    out = dict(_drawn_inputs(seed))
    spreads = {}
    factors = {'ctx': 3.999,
     'c_ctx': 3.807,
     'gla_a_b': 3.621,
     'gla_norm_g': 2.941,
     'ssd_conv_b': 32.183,
     'ssd_d': 18.561,
     'ssd_norm_g': 3.36,
     'router_b': 3.275}
    for name, (base, spread) in spreads.items():
        noise = np.random.default_rng([zlib.crc32(name.encode()), seed]).standard_normal(out[name].shape)
        drawn = base * np.exp(spread * noise) if base else spread * noise
        out[name] = jnp.asarray(drawn.astype(out[name].dtype))
    for name, factor in factors.items():
        out[name] = (out[name] * factor).astype(out[name].dtype)
    return out
```

```python
from contextlib import ExitStack

import numpy as np

import concourse.bass as bass
from concourse import mybir

F32 = mybir.dt.float32
BF16 = mybir.dt.bfloat16
ALU = mybir.AluOpType
ACT = mybir.ActivationFunctionType
AX = mybir.AxisListType

P = 128
D = 1024
T = 512
C = 256
NT = C + T
KD = D // P
TL = T // P
TC = C // P
TT = TL + TC
EPS = 1e-6
N_MOD = 6
GRID_W = 64

GH, GDK, GDV = 4, 128, 256
GQK, GV, GR = GH * GDK, GH * GDV, 16
TAU = 16.0

SI, SHD, SH, SG, SN, SK = 2048, 64, 32, 4, 128, 5
HPG = SH // SG
GW = HPG * SHD
SGN = SG * SN
SCD = SI + 2 * SGN

NE, NG, EPG, FF = 16, 4, 4, 512

SIZES = (GQK, GQK, GV, GV, GR, GR, D, SI, SCD, SH, SH, D, D, D)
OFF = [sum(SIZES[:i]) for i in range(len(SIZES) + 1)]
Q0, K0, V0, R0, LR0, _, U0, Z0, X0, DT0, _, GA0, GB0, GC0, D_IN = OFF
B0, C0 = X0 + SI, X0 + SI + SGN

FG = D // 4
BIG = 1e30


def spans(sizes):
    at, out = 0, {}
    for name, n in sizes:
        out[name] = (at, at + n)
        at += n
    return out, at


COLS, NCOL = spans([("c", 2 * KD), ("ada_b", N_MOD * KD), ("norm1", KD), ("norm2", KD), ("a_b", 2 * GH),
                    ("gla_norm", GDV // P), ("conv_w", SCD // P * SK), ("conv_b", SCD // P), ("ssd_norm", SI // P)])
ROWS, NROW = spans([("dt_bias", 2 * SH), ("a_log", 2 * SH), ("ssd_d", SH), ("router_b", NE),
                    ("first16", NE), ("first4", NG)])
SQ, NSQ = spans([("ident", P), ("upto", P), ("from", P), ("ones", P)])


def build(nc, a, out):
    with ExitStack() as ctx:
        def sem(name):
            return ctx.enter_context(nc.semaphore(name))

        W = 53100
        arena = ctx.enter_context(nc.sbuf_tensor("arena", [P, W], F32))
        psum = ctx.enter_context(nc.psum_tensor("psum", [P, 8 * 512], F32))
        top = [0]

        def view(off, dims):
            n = int(np.prod(dims))
            v = arena[:, off:off + n]
            if len(dims) == 1:
                return v
            names = "abcde"[:len(dims)]
            return v.rearrange(f"p ({' '.join(names)}) -> p {' '.join(names)}", **dict(zip(names, dims)))

        def alloc(*dims):
            off = top[0]
            top[0] += int(np.prod(dims))
            top[0] += top[0] % 2
            assert top[0] <= W, top[0]
            return view(off, dims)

        NS = 3
        ring = [alloc(8 * 512) for _ in range(NS)]
        col = alloc(NCOL)
        row = alloc(NROW)
        sq = alloc(NSQ)
        identb = alloc(P // 2).bitcast(BF16)
        selb = alloc(SH // 2).bitcast(BF16)
        self_ = alloc(SH)
        wsmall = alloc(KD, 2 * GR + 2 * SH)
        mod = alloc(N_MOD * KD, 2)
        modA = alloc(3, KD)
        small = alloc(64)
        base = top[0]
        hT = alloc(KD, NT)
        phase_base = top[0]

        def c_(name):
            return col[:, COLS[name][0]:COLS[name][1]]

        def r_(name):
            return row[:, ROWS[name][0]:ROWS[name][1]]

        def s_(name):
            return sq[:, SQ[name][0]:SQ[name][1]]

        ident = s_("ident")
        mask = [s_("upto"), s_("from")]
        ones = s_("ones")

        xs = alloc(TT, D)
        pos = alloc(TL, D)
        junk = alloc(D)
        top[0] = phase_base
        dt = alloc(TT, 2 * SH)
        acs = alloc(TT, 2 * SH)
        eacs = alloc(TT, 2 * SH)
        wend = alloc(TT, 2 * SH)
        eend = alloc(TT, 2 * SH)
        nega = alloc(2 * SH)
        tmpd = [alloc(TT, 2 * SH) for _ in range(2)]
        acs3 = alloc(TL * 2 * 3 * SH // 2).bitcast(BF16).rearrange("p (t d s h) -> p t d s h", t=TL, d=2, s=3)
        rowsT = alloc(2 * T // 2).bitcast(BF16).rearrange("p (d t) -> p d t", d=2)
        RAW = C + T + 8
        LAT = C + 6
        raw = [alloc(RAW) for _ in range(2)]
        cacc = alloc(RAW)
        xcT = alloc(NT)
        BT = alloc(NT)
        CT = alloc(T)
        Btok = alloc(TT, P)
        xtok = alloc(TT, GW)
        xw = [alloc(GW) for _ in range(2)]
        xdt = alloc(TL, GW)
        yacc = alloc(TL, GW)
        cb = [alloc(TL, P) for _ in range(2)]
        NM = 4
        mm = [alloc(TL, P) for _ in range(NM)]
        S = [alloc(GW) for _ in range(2)]
        vtmp = alloc(GW)
        sz = alloc(GW)
        yT = alloc(SI // P, T)
        ssq = alloc(TL, SG)
        rrow = alloc(T)
        res = alloc(TL, 2 * SH)
        top[0] = phase_base
        gateT = alloc(KD, T)
        mT = alloc(KD, T)
        gate_top = top[0]

        top[0] = gate_top
        qT = alloc(GH, T)
        kT = alloc(GH, NT)
        vtok = alloc(TT, GV)
        otok = alloc(TL, GV)
        lr2 = alloc(2, NT)
        aw = alloc(2, GQK)
        zb = alloc(NT)
        eb = alloc(NT)
        wb = alloc(NT)
        lb = alloc(NT)
        pc = alloc(TT, P + 1)
        dd = lb.rearrange("p (t l) -> p t l", t=TT)
        eq = alloc(TL, P)
        ek = alloc(TT, P)
        ekT = zb.rearrange("p (t l) -> p t l", t=TT)
        sc = alloc(TL, P)
        st = [alloc(GDV) for _ in range(2)]
        sadd = alloc(GDV)
        ea = alloc(TT)
        ebb = alloc(TT)
        fac = alloc(TT)
        dref = alloc(TT)
        gss = alloc(TL, GH)

        top[0] = gate_top
        uT = alloc(KD, T)
        ue = alloc(KD, T // 2)
        uo = alloc(KD, T // 2)
        At = alloc(TL, D)
        fT = alloc(TL, T)
        fC = alloc(2, FG)
        fS = alloc(2, FG)
        fyT = alloc(KD, T)
        top[0] = base
        xr = alloc(TL, D)
        g1row = alloc(D)
        g2row = alloc(D)
        assert top[0] <= phase_base
        pos2 = view(phase_base, (TL, D))
        top[0] = gate_top
        frow = alloc(D)
        h2T = alloc(KD, T)
        yo = alloc(TL, D)
        rw = alloc(KD, NE)
        heT = alloc(FF // P, T)
        sg = [alloc(T) for _ in range(2)]
        score = alloc(TL, NE)
        sel = alloc(TL, NE)
        gate = alloc(TL, NE)
        ra = alloc(TL, NE)
        rb = alloc(TL, NE)
        rc = alloc(TL, NE)
        junk2 = alloc(D)
        v_off = gate_top + GH * T + GH * NT
        oT = view(v_off, (KD, T))

        full = [sem(f"bank{b}_full") for b in range(8)]
        free = [sem(f"bank{b}_free") for b in range(8)]
        strip_in = [sem(f"strip{s}_in") for s in range(NS)]
        made = {}

        def S_(name):
            if name not in made:
                made[name] = sem(name)
            return made[name]

        turn = [0] * 8
        owner = [None] * 8
        place = {}
        nxt = {}

        def bank(key):
            b, n, _ = place[key]
            return psum[:, b * 512:(b + n) * 512]

        def is_full(key):
            return full[place[key][0]], place[key][2] + 1

        def is_free(key):
            return free[place[key][0]], place[key][2] + 1

        def open_(pe, key, n=1, lo=0, hi=8):
            b = nxt.get((lo, hi), lo)
            if b + n > hi:
                b = lo
            nxt[(lo, hi)] = b + n if b + n < hi else lo
            for o in dict.fromkeys(owner[b:b + n]):
                if o is not None:
                    pe.wait_ge(*is_free(o))
            assert key not in place, key
            place[key] = (b, n, turn[b])
            turn[b] += 1
            owner[b:b + n] = [key] * n
            return bank(key)

        strips = []

        def strip(pe, pieces):
            n = len(strips)
            strips.append([pieces, None])
            pe.wait_ge(strip_in[n % NS], 16 * sum(len(strips[i][0]) for i in range(n % NS, n + 1, NS)))
            return ring[n % NS]

        def strip_used(key):
            strips[-1][1] = key

        def w_cols(w, c0, n=512, r0=0, rows=D):
            return w[r0:r0 + rows, c0:c0 + n].rearrange("(k p) n -> p k n", p=P)

        def full_strip(pe, w, c0, n=512, r0=0, rows=D):
            k = rows // P
            slot = strip(pe, [(lambda s: s[:, 0:k * n].rearrange("p (k n) -> p k n", k=k), w_cols(w, c0, n, r0, rows))])
            return slot[:, 0:k * n].rearrange("p (k n) -> p k n", k=k)

        w_in = a["w_in"][0]
        ada_w = a["ada_w"][0]

        block = ctx.enter_context(nc.Block())
        ENG = 3

        def phase_end(eng, n):
            eng.drain().then_inc(S_("phase_done"), 1)
            eng.wait_ge(S_("phase_done"), ENG * n)

        def x_turn(pe, g, m):
            pe.wait_ge(S_("xc_ready"), g * 4 + m + 1)
            for half in range(2):
                key = ("xtok", g, m, half)
                ps = open_(pe, key)
                for t in range(3):
                    tt = half * 3 + t
                    ins = nc.tensor.transpose(ps[:, t * P:(t + 1) * P], xcT[:, tt * P:(tt + 1) * P], ident)
                ins.then_inc(is_full(key)[0], 1)

        def gla_z(pe, h, d):
            pe.wait_ge(*is_free(("lr", 1)))
            key = ("gz", h * 2 + d)
            ps = open_(pe, key, 2, 0, 2)
            for c0, c1 in ((0, T), (T, NT)):
                ins = nc.tensor.matmul(ps[:, c0:c1], aw[0:GR, d, h * P:(h + 1) * P], lr2[0:GR, d, c0:c1],
                                       start=True, stop=True)
            ins.then_inc(is_full(key)[0], 1)

        @block.tensor
        def _(pe):
            mmul = nc.tensor.matmul

            def project_T(slot, m, src, key, nlat=True, nctx=False, koff=0, kn=KD):
                ps = open_(pe, key, 2 if nctx else 1)
                for k in range(kn):
                    ins = mmul(ps[:, 0:T], slot[:, k, m * P:(m + 1) * P], src[:, k, C:NT],
                               start=(k == 0), stop=(k == kn - 1))
                if nctx:
                    for k in range(kn):
                        ins = mmul(ps[:, T:T + C], slot[:, k, m * P:(m + 1) * P], src[:, k, 0:C],
                                   start=(k == 0), stop=(k == kn - 1))
                ins.then_inc(is_full(key)[0], 1)

            def project_tok(slot, n, src, t, key):
                ps = open_(pe, key)
                for k in range(KD):
                    ins = mmul(ps[:, 0:n], src[:, k, t * P:(t + 1) * P], slot[:, k, 0:n],
                               start=(k == 0), stop=(k == KD - 1))
                ins.then_inc(is_full(key)[0], 1)

            def mods(s):
                slot = full_strip(pe, ada_w, s * 512)
                key = ("mod", s)
                ps = open_(pe, key)
                for m in range(4):
                    for k in range(KD):
                        ins = mmul(ps[:, 2 * m:2 * m + 2], slot[:, k, m * P:(m + 1) * P],
                                   c_("c")[:, 2 * k:2 * k + 2], start=(k == 0), stop=(k == KD - 1))
                ins.then_inc(is_full(key)[0], 1)
                strip_used(key)

            pe.wait_ge(S_("c_act"), 1)
            for s in range(4):
                mods(s)
            pe.wait_ge(S_("consts_in"), 16 * 2)
            for k in range(KD):
                pe.wait_ge(S_("x_normed"), TT)
                for key, t0, n in ((("hT", k), TC, TL), (("hTc", k), 0, TC)):
                    ps = open_(pe, key)
                    for t in range(n):
                        ins = nc.tensor.transpose(ps[:, t * P:(t + 1) * P], xs[:, t0 + t, k * P:(k + 1) * P], ident)
                    ins.then_inc(is_full(key)[0], 1)
            for k in range(KD):
                pe.wait_ge(*is_free(("hT", k)))
                pe.wait_ge(*is_free(("hTc", k)))
            phase_end(pe, 1)

            pe.wait_ge(S_("small_in"), 16 * 4)
            key = ("dt",)
            ps = open_(pe, key)
            for t in range(TT):
                for k in range(KD):
                    ins = mmul(ps[:, t * 64:(t + 1) * 64], hT[:, k, t * P:(t + 1) * P], wsmall[:, k, 2 * GR:],
                               start=(k == 0), stop=(k == KD - 1))
            ins.then_inc(is_full(key)[0], 1)
            pe.wait_ge(S_("dta"), 1)
            key = ("acs",)
            ps = open_(pe, key, 2)
            dta = tmpd[0]
            for d in range(2):
                ins = mmul(ps[:, d * 192:(d + 1) * 192], mask[d], dta[:, :, d * SH:(d + 1) * SH], start=True, stop=True)
            ins = mmul(ps[:, 512:512 + TT * 64], ones, dta[:, :, :].rearrange("p t h -> p (t h)"), start=True, stop=True)
            ins.then_inc(is_full(key)[0], 1)
            pe.wait_ge(S_("acs_split"), 1)
            for d in range(2):
                key = ("acsT", d)
                ps = open_(pe, key).bitcast(BF16)
                for t in range(TL):
                    ins = nc.tensor.transpose(ps[0:3 * SH, t * P:(t + 1) * P],
                                              acs3[:, t, d, :, :].rearrange("p s h -> p (s h)"), identb)
                ins.then_inc(is_full(key)[0], 1)

            for g in range(SG):
                slot = full_strip(pe, w_in, X0 + g * GW)
                for m in range(4):
                    project_T(slot, m, hT, ("x", g, m), nctx=True)
                    strip_used(("x", g, m))
                    if m >= 1:
                        x_turn(pe, g, m - 1)
                slot = strip(pe, [(lambda s: s[:, 0:2048].rearrange("p (k n) -> p k n", k=KD)[:, :, 0:P],
                                   w_cols(w_in, B0 + g * SN, SN)),
                                  (lambda s: s[:, 0:2048].rearrange("p (k n) -> p k n", k=KD)[:, :, P:2 * P],
                                   w_cols(w_in, C0 + g * SN, SN))])[:, 0:2048].rearrange("p (k n) -> p k n", k=KD)
                project_T(slot, 0, hT, ("B", g), nctx=True)
                project_T(slot, 1, hT, ("C", g))
                strip_used(("C", g))
                x_turn(pe, g, 3)
                slot = full_strip(pe, w_in, Z0 + g * GW)
                pe.wait_ge(S_("BT_ready"), g + 1)
                for half in range(2):
                    key = ("Btok", g, half)
                    ps = open_(pe, key)
                    for t in range(3):
                        tt = half * 3 + t
                        ins = nc.tensor.transpose(ps[:, t * P:(t + 1) * P], BT[:, tt * P:(tt + 1) * P], ident)
                    ins.then_inc(is_full(key)[0], 1)
                pe.wait_ge(S_("CT_ready"), g + 1)
                key = ("CB", g)
                ps = open_(pe, key)
                for c in range(TL):
                    ins = mmul(ps[:, c * P:(c + 1) * P], BT[:, C + c * P:C + (c + 1) * P],
                               CT[:, c * P:(c + 1) * P], start=True, stop=True)
                ins.then_inc(is_full(key)[0], 1)

                for d in range(2):
                    order = [0, 1, 2, 3, 4, 5] if d == 0 else [1, 0, 5, 4, 3, 2]
                    pe.wait_ge(*is_free(("Btok", g, 1)))
                    nh = [0]

                    def rows_of(h):
                        key = ("R", g, d, h)
                        ps = open_(pe, key, 1, 0, 4)
                        hh = g * HPG + h
                        pe.wait_ge(*is_free(("acsT", d)))
                        ins = mmul(ps[:, :], selb[0:3 * SH, hh:hh + 1].to_broadcast([3 * SH, P]),
                                   rowsT[0:3 * SH, d, :], start=True, stop=True)
                        ins.then_inc(is_full(key)[0], 1)

                    for i, t in enumerate(order):
                        if i >= 2:
                            key = ("off", g, d, i)
                            ps = open_(pe, key)
                            pe.wait_ge(*is_free(("kv", g, d, i - 1)))
                            ins = mmul(ps[:, :], CT[:, (t - TC) * P:(t - TC + 1) * P], S[(i - 1) % 2][:, :],
                                       start=True, stop=True)
                            ins.then_inc(is_full(key)[0], 1)
                        if i < 5:
                            key = ("kv", g, d, i)
                            pe.wait_ge(S_("xw_ready"), (g * 2 + d) * 5 + i + 1)
                            ps = open_(pe, key)
                            ins = mmul(ps[:, :], Btok[:, t, :], xw[i % 2][:, :], start=True, stop=True)
                            ins.then_inc(is_full(key)[0], 1)
                    pe.wait_ge(S_("xdt_ready"), g * 2 + d + 1)
                    ys = [None] * TL
                    rows_of(0)
                    rows_of(1)
                    yb = open_(pe, ("y", g, d), 4, 4, 8)
                    for h in range(HPG):
                        n = (g * 2 + d) * HPG + h
                        if h + 2 < HPG:
                            rows_of(h + 2)
                        pe.wait_ge(S_("M_ready"), n + 1)
                        for c in range(TL):
                            ins = mmul(yb[:, c * 512 + h * SHD:c * 512 + (h + 1) * SHD], mm[n % NM][:, c, :],
                                       xdt[:, c, h * SHD:(h + 1) * SHD], start=True, stop=True)
                        if h < HPG - 1:
                            ins.then_inc(S_("M_used"), 1)
                    ins.then_inc(is_full(("y", g, d))[0], 1)
                for t in range(TL):
                    project_tok(slot, GW, hT, TC + t, ("z", g, t))
                strip_used(("z", g, TL - 1))
                pe.wait_ge(S_("yz_ready"), (g + 1) * TL)
                for m in range(4):
                    key = ("yT", g, m)
                    ps = open_(pe, key)
                    for c in range(TL):
                        ins = nc.tensor.transpose(ps[:, c * P:(c + 1) * P], yacc[:, c, m * P:(m + 1) * P], ident)
                    ins.then_inc(is_full(key)[0], 1)
                pe.wait_ge(*is_free(("yT", g, 3)))

            pe.wait_ge(S_("ssd_rstd"), 1)
            key = ("rrow",)
            ps = open_(pe, key)
            for c in range(TL):
                ins = mmul(ps[:, c * P:(c + 1) * P], small[:, c:c + 1].to_broadcast([P, P]), ident,
                           start=True, stop=True)
            ins.then_inc(is_full(key)[0], 1)

            def gate_T(c0, name):
                for j in range(2):
                    slot = full_strip(pe, w_in, c0 + j * 512)
                    for m in range(4):
                        project_T(slot, m, hT, (name, j * 4 + m))
                        strip_used((name, j * 4 + m))

            gate_T(GC0, "gc")
            for j in range(2):
                keys = [("pc", j * 4 + m) for m in range(4)]
                for kh in range(2):
                    slot = full_strip(pe, a["ssd_proj"][0], j * 512, 512, kh * D, D)
                    if kh == 0:
                        pss = [open_(pe, k) for k in keys]
                    for m in range(4):
                        for k in range(KD):
                            ins = mmul(pss[m][:, :], slot[:, k, m * P:(m + 1) * P], yT[:, kh * KD + k, :],
                                       start=(kh == 0 and k == 0), stop=(kh == 1 and k == KD - 1))
                        if kh == 1:
                            ins.then_inc(is_full(keys[m])[0], 1)
                        elif m == 3:
                            ins.then_inc(S_("pc_half"), 1)
                    strip_used(keys[3] if kh else ("sem", "pc_half", j + 1))
            phase_end(pe, 2)

            slot = full_strip(pe, w_in, Q0)
            for m in range(4):
                project_T(slot, m, hT, ("q", m))
            strip_used(("q", 3))
            slot = full_strip(pe, w_in, K0)
            for m in range(4):
                project_T(slot, m, hT, ("k", m), nctx=True)
            strip_used(("k", 3))
            for j in range(2):
                slot = full_strip(pe, w_in, V0 + j * 512)
                for t in range(TT):
                    project_tok(slot, 512, hT, t, ("v", j, t))
                strip_used(("v", j, TT - 1))
            for d in range(2):
                key = ("lr", d)
                ps = open_(pe, key, 2)
                for c0, c1, o in ((C, NT, 0), (0, C, T)):
                    for k in range(KD):
                        ins = mmul(ps[0:GR, o:o + c1 - c0], wsmall[:, k, d * GR:(d + 1) * GR], hT[:, k, c0:c1],
                                   start=(k == 0), stop=(k == KD - 1))
                ins.then_inc(is_full(key)[0], 1)
            pe.wait_ge(S_("aw_in"), 16)
            for h in range(GH):
                for d in range(2):
                    n = h * 2 + d
                    if n == 0:
                        gla_z(pe, h, d)
                    pe.wait_ge(*is_free(("lr", 1)))
                    order = [0, 1, 2, 3, 4, 5] if d == 0 else [1, 0, 5, 4, 3, 2]
                    pe.wait_ge(S_("qk_ready"), n + 1)
                    key = ("sc", n)
                    ps = open_(pe, key, 1, 2, 8)
                    for c in range(TL):
                        ins = mmul(ps[:, c * P:(c + 1) * P], ek[:, TC + c, :], eq[:, c, :], start=True, stop=True)
                    ins.then_inc(is_full(key)[0], 1)
                    for half in range(2):
                        key = ("ekT", n, half)
                        ps = open_(pe, key, 1, 2, 8)
                        for t in range(3):
                            ins = nc.tensor.transpose(ps[:, t * P:(t + 1) * P], ek[:, half * 3 + t, :], ident)
                        ins.then_inc(is_full(key)[0], 1)
                    if n + 1 < 8:
                        gla_z(pe, (n + 1) // 2, (n + 1) % 2)
                    for j in range(2):
                        pe.wait_ge(*is_free(("v", j, TT - 1)))
                    for i, t in enumerate(order):
                        if i < 5:
                            pe.wait_ge(*is_free(("ekT", n, t // 3)))
                            key = ("gkv", n, i)
                            ps = open_(pe, key, 1, 2, 8)
                            ins = mmul(ps[:, 0:GDV], ekT[:, t, :], vtok[:, t, h * GDV:(h + 1) * GDV],
                                       start=True, stop=True)
                            ins.then_inc(is_full(key)[0], 1)
                        if i >= 2:
                            pe.wait_ge(*is_free(("sc", n)))
                            key = ("o", n, i)
                            ps = open_(pe, key, 1, 2, 8)
                            mmul(ps[:, 0:GDV], sc[:, t - TC, :], vtok[:, t, h * GDV:(h + 1) * GDV],
                                 start=True, stop=False)
                            pe.wait_ge(S_("st_ready"), n * 4 + i - 1)
                            ins = mmul(ps[:, 0:GDV], eq[:, t - TC, :], st[(i - 1) % 2][:, :], start=False, stop=True)
                            ins.then_inc(is_full(key)[0], 1)
            for j in range(2):
                slot = full_strip(pe, w_in, R0 + j * 512)
                for t in range(TL):
                    project_tok(slot, 512, hT, TC + t, ("r", j, t))
                strip_used(("r", j, TL - 1))
            pe.wait_ge(S_("o_gated"), 2 * TL)
            for m in range(KD):
                key = ("oT", m)
                ps = open_(pe, key)
                for c in range(TL):
                    ins = nc.tensor.transpose(ps[:, c * P:(c + 1) * P], otok[:, c, m * P:(m + 1) * P], ident)
                ins.then_inc(is_full(key)[0], 1)
            gate_T(GA0, "ga")

            def branch(w, src, name):
                for j in range(2):
                    slot = full_strip(pe, w, j * 512)
                    for m in range(4):
                        key = (name, j * 4 + m)
                        ps = open_(pe, key)
                        for k in range(KD):
                            ins = mmul(ps[:, :], slot[:, k, m * P:(m + 1) * P], src[:, k, :],
                                       start=(k == 0), stop=(k == KD - 1))
                        ins.then_inc(is_full(key)[0], 1)
                    strip_used((name, j * 4 + 3))

            for m in range(KD):
                pe.wait_ge(*is_free(("oT", m)))
            branch(a["gla_proj"][0], oT, "pa")
            phase_end(pe, 3)

            for j in range(2):
                slot = full_strip(pe, w_in, U0 + j * 512)
                for m in range(4):
                    project_T(slot, m, hT, ("u", j * 4 + m))
                strip_used(("u", j * 4 + 3))
            pe.wait_ge(S_("fconst_in"), 16 * 3)
            pe.wait_ge(S_("u_folded"), 1)
            for r in range(TL):
                src, f = (ue, fC) if r < 2 else (uo, fS)
                key = ("A", r)
                ps = open_(pe, key, 2)
                for g in range(4):
                    o = ps[:, g * FG:(g + 1) * FG]
                    for k in range(2):
                        ins = mmul(o, src[:, 2 * g + k, (r % 2) * P:(r % 2 + 1) * P], f[:, k, :],
                                   start=(k == 0), stop=(k == 1))
                        if r == 2 and k == 0:
                            for q in range(2):
                                mmul(ps[0:1, g * FG:(g + 1) * FG], uT[:, 2 * g + q, T // 2:T // 2 + 1], fC[:, q, :],
                                     start=False, stop=False, skip_group_check=True)
                ins.then_inc(is_full(key)[0], 1)
            for r in range(TL):
                pe.wait_ge(*is_free(("A", r)))
            for m in range(KD):
                key = ("fy", m)
                ps = open_(pe, key)
                for r in range(TL):
                    ins = mmul(ps[:, :], At[:, r, m * P:(m + 1) * P], fT[:, r, :], start=(r == 0), stop=(r == TL - 1))
                ins.then_inc(is_full(key)[0], 1)
            gate_T(GB0, "gb")
            for m in range(KD):
                pe.wait_ge(*is_free(("fy", m)))
            branch(a["fnet_proj"][0], fyT, "pb")
            for s in range(4, 12):
                mods(s)
            phase_end(pe, 4)

            for c, name in ((2, "g1"), (5, "g2")):
                for j in range(2):
                    key = (name, j)
                    ps = open_(pe, key)
                    for m in range(4):
                        ins = mmul(ps[:, m * P:(m + 1) * P],
                                   mod[:, c * KD + j * 4 + m, 0:1].to_broadcast([P, P]), ident, start=True, stop=True)
                    ins.then_inc(is_full(key)[0], 1)
            for j in range(2):
                slot = full_strip(pe, a["w_out"][0], j * 512)
                for t in range(TL):
                    project_tok(slot, 512, mT, t, ("wo", j, t))
                strip_used(("wo", j, TL - 1))
            for k in range(KD):
                pe.wait_ge(S_("x1_normed"), TL)
                key = ("h2T", k)
                ps = open_(pe, key)
                for t in range(TL):
                    ins = nc.tensor.transpose(ps[:, t * P:(t + 1) * P], yo[:, t, k * P:(k + 1) * P], ident)
                ins.then_inc(is_full(key)[0], 1)
            for k in range(KD):
                pe.wait_ge(*is_free(("h2T", k)))
            key = ("route",)
            pe.wait_ge(S_("rw_in"), 16)
            ps = open_(pe, key)
            for t in range(TL):
                for k in range(KD):
                    ins = mmul(ps[:, t * NE:(t + 1) * NE], h2T[:, k, t * P:(t + 1) * P], rw[:, k, :],
                               start=(k == 0), stop=(k == KD - 1))
            ins.then_inc(is_full(key)[0], 1)

            def expert_up(e):
                s1 = full_strip(pe, a["exp_w1"][0, e], 0)
                i1 = len(strips) - 1
                s3 = full_strip(pe, a["exp_w3"][0, e], 0)
                for m in range(4):
                    for slot, nm in ((s1, "w1"), (s3, "w3")):
                        key = (nm, e, m)
                        ps = open_(pe, key)
                        for k in range(KD):
                            ins = mmul(ps[:, :], slot[:, k, m * P:(m + 1) * P], h2T[:, k, :],
                                       start=(k == 0), stop=(k == KD - 1))
                        ins.then_inc(is_full(key)[0], 1)
                strips[i1][1] = ("w1", e, 3)
                strip_used(("w3", e, 3))

            for e in range(NE):
                expert_up(e)
                slot = full_strip(pe, a["exp_w2"][0, e], 0, D, 0, FF)
                for m in range(4):
                    pe.wait_ge(*is_free(("w3", e, m)))
                for t in range(TL):
                    for j in range(2):
                        key = ("w2", e, t, j)
                        ps = open_(pe, key)
                        for k in range(FF // P):
                            ins = mmul(ps[:, :], heT[:, k, t * P:(t + 1) * P], slot[:, k, j * 512:(j + 1) * 512],
                                       start=(k == 0), stop=(k == FF // P - 1))
                        ins.then_inc(is_full(key)[0], 1)
                strip_used(("w2", e, TL - 1, 1))


        @block.sync
        def _(sp):
            sp.dma_start(col, a["cols"]).then_inc(S_("cols_in"), 16)
            for n, (pieces, _) in enumerate(strips):
                if n >= NS:
                    key = strips[n - NS][1]
                    if key[0] == "sem":
                        sp.wait_ge(S_(key[1]), key[2])
                    else:
                        sp.wait_ge(*is_full(key))
                for dst, src in pieces:
                    sp.dma_start(dst(ring[n % NS]), src).then_inc(strip_in[n % NS], 16)
                if n == 0:
                    sp.dma_start(row, a["rows"]).then_inc(S_("rows_in"), 16)
            sp.wait_ge(S_("out_ready"), TL)
            sp.dma_start(out[0].rearrange("(t p) d -> p t d", p=P), yo).then_inc(S_("out_sent"), 16)
            sp.wait_ge(S_("out_sent"), 16)

        @block.scalar
        def _(act):
            run = nc.scalar.activation
            n_ = [0]

            def step(ins):
                n_[0] += 1
                ins.then_inc(S_("act_step"), 1)
                act.wait_ge(S_("act_step"), n_[0])

            act.dma_start(xs[:, 0:TC, :], a["ctx"][0].rearrange("(t p) d -> p t d", p=P)).then_inc(S_("ctx_in"), 16)
            for t in range(TL):
                act.dma_start(xs[:, TC + t, :], a["x"][0, t * P:(t + 1) * P, :]).then_inc(S_("x_in%d" % t), 16)
                act.dma_start(pos[:, t, :], a["pos"][t * P:(t + 1) * P, :]).then_inc(S_("x_in%d" % t), 16)
            act.dma_start(sq, a["squares"]).then_inc(S_("consts_in"), 16)
            act.dma_start(self_[0:3 * SH, :], a["sel"]).then_inc(S_("consts_in"), 16)
            for d0, c0, n in ((0, LR0, 2 * GR), (2 * GR, DT0, 2 * SH)):
                act.dma_start(wsmall[:, :, d0:d0 + n], w_cols(w_in, c0, n),
                              allow_slow_non_contiguous=True).then_inc(S_("small_in"), 32)

            act.wait_ge(S_("cols_in"), 16)
            run(c_("c"), c_("c"), ACT.Silu).then_inc(S_("c_act"), 1)
            for t in range(TT):
                act.wait_ge(S_("x_pos"), t + 1)
                if t:
                    act.wait_ge(S_("x_ss"), t)
                ins = run(junk, xs[:, t, :], ACT.Square, accum_out=small[:, t:t + 1])
                ins.then_inc(S_("x_ss"), 1)
            act.wait_ge(S_("x_var"), 1)
            run(small[:, 16:16 + TT], small[:, 8:8 + TT], ACT.Sqrt).then_inc(S_("x_std"), 1)
            act.wait_ge(S_("modA1"), 1)
            for k in range(KD):
                for key, j, lo, n in ((("hT", k), 0, C, T), (("hTc", k), 1, 0, C)):
                    act.wait_ge(*is_full(key))
                    ps = bank(key)
                    run(hT[:, k, lo:lo + n], ps[:, 0:n], ACT.Identity, scale=modA[:, j, k:k + 1],
                             bias=mod[:, k, j:j + 1]).then_inc(is_free(key)[0], 1)
            phase_end(act, 1)

            run(nega, r_("a_log"), ACT.Exp).then_inc(S_("nega"), 1)
            act.wait_ge(S_("dt_negabs"), 1)
            run(tmpd[1], tmpd[1], ACT.Exp).then_inc(S_("dt_exp"), 1)
            act.wait_ge(S_("dt_w"), 1)
            run(wend, dt, ACT.Ln).then_inc(S_("dt_ln"), 1)
            act.wait_ge(S_("acs_out"), 1)
            run(wend, wend, ACT.Exp).then_inc(S_("acs_exps"), 1)
            run(eend, tmpd[1], ACT.Exp).then_inc(S_("acs_exps"), 1)
            run(eacs, acs, ACT.Exp).then_inc(S_("acs_exps"), 1)
            for d in range(2):
                act.wait_ge(*is_full(("acsT", d)))
                ps = bank(("acsT", d))
                ps = ps.bitcast(BF16)
                run(rowsT[0:3 * SH, d, :], ps[0:3 * SH, 0:T], ACT.Copy).then_inc(is_free(("acsT", d))[0], 1)
            act.wait_ge(S_("raw_zero"), 1)
            for g in range(SG):
                def raw_evac(key, rn):
                    if rn >= 2:
                        act.wait_ge(S_("conv_done"), rn - 1)
                    act.wait_ge(*is_full(key))
                    ps = bank(key)
                    dst = raw[rn % 2]
                    if key[0] != "C":
                        step(run(dst[:, 2:2 + C], ps[:, T:T + C], ACT.Copy))
                    run(dst[:, LAT:LAT + T], ps[:, 0:T], ACT.Copy).then_inc(is_free(key)[0], 1)

                def silu_conv(kind, m, rn):
                    act.wait_ge(S_("conv_done"), rn + 1)
                    if kind == "x":
                        blk = g * 4 + m
                        bias = c_("conv_b")[:, blk:blk + 1]
                        prev = ("xtok", g, m - 1, 1) if m else (("xtok", g - 1, 3, 1) if g else None)
                        if prev:
                            act.wait_ge(*is_full(prev))
                        run(xcT[:, 0:C], cacc[:, 0:C], ACT.Silu, bias=bias)
                        run(xcT[:, C:NT], cacc[:, C + 4:C + 4 + T], ACT.Silu, bias=bias).then_inc(S_("xc_ready"), 1)
                    elif kind == "B":
                        bias = c_("conv_b")[:, 16 + g:17 + g]
                        if g:
                            act.wait_ge(*is_full(("CB", g - 1)))
                        run(BT[:, 0:C], cacc[:, 0:C], ACT.Silu, bias=bias)
                        run(BT[:, C:NT], cacc[:, C + 4:C + 4 + T], ACT.Silu, bias=bias).then_inc(S_("BT_ready"), 1)
                    else:
                        if g:
                            act.wait_ge(*is_full(("off", g - 1, 1, 5)))
                        run(CT, cacc[:, C + 4:C + 4 + T], ACT.Silu, bias=c_("conv_b")[:, 20 + g:21 + g]).then_inc(S_("CT_ready"), 1)

                def xtok_evac(m):
                    if g:
                        act.wait_ge(S_("xw_ready"), g * 10)
                        act.wait_ge(S_("xdt_ready"), g * 2)
                    for half in range(2):
                        key = ("xtok", g, m, half)
                        act.wait_ge(*is_full(key))
                        ps = bank(key)
                        run(xtok[:, half * 3:half * 3 + 3, m * P:(m + 1) * P],
                                 ps[:, 0:3 * P].rearrange("p (t n) -> p t n", t=3), ACT.Copy).then_inc(is_free(key)[0], 1)

                for m in range(4):
                    raw_evac(("x", g, m), g * 6 + m)
                    if m >= 1:
                        silu_conv("x", m - 1, g * 6 + m - 1)
                    if m >= 2:
                        xtok_evac(m - 2)
                raw_evac(("B", g), g * 6 + 4)
                silu_conv("x", 3, g * 6 + 3)
                raw_evac(("C", g), g * 6 + 5)
                silu_conv("B", 0, g * 6 + 4)
                xtok_evac(2)
                xtok_evac(3)
                silu_conv("C", 0, g * 6 + 5)
                for half in range(2):
                    key = ("Btok", g, half)
                    act.wait_ge(*is_full(key))
                    ps = bank(key)
                    if g:
                        act.wait_ge(*is_full(("kv", g - 1, 1, 4)))
                    run(Btok[:, half * 3:half * 3 + 3, :], ps[:, 0:3 * P].rearrange("p (t n) -> p t n", t=3),
                             ACT.Copy).then_inc(is_free(key)[0], 1)
                for d in range(2):
                    for h in range(HPG):
                        n = (g * 2 + d) * HPG + h
                        act.wait_ge(*is_free(("R", g, d, h)))
                        run(mm[n % NM], mm[n % NM], ACT.Exp).then_inc(S_("decay_ready"), 1)
                for t in range(TL):
                    key = ("z", g, t)
                    act.wait_ge(*is_full(key))
                    ps = bank(key)
                    if g or t:
                        act.wait_ge(S_("yz_squared"), g * 4 + t)
                    run(sz, ps[:, :], ACT.Silu).then_inc(is_free(key)[0], 1)
                    act.wait_ge(S_("yz_ready"), g * 4 + t + 1)
                    act.wait_ge(*is_free(key))
                    run(sz, yacc[:, t, :], ACT.Square, accum_out=ssq[:, t, g:g + 1]).then_inc(S_("yz_squared"), 1)
                for m in range(4):
                    key = ("yT", g, m)
                    act.wait_ge(*is_full(key))
                    ps = bank(key)
                    blk = g * 4 + m
                    run(yT[:, blk, :], ps[:, :], ACT.Identity, scale=c_("ssd_norm")[:, blk:blk + 1], bias=0.0).then_inc(is_free(key)[0], 1)
            act.wait_ge(S_("ssd_var"), 1)
            run(small[:, 16:16 + TL], small[:, 8:8 + TL], ACT.Sqrt).then_inc(S_("ssd_std"), 1)
            act.wait_ge(*is_full(("rrow",)))
            ps = bank(("rrow",))
            run(rrow, ps[:, :], ACT.Copy).then_inc(is_free(("rrow",))[0], 1)

            def gates(name):
                for m in range(KD):
                    act.wait_ge(*is_full((name, m)))
                    ps = bank((name, m))
                    run(gateT[:, m, :], ps[:, :], ACT.Sigmoid).then_inc(is_free((name, m))[0], 1)

            gates("gc")
            phase_end(act, 2)

            act.dma_start(aw[0:GR, :, :], a["gla_a_w"][0].rearrange("d r n -> r d n")).then_inc(S_("aw_in"), 16)
            for m in range(4):
                act.wait_ge(*is_full(("q", m)))
                ps = bank(("q", m))
                run(qT[:, m, :], ps[:, :], ACT.Copy).then_inc(is_free(("q", m))[0], 1)
            for m in range(4):
                act.wait_ge(*is_full(("k", m)))
                ps = bank(("k", m))
                run(kT[:, m, 0:C], ps[:, T:NT], ACT.Copy)
                run(kT[:, m, C:NT], ps[:, 0:T], ACT.Copy).then_inc(is_free(("k", m))[0], 1)
            for j in range(2):
                for t in range(TT):
                    act.wait_ge(*is_full(("v", j, t)))
                    ps = bank(("v", j, t))
                    run(vtok[:, t, j * 512:(j + 1) * 512], ps[:, :], ACT.Copy).then_inc(is_free(("v", j, t))[0], 1)
            for d in range(2):
                act.wait_ge(*is_full(("lr", d)))
                ps = bank(("lr", d))
                run(lr2[0:GR, d, 0:C], ps[0:GR, T:NT], ACT.Copy)
                run(lr2[0:GR, d, C:NT], ps[0:GR, 0:T], ACT.Copy).then_inc(is_free(("lr", d))[0], 1)
            for n in range(8):
                act.wait_ge(S_("gz_negabs"), n + 1)
                run(eb, eb, ACT.Exp).then_inc(S_("gz_exp"), 1)
                act.wait_ge(S_("gz_w"), n + 1)
                run(wb, wb, ACT.Ln).then_inc(S_("gz_ln"), 1)
                act.wait_ge(S_("decay_refd"), n + 1)
                sgn = 1.0 if n % 2 == 0 else -1.0
                if n:
                    act.wait_ge(*is_full(("o", n - 1, 5)))
                run(eq, dd[:, TC:TT, :], ACT.Exp, scale=sgn / TAU)
                run(ek, dd, ACT.Exp, scale=-sgn / TAU)
                run(ea, pc[:, :, P // 2], ACT.Exp, scale=1.0 / TAU)
                run(ebb, dref, ACT.Exp, scale=1.0 / TAU).then_inc(S_("gla_exps"), 1)
                for half in range(2):
                    key = ("ekT", n, half)
                    act.wait_ge(*is_full(key))
                    ps = bank(key)
                    run(ekT[:, half * 3:half * 3 + 3, :], ps[:, 0:3 * P].rearrange("p (t n) -> p t n", t=3),
                             ACT.Copy).then_inc(is_free(key)[0], 1)
            act.wait_ge(S_("o_all"), 1)
            for c in range(TL):
                for h in range(GH):
                    if h or c:
                        step(ins)
                    ins = run(zb[:, 0:GDV], otok[:, c, h * GDV:(h + 1) * GDV], ACT.Square,
                              accum_out=gss[:, c, h:h + 1])
            ins.then_inc(S_("o_squared"), 1)
            act.wait_ge(S_("o_var"), 1)
            run(gss, gss, ACT.Sqrt).then_inc(S_("o_std"), 1)
            rbuf = [eb, wb]
            for j in range(2):
                for t in range(TL):
                    i = j * TL + t
                    act.wait_ge(*is_full(("r", j, t)))
                    ps = bank(("r", j, t))
                    if i >= 2:
                        act.wait_ge(S_("o_gated"), i - 1)
                    run(rbuf[i % 2][:, 0:512], ps[:, :], ACT.Silu).then_inc(is_free(("r", j, t))[0], 1)
            for m in range(KD):
                act.wait_ge(*is_full(("oT", m)))
                ps = bank(("oT", m))
                run(oT[:, m, :], ps[:, :], ACT.Identity, scale=c_("gla_norm")[:, m % 2:m % 2 + 1], bias=0.0).then_inc(is_free(("oT", m))[0], 1)
            gates("ga")
            phase_end(act, 3)

            act.dma_start(fT, a["dft_time"].rearrange("(r p) k -> p r k", p=P)).then_inc(S_("fconst_in"), 16)
            act.dma_start(fC, a["dft_cos"].rearrange("(r p) k -> p r k", p=P)).then_inc(S_("fconst_in"), 16)
            act.dma_start(fS, a["dft_sin"].rearrange("(r p) k -> p r k", p=P)).then_inc(S_("fconst_in"), 16)
            for m in range(KD):
                act.wait_ge(*is_full(("u", m)))
                ps = bank(("u", m))
                run(uT[:, m, :], ps[:, :], ACT.Copy).then_inc(is_free(("u", m))[0], 1)
            for r in range(TL):
                act.wait_ge(*is_full(("A", r)))
                ps = bank(("A", r))
                run(At[:, r, :], ps[:, :], ACT.Copy).then_inc(is_free(("A", r))[0], 1)
            for m in range(KD):
                act.wait_ge(*is_full(("fy", m)))
                ps = bank(("fy", m))
                run(fyT[:, m, :], ps[:, :], ACT.Copy).then_inc(is_free(("fy", m))[0], 1)
            gates("gb")
            phase_end(act, 4)

            act.dma_start(xr, a["x"][0].rearrange("(t p) d -> p t d", p=P)).then_inc(S_("xr_in"), 16)
            act.dma_start(pos2, a["pos"].rearrange("(t p) d -> p t d", p=P)).then_inc(S_("xr_in"), 16)
            act.dma_start(rw, a["router_w"].rearrange("(k p) e -> p k e", p=P)).then_inc(S_("rw_in"), 16)
            act.dma_start(frow, a["final_row"]).then_inc(S_("frow_in"), 16)
            for name, dst in (("g1", g1row), ("g2", g2row)):
                for j in range(2):
                    act.wait_ge(*is_full((name, j)))
                    ps = bank((name, j))
                    run(dst[:, j * 512:(j + 1) * 512], ps[:, :], ACT.Copy).then_inc(is_free((name, j))[0], 1)
            for t in range(TL):
                act.wait_ge(S_("x1_ready"), TL + t + 1)
                if t:
                    act.wait_ge(S_("x1_ss"), t)
                ins = run(junk2, xr[:, t, :], ACT.Square, accum_out=small[:, t:t + 1])
                ins.then_inc(S_("x1_ss"), 1)
            act.wait_ge(S_("x1_var"), 1)
            run(small[:, 16:16 + TL], small[:, 8:8 + TL], ACT.Sqrt).then_inc(S_("x1_std"), 1)
            for k in range(KD):
                act.wait_ge(*is_full(("h2T", k)))
                ps = bank(("h2T", k))
                run(h2T[:, k, :], ps[:, :], ACT.Identity, scale=modA[:, 2, k:k + 1],
                         bias=mod[:, 3 * KD + k, 0:1]).then_inc(is_free(("h2T", k))[0], 1)
            act.wait_ge(*is_full(("route",)))
            ps = bank(("route",))
            run(score, ps[:, 0:TL * NE].rearrange("p (t e) -> p t e", t=TL), ACT.Sigmoid).then_inc(is_free(("route",))[0], 1)
            for e in range(NE):
                for m in range(4):
                    n = e * 4 + m
                    if n >= 2:
                        act.wait_ge(*is_free(("w3", (n - 2) // 4, (n - 2) % 4)))
                    act.wait_ge(*is_full(("w1", e, m)))
                    ps = bank(("w1", e, m))
                    run(sg[n % 2], ps[:, :], ACT.Silu).then_inc(is_free(("w1", e, m))[0], 1)
            for t in range(TL):
                act.wait_ge(S_("x2_ready"), t + 1)
                if t:
                    act.wait_ge(S_("x2_ss"), t)
                run(junk2, xr[:, t, :], ACT.Square, accum_out=small[:, 32 + t:33 + t]).then_inc(S_("x2_ss"), 1)
            act.wait_ge(S_("x2_var"), 1)
            run(small[:, 48:48 + TL], small[:, 40:40 + TL], ACT.Sqrt).then_inc(S_("x2_std"), 1)

        @block.vector
        def _(dve):
            v = nc.vector
            n_ = [0]

            def step(ins):
                n_[0] += 1
                ins.then_inc(S_("dve_step"), 1)
                dve.wait_ge(S_("dve_step"), n_[0])

            def modulation(s):
                key = ("mod", s)
                dve.wait_ge(*is_full(key))
                ps = bank(key)
                v.tensor_tensor(mod[:, s * 4:s * 4 + 4, :], ps[:, 0:8].rearrange("p (m j) -> p m j", m=4),
                                     c_("ada_b")[:, s * 4:s * 4 + 4].unsqueeze(2).to_broadcast([P, 4, 2]), ALU.add).then_inc(is_free(key)[0], 1)

            def rstd(dst, ss, var, std, n, width, name_ss, cnt, name_var, name_std):
                dve.wait_ge(S_(name_ss), cnt)
                v.tensor_scalar(var, ss, 1.0 / width, EPS, ALU.mult, ALU.add).then_inc(S_(name_var), 1)
                dve.wait_ge(S_(name_std), 1)
                step(v.reciprocal(dst, std))

            for t in range(TT):
                if t < TC:
                    dve.wait_ge(S_("ctx_in"), 16)
                    v.tensor_scalar(xs[:, t, 0:2], xs[:, t, 0:2], 1.0, None, ALU.mult).then_inc(S_("x_pos"), 1)
                else:
                    dve.wait_ge(S_("x_in%d" % (t - TC)), 32)
                    v.tensor_tensor(xs[:, t, :], xs[:, t, :], pos[:, t - TC, :], ALU.add).then_inc(S_("x_pos"), 1)
            rstd(small[:, 24:24 + TT], small[:, 0:TT], small[:, 8:8 + TT], small[:, 16:16 + TT], TT, D,
                 "x_ss", TT, "x_var", "x_std")
            for t in range(TT):
                v.tensor_scalar(xs[:, t, :], xs[:, t, :], small[:, 24 + t:25 + t], None, ALU.mult).then_inc(S_("x_normed"), 1)
            for s in range(4):
                modulation(s)
            for s in range(4):
                dve.wait_ge(*is_free(("mod", s)))
            for j in range(2):
                ins = v.scalar_tensor_tensor(modA[:, j, :], mod[:, KD:2 * KD, j], 1.0, c_("norm1"), ALU.add, ALU.mult)
                if j == 0:
                    step(ins)
            ins.then_inc(S_("modA1"), 1)
            phase_end(dve, 1)

            for i in range(2):
                ins = v.memset(raw[i], 0.0)
                if i == 0:
                    step(ins)
            ins.then_inc(S_("raw_zero"), 1)
            dve.wait_ge(S_("rows_in"), 16)
            dve.wait_ge(*is_full(("dt",)))
            ps = bank(("dt",))
            x_, e_ = tmpd
            v.tensor_tensor(x_, ps[:, 0:TT * 64].rearrange("p (t h) -> p t h", t=TT),
                                 r_("dt_bias").unsqueeze(1).to_broadcast([P, TT, 64]), ALU.add).then_inc(is_free(("dt",))[0], 1)
            dve.wait_ge(*is_free(("dt",)))
            v.scalar_tensor_tensor(e_, x_, -1.0, x_, ALU.mult, ALU.min).then_inc(S_("dt_negabs"), 1)
            dve.wait_ge(S_("dt_exp"), 1)
            step(v.tensor_scalar(dt, e_, 1.0, None, ALU.add))
            v.scalar_tensor_tensor(eacs, dt, -1.0, e_, ALU.add, ALU.subtract).then_inc(S_("dt_w"), 1)
            dve.wait_ge(S_("dt_ln"), 1)
            step(v.tensor_tensor(wend, wend, eacs, ALU.subtract))
            step(v.scalar_tensor_tensor(dt, x_, 0.0, wend, ALU.max, ALU.add))
            dve.wait_ge(S_("nega"), 1)
            v.scalar_tensor_tensor(tmpd[0], dt, -1.0, nega.unsqueeze(1).to_broadcast([P, TT, 64]),
                                          ALU.mult, ALU.mult).then_inc(S_("dta"), 1)
            dve.wait_ge(*is_full(("acs",)))
            ps = bank(("acs",))
            for d in range(2):
                step(v.tensor_copy(acs[:, :, d * SH:(d + 1) * SH],
                                   ps[:, d * 192:(d + 1) * 192].rearrange("p (t h) -> p t h", t=TT)))
            v.tensor_copy(tmpd[1], ps[:, 512:512 + TT * 64].rearrange("p (t h) -> p t h", t=TT)).then_inc(is_free(("acs",))[0], 1)
            dve.wait_ge(*is_free(("acs",)))
            v.tensor_tensor(wend, tmpd[1], acs, ALU.subtract).then_inc(S_("acs_out"), 1)
            lat = acs[:, TC:TT, :].rearrange("p t (d h) -> p t d h", d=2)
            r4 = res.rearrange("p t (d h) -> p t d h", d=2)
            dve.wait_ge(S_("consts_in"), 16 * 2)
            step(v.tensor_copy(identb, ident))
            step(v.tensor_copy(selb[0:3 * SH, :], self_[0:3 * SH, :]))
            step(v.tensor_copy(acs3[:, :, :, 0, :], lat))
            step(v.tensor_tensor(r4, lat, acs3[:, :, :, 0, :], ALU.subtract))
            step(v.tensor_copy(acs3[:, :, :, 1, :], r4))
            step(v.tensor_tensor(r4, r4, acs3[:, :, :, 1, :], ALU.subtract))
            v.tensor_copy(acs3[:, :, :, 2, :], r4).then_inc(S_("acs_split"), 1)
            dve.wait_ge(S_("acs_exps"), 3)
            step(v.tensor_tensor(wend, wend, dt, ALU.mult))

            heads = lambda x: x.rearrange("p (h q) -> p h q", h=HPG)

            def conv(g, kind, m):
                rn = g * 6 + {"x": m, "B": 4, "C": 5}[kind]
                blk = {"x": g * 4 + m, "B": 16 + g, "C": 20 + g}[kind]
                key = ("x", g, m) if kind == "x" else (kind, g)
                dve.wait_ge(*is_free(key))
                if rn:
                    if kind == "x" and m:
                        dve.wait_ge(S_("xc_ready"), g * 4 + m)
                    elif kind == "x":
                        dve.wait_ge(S_("CT_ready"), g)
                    elif kind == "B":
                        dve.wait_ge(S_("xc_ready"), g * 4 + 4)
                    else:
                        dve.wait_ge(S_("BT_ready"), g + 1)
                lo, hi = (0, C + 4 + T) if kind != "C" else (C + 4, C + 4 + T)
                w = c_("conv_w")
                src = raw[rn % 2]
                step(v.tensor_scalar(cacc[:, lo:hi], src[:, lo:hi], w[:, blk * SK:blk * SK + 1], None, ALU.mult))
                for k in range(1, SK):
                    ins = v.scalar_tensor_tensor(cacc[:, lo:hi], src[:, lo + k:hi + k],
                                                 w[:, blk * SK + k:blk * SK + k + 1], cacc[:, lo:hi], ALU.mult, ALU.add)
                    if k < SK - 1:
                        step(ins)
                ins.then_inc(S_("conv_done"), 1)

            for g in range(SG):
                for m in range(4):
                    conv(g, "x", m)
                conv(g, "B", 0)
                conv(g, "C", 0)
                key = ("CB", g)
                dve.wait_ge(*is_full(key))
                ps = bank(key)
                for d in range(2):
                    ins = v.tensor_tensor(cb[d], ps[:, :].rearrange("p (c l) -> p c l", c=TL),
                                          mask[d].unsqueeze(1).to_broadcast([P, TL, P]), ALU.mult)
                    if d == 0:
                        step(ins)
                ins.then_inc(is_free(key)[0], 1)
                dve.wait_ge(*is_free(key))
                for m in range(4):
                    dve.wait_ge(*is_free(("xtok", g, m, 1)))
                if g:
                    dve.wait_ge(*is_full(("yT", g - 1, 3)))
                    dve.wait_ge(S_("yz_squared"), g * 4)
                dsk = r_("ssd_d")[:, g * HPG:(g + 1) * HPG].unsqueeze(2).to_broadcast([P, HPG, SHD])
                for c in range(TL):
                    step(v.tensor_tensor(heads(yacc[:, c, :]), heads(xtok[:, TC + c, :]), dsk, ALU.mult))
                for d in range(2):
                    order = [0, 1, 2, 3, 4, 5] if d == 0 else [1, 0, 5, 4, 3, 2]
                    hs = d * SH + g * HPG
                    per_head = lambda q, t: q[:, t, hs:hs + HPG].unsqueeze(2).to_broadcast([P, HPG, SHD])

                    def make_xw(i):
                        if i >= 2:
                            dve.wait_ge(*is_full(("kv", g, d, i - 2)))
                        elif g or d:
                            dve.wait_ge(*is_full(("kv", g if d else g - 1, 1 - d, 4)))
                        v.tensor_tensor(heads(xw[i % 2]), heads(xtok[:, order[i], :]), per_head(wend, order[i]),
                                               ALU.mult).then_inc(S_("xw_ready"), 1)

                    make_xw(0)
                    make_xw(1)
                    for i in range(6):
                        if i >= 2:
                            key = ("off", g, d, i)
                            dve.wait_ge(*is_full(key))
                            ps = bank(key)
                            c = order[i] - TC
                            v.tensor_tensor(heads(vtmp), heads(ps[:, :]), per_head(eacs, order[i]), ALU.mult).then_inc(is_free(key)[0], 1)
                            dve.wait_ge(*is_free(key))
                            step(v.tensor_tensor(yacc[:, c, :], yacc[:, c, :], vtmp, ALU.add))
                        if i < 5:
                            key = ("kv", g, d, i)
                            dve.wait_ge(*is_full(key))
                            ps = bank(key)
                            if i == 0:
                                ins = v.tensor_copy(S[0], ps[:, :])
                            else:
                                step(v.tensor_tensor(heads(vtmp), heads(S[(i - 1) % 2]), per_head(eend, order[i]),
                                                     ALU.mult))
                                ins = v.tensor_tensor(S[i % 2], vtmp, ps[:, :], ALU.add)
                            ins.then_inc(is_free(key)[0], 1)
                            dve.wait_ge(*is_free(key))
                            if i + 2 < 5:
                                make_xw(i + 2)
                    if g or d:
                        dve.wait_ge(*is_full(("y", g if d else g - 1, 1 - d)))
                    for c in range(TL):
                        ins = v.tensor_tensor(heads(xdt[:, c, :]), heads(xtok[:, TC + c, :]), per_head(dt, TC + c),
                                              ALU.mult)
                    ins.then_inc(S_("xdt_ready"), 1)

                    def masked(h):
                        n = (g * 2 + d) * HPG + h
                        dve.wait_ge(S_("decay_ready"), n + 1)
                        v.tensor_tensor(mm[n % NM], mm[n % NM], cb[d], ALU.mult).then_inc(S_("M_ready"), 1)

                    for h in range(HPG):
                        n = (g * 2 + d) * HPG + h
                        key = ("R", g, d, h)
                        dve.wait_ge(*is_full(key))
                        ps = bank(key)
                        if n >= NM:
                            o = n - NM
                            if o % HPG == HPG - 1:
                                dve.wait_ge(*is_full(("y", o // HPG // 2, o // HPG % 2)))
                            else:
                                dve.wait_ge(S_("M_used"), o // HPG * (HPG - 1) + o % HPG + 1)
                        for c in range(TL):
                            ins = v.tensor_scalar(mm[n % NM][:, c, :], ps[:, c * P:(c + 1) * P],
                                                  acs[:, TC + c, hs + h:hs + h + 1], 0.0, ALU.subtract, ALU.min)
                        ins.then_inc(is_free(key)[0], 1)
                        if h >= 1:
                            masked(h - 1)
                    masked(HPG - 1)
                    key = ("y", g, d)
                    dve.wait_ge(*is_full(key))
                    ps = bank(key)
                    for c in range(TL):
                        ins = v.tensor_tensor(yacc[:, c, :], yacc[:, c, :], ps[:, c * 512:(c + 1) * 512], ALU.add)
                        if c < TL - 1:
                            step(ins)
                    ins.then_inc(is_free(key)[0], 1)
                    dve.wait_ge(*is_free(key))
                for t in range(TL):
                    dve.wait_ge(*is_free(("z", g, t)))
                    v.tensor_tensor(yacc[:, t, :], yacc[:, t, :], sz, ALU.mult).then_inc(S_("yz_ready"), 1)
            dve.wait_ge(S_("yz_squared"), SG * TL)
            step(v.tensor_reduce(small[:, 0:TL], ssq, AX.X, ALU.add))
            dve.wait_ge(S_("yz_squared"), SG * TL)
            v.tensor_scalar(small[:, 8:8 + TL], small[:, 0:TL], 1.0 / SI, EPS, ALU.mult, ALU.add).then_inc(S_("ssd_var"), 1)
            dve.wait_ge(S_("ssd_std"), 1)
            v.reciprocal(small[:, 0:TL], small[:, 16:16 + TL]).then_inc(S_("ssd_rstd"), 1)
            dve.wait_ge(*is_free(("rrow",)))
            for m in range(KD):
                dve.wait_ge(*is_free(("gc", m)))
                step(v.tensor_tensor(gateT[:, m, :], gateT[:, m, :], rrow, ALU.mult))
            for m in range(KD):
                key = ("pc", m)
                dve.wait_ge(*is_full(key))
                ps = bank(key)
                v.tensor_tensor(mT[:, m, :], ps[:, :], gateT[:, m, :], ALU.mult).then_inc(is_free(key)[0], 1)
            phase_end(dve, 2)

            step(v.memset(pc[:, :, 0:1], 0.0))
            for h in range(GH):
                for d in range(2):
                    n = h * 2 + d
                    order = [0, 1, 2, 3, 4, 5] if d == 0 else [1, 0, 5, 4, 3, 2]
                    key = ("gz", n)
                    dve.wait_ge(*is_full(key))
                    ps = bank(key)
                    v.tensor_scalar(zb, ps[:, 0:NT], c_("a_b")[:, d * GH + h:d * GH + h + 1], None, ALU.add).then_inc(is_free(key)[0], 1)
                    dve.wait_ge(*is_free(key))
                    v.scalar_tensor_tensor(eb, zb, -1.0, zb, ALU.mult, ALU.min).then_inc(S_("gz_negabs"), 1)
                    dve.wait_ge(S_("gz_exp"), n + 1)
                    step(v.tensor_scalar(wb, eb, 1.0, None, ALU.add))
                    v.scalar_tensor_tensor(lb, wb, -1.0, eb, ALU.add, ALU.subtract).then_inc(S_("gz_w"), 1)
                    dve.wait_ge(S_("gz_ln"), n + 1)
                    step(v.tensor_tensor(wb, wb, lb, ALU.subtract))
                    step(v.scalar_tensor_tensor(zb, zb, 0.0, wb, ALU.min, ALU.subtract))
                    for t in range(TT):
                        step(v.tensor_tensor_scan(pc[:, t, 1:P + 1], ones, zb[:, t * P:(t + 1) * P], 0.0,
                                                  ALU.mult, ALU.add))
                    ref = pc[:, :, P // 2:P // 2 + 1]
                    step(v.tensor_tensor(dd, pc[:, :, 1:P + 1] if d == 0 else pc[:, :, 0:P],
                                         ref.to_broadcast([P, TT, P]), ALU.subtract))
                    v.tensor_tensor(dref, pc[:, :, P], pc[:, :, P // 2], ALU.subtract).then_inc(S_("decay_refd"), 1)
                    dve.wait_ge(S_("gla_exps"), n + 1)
                    if n == 0:
                        for m in range(4):
                            dve.wait_ge(*is_free(("k", m)))
                    step(v.scalar_tensor_tensor(eq.rearrange("p c l -> p (c l)"), eq.rearrange("p c l -> p (c l)"),
                                                float(GDK) ** -0.5, qT[:, h, :], ALU.mult, ALU.mult))
                    v.tensor_tensor(ek.rearrange("p c l -> p (c l)"), ek.rearrange("p c l -> p (c l)"),
                                           kT[:, h, :], ALU.mult).then_inc(S_("qk_ready"), 1)
                    key = ("sc", n)
                    dve.wait_ge(*is_full(key))
                    ps = bank(key)
                    v.tensor_tensor(sc, ps[:, :].rearrange("p (c l) -> p c l", c=TL),
                                         mask[d].unsqueeze(1).to_broadcast([P, TL, P]), ALU.mult).then_inc(is_free(key)[0], 1)
                    start, end = (ea, ebb) if d == 0 else (ebb, ea)
                    for i, t in enumerate(order):
                        if i < 5:
                            key = ("gkv", n, i)
                            dve.wait_ge(*is_full(key))
                            ps = bank(key)
                            src = ps[:, 0:GDV]
                            if i:
                                v.tensor_tensor(sadd, src, st[(i - 1) % 2], ALU.add).then_inc(is_free(key)[0], 1)
                                dve.wait_ge(*is_free(key))
                                src = sadd
                            ins = v.tensor_scalar(st[i % 2], src, end[:, t:t + 1], start[:, order[i + 1]:order[i + 1] + 1],
                                                  ALU.mult, ALU.mult)
                            if i:
                                ins.then_inc(S_("st_ready"), 1)
                                dve.wait_ge(S_("st_ready"), n * 4 + i)
                            else:
                                ins.then_inc(is_free(key)[0], 1)
                                dve.wait_ge(*is_free(key))
                        if i >= 2:
                            key = ("o", n, i)
                            dve.wait_ge(*is_full(key))
                            ps = bank(key)
                            o = otok[:, t - TC, h * GDV:(h + 1) * GDV]
                            if d == 0:
                                v.tensor_copy(o, ps[:, 0:GDV]).then_inc(is_free(key)[0], 1)
                            else:
                                v.tensor_tensor(o, o, ps[:, 0:GDV], ALU.add).then_inc(is_free(key)[0], 1)
                            dve.wait_ge(*is_free(key))
            step(v.tensor_scalar(sadd, sadd, 1.0, None, ALU.mult))
            v.tensor_copy(dref, dref).then_inc(S_("o_all"), 1)
            dve.wait_ge(S_("o_squared"), 1)
            v.tensor_scalar(gss, gss, 1.0 / GDV, EPS, ALU.mult, ALU.add).then_inc(S_("o_var"), 1)
            dve.wait_ge(S_("o_std"), 1)
            step(v.reciprocal(gss, gss))
            for c in range(TL):
                o = otok[:, c, :].rearrange("p (h q) -> p h q", h=GH)
                step(v.tensor_tensor(o, o, gss[:, c, :].unsqueeze(2).to_broadcast([P, GH, GDV]), ALU.mult))
            rbuf = [eb, wb]
            for j in range(2):
                for t in range(TL):
                    i = j * TL + t
                    dve.wait_ge(*is_free(("r", j, t)))
                    o = otok[:, t, j * 512:(j + 1) * 512]
                    v.tensor_tensor(o, o, rbuf[i % 2][:, 0:512], ALU.mult).then_inc(S_("o_gated"), 1)

            def merge(gate_name, name, tmp):
                for m in range(KD):
                    dve.wait_ge(*is_free((gate_name, m)))
                    key = (name, m)
                    dve.wait_ge(*is_full(key))
                    ps = bank(key)
                    v.tensor_tensor(tmp, ps[:, :], gateT[:, m, :], ALU.mult).then_inc(is_free(key)[0], 1)
                    dve.wait_ge(*is_free(key))
                    step(v.tensor_tensor(mT[:, m, :], mT[:, m, :], tmp, ALU.add))

            merge("ga", "pa", zb[:, 0:T])
            phase_end(dve, 3)

            for m in range(KD):
                dve.wait_ge(*is_free(("u", m)))
            H = T // 2
            v.tensor_tensor(ue[:, :, 1:H], uT[:, :, 1:H], uT[:, :, T - 1:H:-1], ALU.add)
            v.tensor_tensor(uo[:, :, 1:H], uT[:, :, 1:H], uT[:, :, T - 1:H:-1], ALU.subtract)
            v.tensor_copy(ue[:, :, 0:1], uT[:, :, 0:1])
            v.memset(uo[:, :, 0:1], 0.0).then_inc(S_("u_folded"), 1)
            merge("gb", "pb", At[:, 0, 0:T])
            for s in range(4, 12):
                modulation(s)
            for s in range(4, 12):
                dve.wait_ge(*is_free(("mod", s)))
            step(v.scalar_tensor_tensor(modA[:, 2, :], mod[:, 4 * KD:5 * KD, 0], 1.0, c_("norm2"), ALU.add, ALU.mult))
            phase_end(dve, 4)

            dve.wait_ge(S_("xr_in"), 32)
            step(v.tensor_tensor(xr, xr, pos2, ALU.add))
            for j in range(2):
                dve.wait_ge(*is_free(("g1", j)))
                dve.wait_ge(*is_free(("g2", j)))
            for j in range(2):
                for t in range(TL):
                    key = ("wo", j, t)
                    dve.wait_ge(*is_full(key))
                    ps = bank(key)
                    sl = slice(j * 512, (j + 1) * 512)
                    v.tensor_tensor(yo[:, t, sl], ps[:, :], g1row[:, sl], ALU.mult).then_inc(is_free(key)[0], 1)
                    dve.wait_ge(*is_free(key))
                    v.tensor_tensor(xr[:, t, sl], xr[:, t, sl], yo[:, t, sl], ALU.add).then_inc(S_("x1_ready"), 1)
            rstd(small[:, 24:24 + TL], small[:, 0:TL], small[:, 8:8 + TL], small[:, 16:16 + TL], TL, D,
                 "x1_ss", TL, "x1_var", "x1_std")
            dve.wait_ge(S_("x1_ready"), 2 * TL)
            for t in range(TL):
                v.tensor_scalar(yo[:, t, :], xr[:, t, :], small[:, 24 + t:25 + t], None, ALU.mult).then_inc(S_("x1_normed"), 1)

            dve.wait_ge(*is_free(("route",)))
            step(v.tensor_tensor(sel, score, r_("router_b").unsqueeze(1).to_broadcast([P, TL, NE]), ALU.add))
            G = TL * NG
            q = sel.rearrange("p t (g e) -> p (t g) e", g=NG)
            f = lambda x, i: x.rearrange("p t (i g) -> p i (t g)", i=NG)[:, i, :]
            fl = lambda x, i: x.rearrange("p t e -> p (t e)")[:, i * G:(i + 1) * G]
            for i in range(2):
                step(v.tensor_tensor(fl(ra, i), q[:, :, 2 * i], q[:, :, 2 * i + 1], ALU.max))
                step(v.tensor_tensor(fl(ra, 2 + i), q[:, :, 2 * i], q[:, :, 2 * i + 1], ALU.min))
            step(v.tensor_tensor(fl(rb, 0), fl(ra, 0), fl(ra, 1), ALU.max))
            step(v.tensor_tensor(fl(rb, 1), fl(ra, 0), fl(ra, 1), ALU.min))
            step(v.tensor_tensor(fl(rb, 2), fl(ra, 2), fl(ra, 3), ALU.max))
            step(v.tensor_tensor(fl(rb, 1), fl(rb, 1), fl(rb, 2), ALU.max))
            step(v.tensor_tensor(fl(rb, 0), fl(rb, 0), fl(rb, 1), ALU.add))
            gs = fl(rb, 0).rearrange("p (t g) -> p t g", t=TL)

            def first_max(dst, src, weights, n, red, tmp):
                step(v.tensor_reduce(red, src, AX.X, ALU.max))
                step(v.tensor_tensor(tmp, src, red.unsqueeze(2).to_broadcast([P, TL, n]), ALU.is_equal))
                step(v.tensor_tensor(tmp, tmp, weights.unsqueeze(1).to_broadcast([P, TL, n]), ALU.mult))
                step(v.tensor_reduce(red, tmp, AX.X, ALU.max))
                step(v.tensor_tensor(dst, tmp, red.unsqueeze(2).to_broadcast([P, TL, n]), ALU.is_equal))

            red = small[:, 56:56 + TL]
            bestg = fl(rb, 2).rearrange("p (t g) -> p t g", t=TL)
            tmpg = fl(rb, 3).rearrange("p (t g) -> p t g", t=TL)
            first_max(bestg, gs, r_("first4"), NG, red, tmpg)
            step(v.tensor_scalar(tmpg, bestg, 1.0, BIG, ALU.subtract, ALU.mult))
            step(v.tensor_tensor(ra.rearrange("p t (g e) -> p (t g) e", g=NG), q,
                                 fl(rb, 3).unsqueeze(2).to_broadcast([P, G, EPG]), ALU.add))
            first_max(rc, ra, r_("first16"), NE, red, sel)
            step(v.scalar_tensor_tensor(ra, rc, -4.0 * BIG, ra, ALU.mult, ALU.add))
            first_max(rb, ra, r_("first16"), NE, red, sel)
            step(v.tensor_tensor(rc, rc, rb, ALU.add))
            step(v.tensor_tensor(rc, rc, score, ALU.mult))
            step(v.tensor_reduce(red, rc, AX.X, ALU.add))
            step(v.reciprocal(small[:, 60:60 + TL], red))
            step(v.tensor_tensor(gate, rc, small[:, 60:60 + TL].unsqueeze(2).to_broadcast([P, TL, NE]), ALU.mult))

            for e in range(NE):
                for m in range(4):
                    dve.wait_ge(*is_free(("w1", e, m)))
                    key = ("w3", e, m)
                    dve.wait_ge(*is_full(key))
                    ps = bank(key)
                    n = e * 4 + m
                    if e:
                        dve.wait_ge(*is_full(("w2", e - 1, TL - 1, 1)))
                    ins = v.tensor_tensor(heT[:, m, :], sg[n % 2], ps[:, :], ALU.mult)
                    ins.then_inc(is_free(key)[0], 1)
                for t in range(TL):
                    for j in range(2):
                        key = ("w2", e, t, j)
                        dve.wait_ge(*is_full(key))
                        ps = bank(key)
                        y = yo[:, t, j * 512:(j + 1) * 512]
                        w = gate[:, t, e:e + 1]
                        if e == 0:
                            ins = v.tensor_scalar(y, ps[:, :], w, None, ALU.mult)
                        else:
                            dve.wait_ge(*is_free(("w2", e - 1, t, j)))
                            ins = v.scalar_tensor_tensor(y, ps[:, :], w, y, ALU.mult, ALU.add)
                        ins.then_inc(is_free(key)[0], 1)
            for t in range(TL):
                for j in range(2):
                    dve.wait_ge(*is_free(("w2", NE - 1, t, j)))
                step(v.tensor_tensor(yo[:, t, :], yo[:, t, :], g2row, ALU.mult))
                v.tensor_tensor(xr[:, t, :], xr[:, t, :], yo[:, t, :], ALU.add).then_inc(S_("x2_ready"), 1)
            rstd(small[:, 24:24 + TL], small[:, 32:32 + TL], small[:, 40:40 + TL], small[:, 48:48 + TL], TL, D,
                 "x2_ss", TL, "x2_var", "x2_std")
            dve.wait_ge(S_("x2_ready"), TL)
            dve.wait_ge(S_("frow_in"), 16)
            for t in range(TL):
                v.scalar_tensor_tensor(yo[:, t, :], xr[:, t, :], small[:, 24 + t:25 + t], frow,
                                              ALU.mult, ALU.mult).then_inc(S_("out_ready"), 1)


def grid_positions():
    t = np.arange(T)
    quarter = D // 4
    freqs = np.exp(-np.log(10000.0) * np.arange(quarter, dtype=np.float32) / quarter).astype(np.float32)
    ar = (t // GRID_W).astype(np.float32)[:, None] * freqs
    ac = (t % GRID_W).astype(np.float32)[:, None] * freqs
    return np.concatenate([np.sin(ar), np.cos(ar), np.sin(ac), np.cos(ac)], axis=-1).astype(np.float32)


def constants():
    i = np.arange(P)
    squares = np.concatenate([np.eye(P), i[:, None] <= i[None, :], i[:, None] >= i[None, :], np.ones((P, P))], axis=1)
    k = np.arange(T)
    h = np.arange(T // 2)
    time = np.concatenate([np.cos(2 * np.pi * np.outer(h, k) / T), np.sin(2 * np.pi * np.outer(h, k) / T)])
    time[T // 2] = np.cos(np.pi * k)
    ang = 2 * np.pi * np.outer(np.arange(FG), np.arange(FG)) / FG
    unit = 1.0 / np.sqrt(T * FG)
    return {
        "squares": squares.astype(np.float32),
        "sel": np.tile(np.eye(SH), (3, 1)).astype(np.float32),
        "pos": grid_positions(),
        "dft_time": time.astype(np.float32),
        "dft_cos": (unit * np.cos(ang)).astype(np.float32),
        "dft_sin": (-unit * np.sin(ang)).astype(np.float32),
    }


def kernel(**inputs):
    import concourse.bacc as bacc
    from concourse.bass_utils import run_bass_kernel_spmd

    v = {k: np.asarray(x) for k, x in inputs.items()}
    f = np.float32

    def blocks(x):
        return np.ascontiguousarray(x.reshape(-1, P).T)

    both = np.stack([v["c"][0].reshape(KD, P), v["c_ctx"].reshape(KD, P)], axis=1).reshape(2 * KD, P).T
    conv_w = v["ssd_conv_w"][0].T.reshape(SCD // P, P, SK).transpose(1, 0, 2).reshape(P, -1)
    cols = np.concatenate([both, blocks(v["ada_b"][0]), blocks(v["norm1_g"][0]), blocks(v["norm2_g"][0]),
                           blocks(v["gla_a_b"][0].reshape(-1)), blocks(v["gla_norm_g"][0]), conv_w,
                           blocks(v["ssd_conv_b"][0]), blocks(v["ssd_norm_g"][0])], axis=1)
    rows = np.concatenate([v["ssd_dt_bias"][0].reshape(-1), v["ssd_a_log"][0].reshape(-1), v["ssd_d"][0],
                           v["router_b"], np.arange(NE, 0, -1, dtype=f), np.arange(NG, 0, -1, dtype=f)])
    arrays = {"cols": cols, "rows": np.broadcast_to(rows, (P, NROW)), "final_row": np.broadcast_to(v["final_g"], (P, D))}
    arrays.update(constants())
    for name in ("x", "ctx", "ada_w", "w_in", "gla_a_w", "gla_proj", "fnet_proj", "ssd_proj", "w_out", "router_w",
                 "exp_w1", "exp_w3", "exp_w2"):
        arrays[name] = v[name]
    arrays = {k: np.ascontiguousarray(x) for k, x in arrays.items()}
    nc = bacc.Bacc("TRN2", target_bir_lowering=False, num_devices=1)
    aps = {k: nc.dram_tensor(f"{k}_d", x.shape, mybir.dt.from_np(x.dtype), kind="ExternalInput").ap()
           for k, x in arrays.items()}
    out = nc.dram_tensor("out_d", (1, T, D), F32, kind="ExternalOutput").ap()
    build(nc, aps, out)
    r = run_bass_kernel_spmd(nc, [{f"{k}_d": x for k, x in arrays.items()}], core_ids=[0])
    return r.results[0]["out_d"]
```

```python
from contextlib import ExitStack

import numpy as np

import concourse.bass as bass
from concourse import mybir

F32 = mybir.dt.float32
BF16 = mybir.dt.bfloat16
I32 = mybir.dt.int32
ALU = mybir.AluOpType
ACT = mybir.ActivationFunctionType
AX = mybir.AxisListType

P = 128
D = 1024
T = 512
C = 256
NT = C + T
KD = D // P
TL = T // P
TC = C // P
TT = TL + TC
EPS = 1e-6
N_MOD = 6
GRID_W = 64

GH, GDK, GDV = 4, 128, 256
GQK, GV, GR = GH * GDK, GH * GDV, 16
TAU = 16.0

SI, SHD, SH, SG, SN, SK = 2048, 64, 32, 4, 128, 5
HPG = SH // SG
GW = HPG * SHD
SGN = SG * SN
SCD = SI + 2 * SGN

NE, NG, EPG, FF = 16, 4, 4, 512

SIZES = (GQK, GQK, GV, GV, GR, GR, D, SI, SCD, SH, SH, D, D, D)
OFF = [sum(SIZES[:i]) for i in range(len(SIZES) + 1)]
Q0, K0, V0, R0, LR0, _, U0, Z0, X0, DT0, _, GA0, GB0, GC0, D_IN = OFF
B0, C0 = X0 + SI, X0 + SI + SGN

FG = D // 4
BIG = 1e30

ROWS_A_TILE = 128
XTILES = 2 * T // ROWS_A_TILE + NE + 2


def spans(sizes):
    at, out = 0, {}
    for name, n in sizes:
        out[name] = (at, at + n)
        at += n
    return out, at


COLS, NCOL = spans([("c", 2 * KD), ("ada_b", N_MOD * KD), ("norm1", KD), ("norm2", KD), ("a_b", 2 * GH),
                    ("gla_norm", GDV // P), ("conv_w", SCD // P * SK), ("conv_b", SCD // P), ("ssd_norm", SI // P)])
ROWS, NROW = spans([("dt_bias", 2 * SH), ("a_log", 2 * SH), ("ssd_d", SH), ("router_b", NE),
                    ("first16", NE), ("first4", NG), ("filled_tiles", T // ROWS_A_TILE - 1)])
SQ, NSQ = spans([("ident", P), ("upto", P), ("from", P), ("ones", P)])


def build(nc, a, out):
    with ExitStack() as ctx:
        def sem(name):
            return ctx.enter_context(nc.semaphore(name))

        W = 53100
        arena = ctx.enter_context(nc.sbuf_tensor("arena", [P, W], F32))
        psum = ctx.enter_context(nc.psum_tensor("psum", [P, 8 * 512], F32))
        top = [0]

        def view(off, dims):
            n = int(np.prod(dims))
            v = arena[:, off:off + n]
            if len(dims) == 1:
                return v
            names = "abcde"[:len(dims)]
            return v.rearrange(f"p ({' '.join(names)}) -> p {' '.join(names)}", **dict(zip(names, dims)))

        def alloc(*dims):
            off = top[0]
            top[0] += int(np.prod(dims))
            top[0] += top[0] % 2
            assert top[0] <= W, top[0]
            return view(off, dims)

        NS = 3
        ring = [alloc(8 * 512) for _ in range(NS)]
        col = alloc(NCOL)
        row = alloc(NROW)
        sq = alloc(NSQ)
        identb = alloc(P // 2).bitcast(BF16)
        selb = alloc(SH // 2).bitcast(BF16)
        self_ = alloc(SH)
        wsmall = alloc(KD, 2 * GR + 2 * SH)
        mod = alloc(N_MOD * KD, 2)
        modA = alloc(3, KD)
        small = alloc(64)
        base = top[0]
        hT = alloc(KD, NT)
        phase_base = top[0]

        def c_(name):
            return col[:, COLS[name][0]:COLS[name][1]]

        def r_(name):
            return row[:, ROWS[name][0]:ROWS[name][1]]

        def s_(name):
            return sq[:, SQ[name][0]:SQ[name][1]]

        ident = s_("ident")
        mask = [s_("upto"), s_("from")]
        ones = s_("ones")

        xs = alloc(TT, D)
        pos = alloc(TL, D)
        junk = alloc(D)
        modrow = alloc(4 * 512)
        top[0] = phase_base
        dt = alloc(TT, 2 * SH)
        acs = alloc(TT, 2 * SH)
        eacs = alloc(TT, 2 * SH)
        wend = alloc(TT, 2 * SH)
        eend = alloc(TT, 2 * SH)
        nega = alloc(2 * SH)
        tmpd = [alloc(TT, 2 * SH) for _ in range(2)]
        acs3 = alloc(TL * 2 * 3 * SH // 2).bitcast(BF16).rearrange("p (t d s h) -> p t d s h", t=TL, d=2, s=3)
        rowsT = alloc(2 * T // 2).bitcast(BF16).rearrange("p (d t) -> p d t", d=2)
        RAW = C + T + 8
        LAT = C + 6
        raw = [alloc(RAW) for _ in range(2)]
        cacc = alloc(RAW)
        xcT = alloc(NT)
        BT = alloc(NT)
        CT = alloc(T)
        Btok = alloc(TT, P)
        xtok = alloc(TT, GW)
        xw = [alloc(GW) for _ in range(2)]
        xdt = alloc(TL, GW)
        yacc = alloc(TL, GW)
        cb = [alloc(TL, P) for _ in range(2)]
        NM = 4
        mm = [alloc(TL, P) for _ in range(NM)]
        S = [alloc(GW) for _ in range(2)]
        vtmp = alloc(GW)
        sz = alloc(TL, GW)
        yT = alloc(SI // P, T)
        ssq = alloc(TL, SG)
        rrow = alloc(T)
        res = alloc(TL, 2 * SH)
        top[0] = phase_base
        gateT = alloc(KD, T)
        mT = alloc(KD, T)
        gate_top = top[0]

        top[0] = gate_top
        qT = alloc(GH, T)
        kT = alloc(GH, NT)
        vtok = alloc(TT, GV)
        otok = alloc(TL, GV)
        lr2 = alloc(2, NT)
        aw = alloc(2, GQK)
        zb = alloc(NT)
        eb = alloc(NT)
        wb = alloc(NT)
        lb = alloc(NT)
        pc = alloc(TT, P + 1)
        dd = lb.rearrange("p (t l) -> p t l", t=TT)
        eq = alloc(TL, P)
        ek = alloc(TT, P)
        ekT = zb.rearrange("p (t l) -> p t l", t=TT)
        sc = alloc(TL, P)
        st = [alloc(GDV) for _ in range(2)]
        sadd = alloc(GDV)
        ea = alloc(TT)
        ebb = alloc(TT)
        fac = alloc(TT)
        dref = alloc(TT)
        gss = alloc(TL, GH)

        top[0] = gate_top
        uT = alloc(KD, T)
        ue = alloc(KD, T // 2)
        uo = alloc(KD, T // 2)
        At = alloc(TL, D)
        fT = alloc(TL, T)
        fC = alloc(2, FG)
        fS = alloc(2, FG)
        fyT = alloc(KD, T)
        ada_acc = alloc(8, 512)
        top[0] = base
        xr = alloc(TL, D)
        g1row = alloc(D)
        g2row = alloc(D)
        assert top[0] <= phase_base
        pos2 = view(phase_base, (TL, D))
        h2T = view(phase_base, (KD, T))
        top[0] = gate_top
        frow = alloc(D)
        yo = alloc(TL, D)
        rw = alloc(KD, NE)
        score = alloc(TL, NE)
        sel = alloc(TL, NE)
        ra = alloc(TL, NE)
        rb = alloc(TL, NE)
        rc = alloc(TL, NE)
        oh = [alloc(TL, NE) for _ in range(2)]
        slot_of = alloc(TL, NE)
        cnt = alloc(NE)
        over = alloc(NE, T // ROWS_A_TILE - 1)
        ntile = alloc(NE)
        first_tile = alloc(NE + 2)
        first_tile_i = alloc(NE + 2).bitcast(I32)
        share = alloc(2, TL)
        xidx = alloc(2 * TL).bitcast(I32)
        yidx = alloc(2 * TL).bitcast(I32)
        xrow = alloc(D)
        XT = alloc(KD, ROWS_A_TILE)
        sg = alloc(FF // P, ROWS_A_TILE)
        heT = alloc(FF // P, ROWS_A_TILE)
        YT = alloc(KD, ROWS_A_TILE)
        ysb = alloc(D)
        junk2 = xrow
        wset0 = top[0]
        wmem = [[alloc(8 * 512) for _ in range(3)], ring]
        yback = view(wset0, (2 * TL, D))
        v_off = gate_top + GH * T + GH * NT
        oT = view(v_off, (KD, T))
        zeros = yT[:, 0:2, :].rearrange("p a b -> p (a b)")
        slots = nc.dram_tensor("slots", [XTILES * ROWS_A_TILE, D], F32).ap()

        full = [sem(f"bank{b}_full") for b in range(8)]
        free = [sem(f"bank{b}_free") for b in range(8)]
        strip_in = [sem(f"strip{s}_in") for s in range(NS)]
        made = {}

        def S_(name):
            if name not in made:
                made[name] = sem(name)
            return made[name]

        turn = [0] * 8
        owner = [None] * 8
        place = {}
        nxt = {}

        def bank(key):
            b, n, _ = place[key]
            return psum[:, b * 512:(b + n) * 512]

        def is_full(key):
            return full[place[key][0]], place[key][2] + 1

        def is_free(key):
            return free[place[key][0]], place[key][2] + 1

        def open_(pe, key, n=1, lo=0, hi=8):
            b = nxt.get((lo, hi), lo)
            if b + n > hi:
                b = lo
            nxt[(lo, hi)] = b + n if b + n < hi else lo
            for o in dict.fromkeys(owner[b:b + n]):
                if o is not None:
                    pe.wait_ge(*is_free(o))
            assert key not in place, key
            place[key] = (b, n, turn[b])
            turn[b] += 1
            owner[b:b + n] = [key] * n
            return bank(key)

        strips = []
        ada_at = {}

        def strip(pe, pieces):
            n = len(strips)
            strips.append([pieces, None])
            pe.wait_ge(strip_in[n % NS], 16 * sum(len(strips[i][0]) for i in range(n % NS, n + 1, NS)))
            return ring[n % NS]

        def strip_used(key):
            strips[-1][1] = key

        def w_cols(w, c0, n=512, r0=0, rows=D):
            return w[r0:r0 + rows, c0:c0 + n].rearrange("(k p) n -> p k n", p=P)

        def full_strip(pe, w, c0, n=512, r0=0, rows=D):
            k = rows // P
            slot = strip(pe, [(lambda s: s[:, 0:k * n].rearrange("p (k n) -> p k n", k=k), w_cols(w, c0, n, r0, rows))])
            return slot[:, 0:k * n].rearrange("p (k n) -> p k n", k=k)

        w_in = a["w_in"][0]
        ada_w = a["ada_w"][0]

        Z_PARTS = (3, 3, 3, 3, 3, 1)

        side = [("v", 1, t) for t in range(TT)] + [("ga", m) for m in range(KD)]
        SIDE_AHEAD = len(side) * KD // (2 * GH) - TT

        block = ctx.enter_context(nc.Block())
        ENG = 3

        def phase_end(eng, n):
            eng.drain().then_inc(S_("phase_done"), 1)
            eng.wait_ge(S_("phase_done"), ENG * n)

        def x_turn(pe, g, m):
            pe.wait_ge(S_("xc_ready"), g * 4 + m + 1)
            for half in range(2):
                key = ("xtok", g, m, half)
                ps = open_(pe, key)
                for t in range(3):
                    tt = half * 3 + t
                    ins = nc.tensor.transpose(ps[:, t * P:(t + 1) * P], xcT[:, tt * P:(tt + 1) * P], ident)
                ins.then_inc(is_full(key)[0], 1)

        def gla_z(pe, h, d):
            pe.wait_ge(*is_free(("lr", 1)))
            key = ("gz", h * 2 + d)
            ps = open_(pe, key, 2, 0, 2)
            for c0, c1 in ((0, T), (T, NT)):
                ins = nc.tensor.matmul(ps[:, c0:c1], aw[0:GR, d, h * P:(h + 1) * P], lr2[0:GR, d, c0:c1],
                                       start=True, stop=True)
            ins.then_inc(is_full(key)[0], 1)

        @block.tensor
        def _(pe):
            mmul = nc.tensor.matmul

            def project_T(slot, m, src, key, nlat=True, nctx=False, koff=0, kn=KD):
                ps = open_(pe, key, 2 if nctx else 1)
                for k in range(kn):
                    ins = mmul(ps[:, 0:T], slot[:, k, m * P:(m + 1) * P], src[:, k, C:NT],
                               start=(k == 0), stop=(k == kn - 1))
                if nctx:
                    for k in range(kn):
                        ins = mmul(ps[:, T:T + C], slot[:, k, m * P:(m + 1) * P], src[:, k, 0:C],
                                   start=(k == 0), stop=(k == kn - 1))
                ins.then_inc(is_full(key)[0], 1)

            def project_tok(slot, n, src, t, key):
                ps = open_(pe, key)
                for k in range(KD):
                    ins = mmul(ps[:, 0:n], src[:, k, t * P:(t + 1) * P], slot[:, k, 0:n],
                               start=(k == 0), stop=(k == KD - 1))
                ins.then_inc(is_full(key)[0], 1)

            def ada_strip(s):
                n = len(strips)
                pieces = [(lambda q: q.rearrange("p (k n) -> p k n", k=KD), w_cols(ada_w, s * 512))]
                strips.append([pieces, ("sem", "ada_summed", s - 3)])
                ada_at[s] = (ring[n % NS].rearrange("p (k n) -> p k n", k=KD), strip_in[n % NS],
                             16 * sum(len(strips[i][0]) for i in range(n % NS, n + 1, NS)))

            pe.wait_ge(S_("c_act"), 1)
            for s in range(4):
                slot = full_strip(pe, ada_w, s * 512)
                key = ("modrow", s)
                ps = open_(pe, key)
                for k in range(KD):
                    ins = mmul(ps[0:2, :], c_("c")[:, 2 * k:2 * k + 2], slot[:, k, :],
                               start=(k == 0), stop=(k == KD - 1))
                ins.then_inc(is_full(key)[0], 1)
                strip_used(key)
            pe.wait_ge(S_("consts_in"), 16 * 2)
            for k in range(KD):
                pe.wait_ge(S_("x_normed"), TT)
                for key, t0, n in ((("hT", k), TC, TL), (("hTc", k), 0, TC)):
                    ps = open_(pe, key)
                    for t in range(n):
                        ins = nc.tensor.transpose(ps[:, t * P:(t + 1) * P], xs[:, t0 + t, k * P:(k + 1) * P], ident)
                    ins.then_inc(is_full(key)[0], 1)
                if k == 0:
                    for s in range(4):
                        pe.wait_ge(*is_free(("modrow", s)))
                    key = ("mod",)
                    ps = open_(pe, key)
                    for m in range(16):
                        ins = mmul(ps[:, 2 * m:2 * m + 2], modrow[0:2, m * P:(m + 1) * P], ident[0:2, 0:2],
                                   start=True, stop=True)
                    ins.then_inc(is_full(key)[0], 1)
            for k in range(KD):
                pe.wait_ge(*is_free(("hT", k)))
                pe.wait_ge(*is_free(("hTc", k)))
            phase_end(pe, 1)

            pe.wait_ge(S_("small_in"), 16 * 4)
            key = ("dt",)
            ps = open_(pe, key)
            for t in range(TT):
                for k in range(KD):
                    ins = mmul(ps[:, t * 64:(t + 1) * 64], hT[:, k, t * P:(t + 1) * P], wsmall[:, k, 2 * GR:],
                               start=(k == 0), stop=(k == KD - 1))
            ins.then_inc(is_full(key)[0], 1)
            pe.wait_ge(S_("dta"), 1)
            key = ("acs",)
            ps = open_(pe, key, 2)
            dta = tmpd[0]
            for d in range(2):
                ins = mmul(ps[:, d * 192:(d + 1) * 192], mask[d], dta[:, :, d * SH:(d + 1) * SH], start=True, stop=True)
            ins = mmul(ps[:, 512:512 + TT * 64], ones, dta[:, :, :].rearrange("p t h -> p (t h)"), start=True, stop=True)
            ins.then_inc(is_full(key)[0], 1)
            pe.wait_ge(S_("acs_split"), 1)
            for d in range(2):
                key = ("acsT", d)
                ps = open_(pe, key).bitcast(BF16)
                for t in range(TL):
                    ins = nc.tensor.transpose(ps[0:3 * SH, t * P:(t + 1) * P],
                                              acs3[:, t, d, :, :].rearrange("p s h -> p (s h)"), identb)
                ins.then_inc(is_full(key)[0], 1)

            def y_turn(g):
                pe.wait_ge(S_("yz_ready"), (g + 1) * TL)
                for m in range(4):
                    key = ("yT", g, m)
                    ps = open_(pe, key)
                    for c in range(TL):
                        ins = nc.tensor.transpose(ps[:, c * P:(c + 1) * P], yacc[:, c, m * P:(m + 1) * P], ident)
                    ins.then_inc(is_full(key)[0], 1)

            for g in range(SG):
                slot = full_strip(pe, w_in, X0 + g * GW)
                for m in range(4):
                    project_T(slot, m, hT, ("x", g, m), nctx=True)
                    strip_used(("x", g, m))
                    if m == 0 and g:
                        y_turn(g - 1)
                    if m >= 1:
                        x_turn(pe, g, m - 1)
                slot = strip(pe, [(lambda s: s[:, 0:2048].rearrange("p (k n) -> p k n", k=KD)[:, :, 0:P],
                                   w_cols(w_in, B0 + g * SN, SN)),
                                  (lambda s: s[:, 0:2048].rearrange("p (k n) -> p k n", k=KD)[:, :, P:2 * P],
                                   w_cols(w_in, C0 + g * SN, SN))])[:, 0:2048].rearrange("p (k n) -> p k n", k=KD)
                project_T(slot, 0, hT, ("B", g), nctx=True)
                project_T(slot, 1, hT, ("C", g))
                strip_used(("C", g))
                x_turn(pe, g, 3)
                slot = full_strip(pe, w_in, Z0 + g * GW)
                z_done = [0]

                def z_part(n):
                    for q in range(z_done[0], z_done[0] + n):
                        t, k = q // KD, q % KD
                        key = ("z", g, t)
                        if k == 0:
                            open_(pe, key, 1, 0, 4)
                        ins = mmul(bank(key)[:, :], hT[:, k, (TC + t) * P:(TC + t + 1) * P], slot[:, k, :],
                                   start=(k == 0), stop=(k == KD - 1))
                        if k == KD - 1:
                            ins.then_inc(is_full(key)[0], 1)
                    z_done[0] += n

                pe.wait_ge(S_("BT_ready"), g + 1)
                for half in range(2):
                    key = ("Btok", g, half)
                    ps = open_(pe, key)
                    for t in range(3):
                        tt = half * 3 + t
                        ins = nc.tensor.transpose(ps[:, t * P:(t + 1) * P], BT[:, tt * P:(tt + 1) * P], ident)
                    ins.then_inc(is_full(key)[0], 1)
                pe.wait_ge(S_("CT_ready"), g + 1)
                key = ("CB", g)
                ps = open_(pe, key)
                for c in range(TL):
                    ins = mmul(ps[:, c * P:(c + 1) * P], BT[:, C + c * P:C + (c + 1) * P],
                               CT[:, c * P:(c + 1) * P], start=True, stop=True)
                ins.then_inc(is_full(key)[0], 1)

                for d in range(2):
                    order = [0, 1, 2, 3, 4, 5] if d == 0 else [1, 0, 5, 4, 3, 2]
                    pe.wait_ge(*is_free(("Btok", g, 1)))
                    nh = [0]

                    def rows_of(h):
                        key = ("R", g, d, h)
                        ps = open_(pe, key, 1, 0, 4)
                        hh = g * HPG + h
                        pe.wait_ge(*is_free(("acsT", d)))
                        ins = mmul(ps[:, :], selb[0:3 * SH, hh:hh + 1].to_broadcast([3 * SH, P]),
                                   rowsT[0:3 * SH, d, :], start=True, stop=True)
                        ins.then_inc(is_full(key)[0], 1)

                    for i, t in enumerate(order):
                        if i >= 2:
                            key = ("off", g, d, i)
                            ps = open_(pe, key, 1, 4, 8)
                            pe.wait_ge(*is_free(("kv", g, d, i - 1)))
                            ins = mmul(ps[:, :], CT[:, (t - TC) * P:(t - TC + 1) * P], S[(i - 1) % 2][:, :],
                                       start=True, stop=True)
                            ins.then_inc(is_full(key)[0], 1)
                        if i < 5:
                            key = ("kv", g, d, i)
                            pe.wait_ge(S_("xw_ready"), (g * 2 + d) * 5 + i + 1)
                            ps = open_(pe, key, 1, 4, 8)
                            ins = mmul(ps[:, :], Btok[:, t, :], xw[i % 2][:, :], start=True, stop=True)
                            ins.then_inc(is_full(key)[0], 1)
                        z_part(Z_PARTS[i])
                    pe.wait_ge(S_("xdt_ready"), g * 2 + d + 1)
                    ys = [None] * TL
                    rows_of(0)
                    rows_of(1)
                    yb = open_(pe, ("y", g, d), 4, 4, 8)
                    for h in range(HPG):
                        n = (g * 2 + d) * HPG + h
                        if h + 2 < HPG:
                            rows_of(h + 2)
                        pe.wait_ge(S_("M_ready"), n + 1)
                        for c in range(TL):
                            ins = mmul(yb[:, c * 512 + h * SHD:c * 512 + (h + 1) * SHD], mm[n % NM][:, c, :],
                                       xdt[:, c, h * SHD:(h + 1) * SHD], start=True, stop=True)
                        if h < HPG - 1:
                            ins.then_inc(S_("M_used"), 1)
                    ins.then_inc(is_full(("y", g, d))[0], 1)
                strip_used(("z", g, TL - 1))
            y_turn(SG - 1)
            pe.wait_ge(*is_free(("yT", SG - 1, 3)))

            pe.wait_ge(S_("ssd_rstd"), 1)
            key = ("rrow",)
            ps = open_(pe, key)
            for c in range(TL):
                ins = mmul(ps[:, c * P:(c + 1) * P], small[:, c:c + 1].to_broadcast([P, P]), ident,
                           start=True, stop=True)
            ins.then_inc(is_full(key)[0], 1)

            def gate_T(c0, name, ada=(None, None)):
                for j in range(2):
                    slot = full_strip(pe, w_in, c0 + j * 512)
                    for m in range(4):
                        project_T(slot, m, hT, (name, j * 4 + m))
                        strip_used((name, j * 4 + m))
                    if ada[j]:
                        ada_strip(ada[j])

            gate_T(GC0, "gc")
            for j in range(2):
                keys = [("pc", j * 4 + m) for m in range(4)]
                for kh in range(2):
                    slot = full_strip(pe, a["ssd_proj"][0], j * 512, 512, kh * D, D)
                    if kh == 0:
                        pss = [open_(pe, k) for k in keys]
                    for m in range(4):
                        for k in range(KD):
                            ins = mmul(pss[m][:, :], slot[:, k, m * P:(m + 1) * P], yT[:, kh * KD + k, :],
                                       start=(kh == 0 and k == 0), stop=(kh == 1 and k == KD - 1))
                        if kh == 1:
                            ins.then_inc(is_full(keys[m])[0], 1)
                        elif m == 3:
                            ins.then_inc(S_("pc_half"), 1)
                    strip_used(keys[3] if kh else ("sem", "pc_half", j + 1))
            phase_end(pe, 2)

            slot = full_strip(pe, w_in, Q0)
            for m in range(4):
                project_T(slot, m, hT, ("q", m))
            strip_used(("q", 3))
            slot = full_strip(pe, w_in, K0)
            for m in range(4):
                project_T(slot, m, hT, ("k", m), nctx=True)
            strip_used(("k", 3))
            slot = full_strip(pe, w_in, V0)
            for t in range(TT):
                project_tok(slot, 512, hT, t, ("v", 0, t))
            strip_used(("v", 0, TT - 1))
            for d in range(2):
                key = ("lr", d)
                ps = open_(pe, key, 2)
                for c0, c1, o in ((C, NT, 0), (0, C, T)):
                    for k in range(KD):
                        ins = mmul(ps[0:GR, o:o + c1 - c0], wsmall[:, k, d * GR:(d + 1) * GR], hT[:, k, c0:c1],
                                   start=(k == 0), stop=(k == KD - 1))
                ins.then_inc(is_full(key)[0], 1)
            pe.wait_ge(S_("aw_in"), 16)
            side_done = [0]
            side_slot = [None]

            def side_part(n):
                for q in range(side_done[0], side_done[0] + n):
                    i, k = q // KD, q % KD
                    key = side[i]
                    if k == 0:
                        if i == 0:
                            side_slot[0] = full_strip(pe, w_in, V0 + 512)
                        elif i in (TT, TT + 4):
                            side_slot[0] = full_strip(pe, w_in, GA0 + (i - TT) // 4 * 512)
                        open_(pe, key, 1, 2, 4)
                    slot = side_slot[0]
                    if key[0] == "v":
                        ins = mmul(bank(key)[:, :], hT[:, k, key[2] * P:(key[2] + 1) * P], slot[:, k, :],
                                   start=(k == 0), stop=(k == KD - 1))
                    else:
                        ins = mmul(bank(key)[:, :], slot[:, k, key[1] % 4 * P:(key[1] % 4 + 1) * P], hT[:, k, C:NT],
                                   start=(k == 0), stop=(k == KD - 1))
                    if k == KD - 1:
                        ins.then_inc(is_full(key)[0], 1)
                        if i in (TT - 1, TT + 3, TT + 7):
                            strip_used(key)
                side_done[0] += n

            for h in range(GH):
                for d in range(2):
                    n = h * 2 + d
                    if n == 0:
                        gla_z(pe, h, d)
                    pe.wait_ge(*is_free(("lr", 1)))
                    order = [0, 1, 2, 3, 4, 5] if d == 0 else [1, 0, 5, 4, 3, 2]
                    side_part(SIDE_AHEAD)
                    pe.wait_ge(S_("qk_ready"), n + 1)
                    key = ("sc", n)
                    ps = open_(pe, key, 1, 4, 8)
                    for c in range(TL):
                        ins = mmul(ps[:, c * P:(c + 1) * P], ek[:, TC + c, :], eq[:, c, :], start=True, stop=True)
                    ins.then_inc(is_full(key)[0], 1)
                    for half in range(2):
                        key = ("ekT", n, half)
                        ps = open_(pe, key, 1, 4, 8)
                        for t in range(3):
                            ins = nc.tensor.transpose(ps[:, t * P:(t + 1) * P], ek[:, half * 3 + t, :], ident)
                        ins.then_inc(is_full(key)[0], 1)
                    if n + 1 < 8:
                        gla_z(pe, (n + 1) // 2, (n + 1) % 2)
                    pe.wait_ge(*is_free(("v", h // 2, TT - 1)))
                    for i, t in enumerate(order):
                        if i < 5:
                            pe.wait_ge(*is_free(("ekT", n, t // 3)))
                            key = ("gkv", n, i)
                            ps = open_(pe, key, 1, 4, 8)
                            ins = mmul(ps[:, 0:GDV], ekT[:, t, :], vtok[:, t, h * GDV:(h + 1) * GDV],
                                       start=True, stop=True)
                            ins.then_inc(is_full(key)[0], 1)
                        if i >= 2:
                            pe.wait_ge(*is_free(("sc", n)))
                            key = ("o", n, i)
                            ps = open_(pe, key, 1, 4, 8)
                            mmul(ps[:, 0:GDV], sc[:, t - TC, :], vtok[:, t, h * GDV:(h + 1) * GDV],
                                 start=True, stop=False)
                            pe.wait_ge(S_("st_ready"), n * 4 + i - 1)
                            ins = mmul(ps[:, 0:GDV], eq[:, t - TC, :], st[(i - 1) % 2][:, :], start=False, stop=True)
                            ins.then_inc(is_full(key)[0], 1)
                        side_part(1)
            for j in range(2):
                slot = full_strip(pe, w_in, R0 + j * 512)
                for t in range(TL):
                    project_tok(slot, 512, hT, TC + t, ("r", j, t))
                strip_used(("r", j, TL - 1))
            pe.wait_ge(S_("o_gated"), 2 * TL)
            for m in range(KD):
                key = ("oT", m)
                ps = open_(pe, key)
                for c in range(TL):
                    ins = nc.tensor.transpose(ps[:, c * P:(c + 1) * P], otok[:, c, m * P:(m + 1) * P], ident)
                ins.then_inc(is_full(key)[0], 1)

            def branch(w, src, name, ada=(None, None)):
                for j in range(2):
                    slot = full_strip(pe, w, j * 512)
                    for m in range(4):
                        key = (name, j * 4 + m)
                        ps = open_(pe, key)
                        for k in range(KD):
                            ins = mmul(ps[:, :], slot[:, k, m * P:(m + 1) * P], src[:, k, :],
                                       start=(k == 0), stop=(k == KD - 1))
                        ins.then_inc(is_full(key)[0], 1)
                    strip_used((name, j * 4 + 3))
                    if ada[j]:
                        ada_strip(ada[j])

            for m in range(KD):
                pe.wait_ge(*is_free(("oT", m)))
            branch(a["gla_proj"][0], oT, "pa")
            phase_end(pe, 3)

            for j in range(2):
                slot = full_strip(pe, w_in, U0 + j * 512)
                for m in range(4):
                    project_T(slot, m, hT, ("u", j * 4 + m))
                strip_used(("u", j * 4 + 3))
            for s in range(4, 7):
                ada_strip(s)
            pe.wait_ge(S_("fconst_in"), 16 * 3)
            pe.wait_ge(S_("u_folded"), 1)
            for r in range(TL):
                src, f = (ue, fC) if r < 2 else (uo, fS)
                key = ("A", r)
                ps = open_(pe, key, 2)
                for g in range(4):
                    o = ps[:, g * FG:(g + 1) * FG]
                    for k in range(2):
                        ins = mmul(o, src[:, 2 * g + k, (r % 2) * P:(r % 2 + 1) * P], f[:, k, :],
                                   start=(k == 0), stop=(k == 1))
                        if r == 2 and k == 0:
                            for q in range(2):
                                mmul(ps[0:1, g * FG:(g + 1) * FG], uT[:, 2 * g + q, T // 2:T // 2 + 1], fC[:, q, :],
                                     start=False, stop=False, skip_group_check=True)
                ins.then_inc(is_full(key)[0], 1)
            for r in range(TL):
                pe.wait_ge(*is_free(("A", r)))
            for m in range(KD):
                key = ("fy", m)
                ps = open_(pe, key)
                for r in range(TL):
                    ins = mmul(ps[:, :], At[:, r, m * P:(m + 1) * P], fT[:, r, :], start=(r == 0), stop=(r == TL - 1))
                ins.then_inc(is_full(key)[0], 1)
            gate_T(GB0, "gb", (7, 8))
            for s in (9, 10):
                ada_strip(s)
            for m in range(KD):
                pe.wait_ge(*is_free(("fy", m)))
            branch(a["fnet_proj"][0], fyT, "pb", (11, None))
            key = ("mod2",)
            pe.wait_ge(S_("ada_summed"), 8)
            ps = open_(pe, key)
            for m in range(32):
                ins = mmul(ps[:, m:m + 1], ada_acc[:, m // 4, m % 4 * P:(m % 4 + 1) * P], ones[:, 0:1],
                           start=True, stop=True)
            ins.then_inc(is_full(key)[0], 1)
            phase_end(pe, 4)

            for c, name in ((2, "g1"), (5, "g2")):
                for j in range(2):
                    key = (name, j)
                    ps = open_(pe, key)
                    for m in range(4):
                        ins = mmul(ps[:, m * P:(m + 1) * P],
                                   mod[:, c * KD + j * 4 + m, 0:1].to_broadcast([P, P]), ident, start=True, stop=True)
                    ins.then_inc(is_full(key)[0], 1)
            for j in range(2):
                slot = full_strip(pe, a["w_out"][0], j * 512)
                for t in range(TL):
                    project_tok(slot, 512, mT, t, ("wo", j, t))
                strip_used(("wo", j, TL - 1))
            for k in range(KD):
                pe.wait_ge(S_("x1_normed"), TL)
                key = ("h2T", k)
                ps = open_(pe, key)
                for t in range(TL):
                    ins = nc.tensor.transpose(ps[:, t * P:(t + 1) * P], yo[:, t, k * P:(k + 1) * P], ident)
                ins.then_inc(is_full(key)[0], 1)
            for k in range(KD):
                pe.wait_ge(*is_free(("h2T", k)))
            key = ("route",)
            pe.wait_ge(S_("rw_in"), 16)
            ps = open_(pe, key)
            for t in range(TL):
                for k in range(KD):
                    ins = mmul(ps[:, t * NE:(t + 1) * NE], h2T[:, k, t * P:(t + 1) * P], rw[:, k, :],
                               start=(k == 0), stop=(k == KD - 1))
            ins.then_inc(is_full(key)[0], 1)

            pe.wait_ge(S_("picked"), 1)
            ps = open_(pe, ("rank",))
            for t in range(TL):
                for b in range(t):
                    mmul(ps[:, t * NE:(t + 1) * NE], ones, slot_of[:, b, :], start=(b == 0), stop=False)
                mmul(ps[:, t * NE:(t + 1) * NE], mask[0], slot_of[:, t, :], start=(t == 0), stop=True)
            for t in range(TL):
                ins = mmul(ps[:, TL * NE:(TL + 1) * NE], ones, slot_of[:, t, :], start=(t == 0), stop=(t == TL - 1))
            ins.then_inc(is_full(("rank",))[0], 1)

            R = ROWS_A_TILE
            psG = open_(pe, ("G",), 1, 0, 1)
            psU = open_(pe, ("U",), 1, 1, 2)
            psX = open_(pe, ("X",), 2, 2, 4)
            psD = open_(pe, ("D",), 2, 4, 6)
            psY = open_(pe, ("Y",), 2, 6, 8)

            def turn_x():
                for k in range(KD):
                    ins = nc.tensor.transpose(psX[:, k * R:(k + 1) * R], xrow[0:R, k * P:(k + 1) * P],
                                              ident[0:R, 0:R])
                ins.then_inc(S_("x_turned"), 1)

            def turn_y():
                for k in range(KD):
                    ins = nc.tensor.transpose(psY[0:R, k * P:(k + 1) * P], YT[:, k, :], ident)
                ins.then_inc(S_("y_turned"), 1)

            pe.wait_ge(S_("xrow_in"), 16)
            turn_x()
            pe.wait_ge(S_("tiles_known"), 1)
            with pe.Fori(0, NE // 2) as pair:
                for par in range(2):
                    w1, w3, w2 = (w.rearrange("p (k n) -> p k n", k=k) for w, k in zip(wmem[par], (KD, KD, FF // P)))
                    e = pair * 2 + par
                    lo = pe.value_load(first_tile_i[0:1, bass.ds(e, 1)], min_val=0, max_val=XTILES)
                    hi = pe.value_load(first_tile_i[0:1, bass.ds(e + 1, 1)], min_val=0, max_val=XTILES)
                    pe.wait_ge(S_("w_in%d" % par), pair * 48 + 48)
                    pe.sem_inc(S_("pe_passed"), 1)
                    with pe.Fori(lo, hi) as j:
                        pe.wait_ge(S_("x_ready"), j + 1)
                        for m in range(FF // P):
                            for w, ps in ((w1, psG), (w3, psU)):
                                for k in range(KD):
                                    ins = mmul(ps[:, m * R:(m + 1) * R], w[:, k, m * P:(m + 1) * P], XT[:, k, :],
                                               start=(k == 0), stop=(k == KD - 1))
                        ins.then_inc(S_("up_full"), 1)
                        pe.wait_ge(S_("xrow_in"), j * 16 + 32)
                        pe.sem_inc(S_("pe_passed"), 1)
                        turn_x()
                        pe.wait_ge(S_("yT_ready"), j + 1)
                        pe.wait_ge(S_("y_ready"), j + 1)
                        pe.sem_inc(S_("pe_passed"), 1)
                        turn_y()
                        pe.wait_ge(S_("he_ready"), j + 1)
                        for m in range(KD):
                            for k in range(FF // P):
                                ins = mmul(psD[:, m * R:(m + 1) * R], w2[:, k, m * P:(m + 1) * P], heT[:, k, :],
                                           start=(k == 0), stop=(k == FF // P - 1))
                        ins.then_inc(S_("down_full"), 1)
            n = pe.value_load(first_tile_i[0:1, NE:NE + 1], min_val=1, max_val=XTILES)
            pe.wait_ge(S_("yT_ready"), n + 1)
            pe.wait_ge(S_("y_ready"), n + 1)
            pe.sem_inc(S_("pe_passed"), 1)
            turn_y()

        @block.sync
        def _(sp):
            sp.dma_start(col, a["cols"]).then_inc(S_("cols_in"), 16)
            for n, (pieces, _) in enumerate(strips):
                if n >= NS:
                    key = strips[n - NS][1]
                    if key[0] == "sem":
                        sp.wait_ge(S_(key[1]), key[2])
                    else:
                        sp.wait_ge(*is_full(key))
                for dst, src in pieces:
                    sp.dma_start(dst(ring[n % NS]), src).then_inc(strip_in[n % NS], 16)
                if n == 0:
                    sp.dma_start(row, a["rows"]).then_inc(S_("rows_in"), 16)
            sp.wait_ge(S_("phase_done"), ENG * 4)

            def weights(e, par, names, slots):
                for name, i in zip(names, slots):
                    src = a[name][0, e] if isinstance(e, int) else a[name][0, bass.ds(e, 1), :, :].rearrange("o r n -> (o r) n")
                    k = FF // P if name == "exp_w2" else KD
                    sp.dma_start(wmem[par][i].rearrange("p (k n) -> p k n", k=k),
                                 src.rearrange("(k p) n -> p k n", p=P)).then_inc(S_("w_in%d" % par), 16)

            weights(0, 0, ("exp_w1", "exp_w3", "exp_w2"), (0, 1, 2))
            for n in range(len(strips) - NS, len(strips)):
                sp.wait_ge(*is_full(strips[n][1]))
            weights(1, 1, ("exp_w1", "exp_w3", "exp_w2"), (0, 1, 2))
            sp.wait_ge(S_("tiles_known"), 1)
            with sp.Fori(1, NE // 2) as pair:
                for par in range(2):
                    e = pair * 2 + par
                    used = sp.value_load(first_tile_i[0:1, bass.ds(e - 1, 1)], min_val=1, max_val=XTILES)
                    sp.wait_ge(S_("up_full"), used)
                    weights(e, par, ("exp_w1", "exp_w3"), (0, 1))
                    sp.wait_ge(S_("down_full"), used)
                    weights(e, par, ("exp_w2",), (2,))
            sp.wait_ge(S_("out_ready"), TL)
            sp.dma_start(out[0].rearrange("(t p) d -> p t d", p=P), yo).then_inc(S_("out_sent"), 16)
            sp.wait_ge(S_("out_sent"), 16)

        @block.scalar
        def _(act):
            run = nc.scalar.activation
            n_ = [0]

            def step(ins):
                n_[0] += 1
                ins.then_inc(S_("act_step"), 1)
                act.wait_ge(S_("act_step"), n_[0])

            act.dma_start(xs[:, 0:TC, :], a["ctx"][0].rearrange("(t p) d -> p t d", p=P)).then_inc(S_("ctx_in"), 16)
            for t in range(TL):
                act.dma_start(xs[:, TC + t, :], a["x"][0, t * P:(t + 1) * P, :]).then_inc(S_("x_in%d" % t), 16)
                act.dma_start(pos[:, t, :], a["pos"][t * P:(t + 1) * P, :]).then_inc(S_("x_in%d" % t), 16)
            act.dma_start(sq, a["squares"]).then_inc(S_("consts_in"), 16)
            act.dma_start(self_[0:3 * SH, :], a["sel"]).then_inc(S_("consts_in"), 16)
            for d0, c0, n in ((0, LR0, 2 * GR), (2 * GR, DT0, 2 * SH)):
                act.dma_start(wsmall[:, :, d0:d0 + n], w_cols(w_in, c0, n),
                              allow_slow_non_contiguous=True).then_inc(S_("small_in"), 32)

            act.wait_ge(S_("cols_in"), 16)
            run(c_("c"), c_("c"), ACT.Silu).then_inc(S_("c_act"), 1)
            for t in range(TT):
                act.wait_ge(S_("x_pos"), t + 1)
                if t:
                    act.wait_ge(S_("x_ss"), t)
                ins = run(junk, xs[:, t, :], ACT.Square, accum_out=small[:, t:t + 1])
                ins.then_inc(S_("x_ss"), 1)
            act.wait_ge(S_("x_var"), 1)
            run(small[:, 16:16 + TT], small[:, 8:8 + TT], ACT.Sqrt).then_inc(S_("x_std"), 1)
            for s in range(4):
                key = ("modrow", s)
                act.wait_ge(*is_full(key))
                run(modrow[0:2, s * 512:(s + 1) * 512], bank(key)[0:2, :], ACT.Copy).then_inc(is_free(key)[0], 1)
            act.wait_ge(S_("modA1"), 1)
            for k in range(KD):
                for key, j, lo, n in ((("hT", k), 0, C, T), (("hTc", k), 1, 0, C)):
                    act.wait_ge(*is_full(key))
                    ps = bank(key)
                    run(hT[:, k, lo:lo + n], ps[:, 0:n], ACT.Identity, scale=modA[:, j, k:k + 1],
                             bias=mod[:, k, j:j + 1]).then_inc(is_free(key)[0], 1)
            phase_end(act, 1)

            run(nega, r_("a_log"), ACT.Exp).then_inc(S_("nega"), 1)
            act.wait_ge(S_("dt_negabs"), 1)
            run(tmpd[1], tmpd[1], ACT.Exp).then_inc(S_("dt_exp"), 1)
            act.wait_ge(S_("dt_w"), 1)
            run(wend, dt, ACT.Ln).then_inc(S_("dt_ln"), 1)
            act.wait_ge(S_("acs_out"), 1)
            run(wend, wend, ACT.Exp).then_inc(S_("acs_exps"), 1)
            run(eend, tmpd[1], ACT.Exp).then_inc(S_("acs_exps"), 1)
            run(eacs, acs, ACT.Exp).then_inc(S_("acs_exps"), 1)
            for d in range(2):
                act.wait_ge(*is_full(("acsT", d)))
                ps = bank(("acsT", d))
                ps = ps.bitcast(BF16)
                run(rowsT[0:3 * SH, d, :], ps[0:3 * SH, 0:T], ACT.Copy).then_inc(is_free(("acsT", d))[0], 1)
            act.wait_ge(S_("raw_zero"), 1)

            def yT_evac(g):
                if g == 0:
                    act.wait_ge(S_("x_zeroed"), 16)
                for m in range(4):
                    key = ("yT", g, m)
                    act.wait_ge(*is_full(key))
                    blk = g * 4 + m
                    run(yT[:, blk, :], bank(key)[:, :], ACT.Identity, scale=c_("ssd_norm")[:, blk:blk + 1],
                        bias=0.0).then_inc(is_free(key)[0], 1)

            for g in range(SG):
                def raw_evac(key, rn):
                    if rn >= 2:
                        act.wait_ge(S_("conv_done"), rn - 1)
                    act.wait_ge(*is_full(key))
                    ps = bank(key)
                    dst = raw[rn % 2]
                    if key[0] != "C":
                        step(run(dst[:, 2:2 + C], ps[:, T:T + C], ACT.Copy))
                    run(dst[:, LAT:LAT + T], ps[:, 0:T], ACT.Copy).then_inc(is_free(key)[0], 1)

                def silu_conv(kind, m, rn):
                    act.wait_ge(S_("conv_done"), rn + 1)
                    if kind == "x":
                        blk = g * 4 + m
                        bias = c_("conv_b")[:, blk:blk + 1]
                        prev = ("xtok", g, m - 1, 1) if m else (("xtok", g - 1, 3, 1) if g else None)
                        if prev:
                            act.wait_ge(*is_full(prev))
                        run(xcT[:, 0:C], cacc[:, 0:C], ACT.Silu, bias=bias)
                        run(xcT[:, C:NT], cacc[:, C + 4:C + 4 + T], ACT.Silu, bias=bias).then_inc(S_("xc_ready"), 1)
                    elif kind == "B":
                        bias = c_("conv_b")[:, 16 + g:17 + g]
                        if g:
                            act.wait_ge(*is_full(("CB", g - 1)))
                        run(BT[:, 0:C], cacc[:, 0:C], ACT.Silu, bias=bias)
                        run(BT[:, C:NT], cacc[:, C + 4:C + 4 + T], ACT.Silu, bias=bias).then_inc(S_("BT_ready"), 1)
                    else:
                        if g:
                            act.wait_ge(*is_full(("off", g - 1, 1, 5)))
                        run(CT, cacc[:, C + 4:C + 4 + T], ACT.Silu, bias=c_("conv_b")[:, 20 + g:21 + g]).then_inc(S_("CT_ready"), 1)

                def xtok_evac(m):
                    if g:
                        act.wait_ge(S_("xw_ready"), g * 10)
                        act.wait_ge(S_("xdt_ready"), g * 2)
                    for half in range(2):
                        key = ("xtok", g, m, half)
                        act.wait_ge(*is_full(key))
                        ps = bank(key)
                        run(xtok[:, half * 3:half * 3 + 3, m * P:(m + 1) * P],
                                 ps[:, 0:3 * P].rearrange("p (t n) -> p t n", t=3), ACT.Copy).then_inc(is_free(key)[0], 1)

                for m in range(4):
                    raw_evac(("x", g, m), g * 6 + m)
                    if m == 0 and g:
                        yT_evac(g - 1)
                    if m >= 1:
                        silu_conv("x", m - 1, g * 6 + m - 1)
                    if m >= 2:
                        xtok_evac(m - 2)
                raw_evac(("B", g), g * 6 + 4)
                silu_conv("x", 3, g * 6 + 3)
                raw_evac(("C", g), g * 6 + 5)
                silu_conv("B", 0, g * 6 + 4)
                xtok_evac(2)
                xtok_evac(3)
                silu_conv("C", 0, g * 6 + 5)
                for half in range(2):
                    key = ("Btok", g, half)
                    act.wait_ge(*is_full(key))
                    ps = bank(key)
                    if g:
                        act.wait_ge(*is_full(("kv", g - 1, 1, 4)))
                    run(Btok[:, half * 3:half * 3 + 3, :], ps[:, 0:3 * P].rearrange("p (t n) -> p t n", t=3),
                             ACT.Copy).then_inc(is_free(key)[0], 1)
                for d in range(2):
                    for t in (2 * d, 2 * d + 1):
                        key = ("z", g, t)
                        act.wait_ge(*is_full(key))
                        if g:
                            act.wait_ge(S_("yz_squared"), g * 4)
                        run(sz[:, t, :], bank(key)[:, :], ACT.Silu).then_inc(is_free(key)[0], 1)
                    for h in range(HPG):
                        n = (g * 2 + d) * HPG + h
                        act.wait_ge(*is_free(("R", g, d, h)))
                        run(mm[n % NM], mm[n % NM], ACT.Exp).then_inc(S_("decay_ready"), 1)
                for t in range(TL):
                    act.wait_ge(S_("yz_ready"), g * 4 + t + 1)
                    run(sz[:, t, :], yacc[:, t, :], ACT.Square, accum_out=ssq[:, t, g:g + 1]).then_inc(S_("yz_squared"), 1)
            yT_evac(SG - 1)
            act.wait_ge(S_("ssd_var"), 1)
            run(small[:, 16:16 + TL], small[:, 8:8 + TL], ACT.Sqrt).then_inc(S_("ssd_std"), 1)
            act.wait_ge(*is_full(("rrow",)))
            ps = bank(("rrow",))
            run(rrow, ps[:, :], ACT.Copy).then_inc(is_free(("rrow",))[0], 1)

            def gates(name):
                for m in range(KD):
                    act.wait_ge(*is_full((name, m)))
                    ps = bank((name, m))
                    run(gateT[:, m, :], ps[:, :], ACT.Sigmoid).then_inc(is_free((name, m))[0], 1)

            gates("gc")
            phase_end(act, 2)

            act.dma_start(aw[0:GR, :, :], a["gla_a_w"][0].rearrange("d r n -> r d n")).then_inc(S_("aw_in"), 16)
            for m in range(4):
                act.wait_ge(*is_full(("q", m)))
                ps = bank(("q", m))
                run(qT[:, m, :], ps[:, :], ACT.Copy).then_inc(is_free(("q", m))[0], 1)
            for m in range(4):
                act.wait_ge(*is_full(("k", m)))
                ps = bank(("k", m))
                run(kT[:, m, 0:C], ps[:, T:NT], ACT.Copy)
                run(kT[:, m, C:NT], ps[:, 0:T], ACT.Copy).then_inc(is_free(("k", m))[0], 1)

            def side_evac(key):
                act.wait_ge(*is_full(key))
                dst = vtok[:, key[2], key[1] * 512:(key[1] + 1) * 512] if key[0] == "v" else gateT[:, key[1], :]
                run(dst, bank(key)[:, :], ACT.Copy).then_inc(is_free(key)[0], 1)

            for t in range(TT):
                side_evac(("v", 0, t))
            for d in range(2):
                act.wait_ge(*is_full(("lr", d)))
                ps = bank(("lr", d))
                run(lr2[0:GR, d, 0:C], ps[0:GR, T:NT], ACT.Copy)
                run(lr2[0:GR, d, C:NT], ps[0:GR, 0:T], ACT.Copy).then_inc(is_free(("lr", d))[0], 1)
            for n in range(8):
                act.wait_ge(S_("gz_negabs"), n + 1)
                run(eb, eb, ACT.Exp).then_inc(S_("gz_exp"), 1)
                act.wait_ge(S_("gz_w"), n + 1)
                run(wb, wb, ACT.Ln).then_inc(S_("gz_ln"), 1)
                act.wait_ge(S_("decay_refd"), n + 1)
                sgn = 1.0 if n % 2 == 0 else -1.0
                if n:
                    act.wait_ge(*is_full(("o", n - 1, 5)))
                run(eq, dd[:, TC:TT, :], ACT.Exp, scale=sgn / TAU)
                run(ek, dd, ACT.Exp, scale=-sgn / TAU)
                run(ea, pc[:, :, P // 2], ACT.Exp, scale=1.0 / TAU)
                run(ebb, dref, ACT.Exp, scale=1.0 / TAU).then_inc(S_("gla_exps"), 1)
                for half in range(2):
                    key = ("ekT", n, half)
                    act.wait_ge(*is_full(key))
                    ps = bank(key)
                    run(ekT[:, half * 3:half * 3 + 3, :], ps[:, 0:3 * P].rearrange("p (t n) -> p t n", t=3),
                             ACT.Copy).then_inc(is_free(key)[0], 1)
                a_n = (SIDE_AHEAD + TT)
                for i in range(n * a_n // KD, (n + 1) * a_n // KD):
                    side_evac(side[i])
            for m in range(KD):
                act.wait_ge(*is_free(("ga", m)))
                run(gateT[:, m, :], gateT[:, m, :], ACT.Sigmoid).then_inc(S_("ga_ready"), 1)
            act.wait_ge(S_("o_all"), 1)
            for c in range(TL):
                for h in range(GH):
                    if h or c:
                        step(ins)
                    ins = run(zb[:, 0:GDV], otok[:, c, h * GDV:(h + 1) * GDV], ACT.Square,
                              accum_out=gss[:, c, h:h + 1])
            ins.then_inc(S_("o_squared"), 1)
            act.wait_ge(S_("o_var"), 1)
            run(gss, gss, ACT.Sqrt).then_inc(S_("o_std"), 1)
            rbuf = [eb, wb]
            for j in range(2):
                for t in range(TL):
                    i = j * TL + t
                    act.wait_ge(*is_full(("r", j, t)))
                    ps = bank(("r", j, t))
                    if i >= 2:
                        act.wait_ge(S_("o_gated"), i - 1)
                    run(rbuf[i % 2][:, 0:512], ps[:, :], ACT.Silu).then_inc(is_free(("r", j, t))[0], 1)
            for m in range(KD):
                act.wait_ge(*is_full(("oT", m)))
                ps = bank(("oT", m))
                run(oT[:, m, :], ps[:, :], ACT.Identity, scale=c_("gla_norm")[:, m % 2:m % 2 + 1], bias=0.0).then_inc(is_free(("oT", m))[0], 1)
            phase_end(act, 3)

            act.dma_start(fT, a["dft_time"].rearrange("(r p) k -> p r k", p=P)).then_inc(S_("fconst_in"), 16)
            act.dma_start(fC, a["dft_cos"].rearrange("(r p) k -> p r k", p=P)).then_inc(S_("fconst_in"), 16)
            act.dma_start(fS, a["dft_sin"].rearrange("(r p) k -> p r k", p=P)).then_inc(S_("fconst_in"), 16)
            for m in range(KD):
                act.wait_ge(*is_full(("u", m)))
                ps = bank(("u", m))
                run(uT[:, m, :], ps[:, :], ACT.Copy).then_inc(is_free(("u", m))[0], 1)
            for r in range(TL):
                act.wait_ge(*is_full(("A", r)))
                ps = bank(("A", r))
                run(At[:, r, :], ps[:, :], ACT.Copy).then_inc(is_free(("A", r))[0], 1)
            for m in range(KD):
                act.wait_ge(*is_full(("fy", m)))
                ps = bank(("fy", m))
                run(fyT[:, m, :], ps[:, :], ACT.Copy).then_inc(is_free(("fy", m))[0], 1)
            gates("gb")
            phase_end(act, 4)

            act.dma_start(xr, a["x"][0].rearrange("(t p) d -> p t d", p=P)).then_inc(S_("xr_in"), 16)
            act.dma_start(pos2, a["pos"].rearrange("(t p) d -> p t d", p=P)).then_inc(S_("xr_in"), 16)
            act.dma_start(rw, a["router_w"].rearrange("(k p) e -> p k e", p=P)).then_inc(S_("rw_in"), 16)
            act.dma_start(frow, a["final_row"]).then_inc(S_("frow_in"), 16)
            for name, dst in (("g1", g1row), ("g2", g2row)):
                for j in range(2):
                    act.wait_ge(*is_full((name, j)))
                    ps = bank((name, j))
                    run(dst[:, j * 512:(j + 1) * 512], ps[:, :], ACT.Copy).then_inc(is_free((name, j))[0], 1)
            for t in range(TL):
                act.wait_ge(S_("x1_ready"), TL + t + 1)
                if t:
                    act.wait_ge(S_("x1_ss"), t)
                ins = run(junk2, xr[:, t, :], ACT.Square, accum_out=small[:, t:t + 1])
                ins.then_inc(S_("x1_ss"), 1)
            act.wait_ge(S_("x1_var"), 1)
            run(small[:, 16:16 + TL], small[:, 8:8 + TL], ACT.Sqrt).then_inc(S_("x1_std"), 1)
            for k in range(KD):
                act.wait_ge(*is_full(("h2T", k)))
                ps = bank(("h2T", k))
                run(h2T[:, k, :], ps[:, :], ACT.Identity, scale=modA[:, 2, k:k + 1],
                         bias=mod[:, 3 * KD + k, 0:1]).then_inc(is_free(("h2T", k))[0], 1)
            act.wait_ge(*is_full(("route",)))
            ps = bank(("route",))
            run(score, ps[:, 0:TL * NE].rearrange("p (t e) -> p t e", t=TL), ACT.Sigmoid).then_inc(is_free(("route",))[0], 1)
            R = ROWS_A_TILE
            psG, psD = bank(("G",)), bank(("D",))
            act.wait_ge(S_("yT_zero"), 1)
            run(YT, YT, ACT.Copy).then_inc(S_("yT_ready"), 1)
            act.wait_ge(S_("tiles_known"), 1)
            n = act.value_load(first_tile_i[0:1, NE:NE + 1], min_val=1, max_val=XTILES)
            with act.Fori(0, n) as j:
                act.wait_ge(S_("up_full"), j + 1)
                run(sg, psG[:, :].rearrange("p (m r) -> p m r", r=R), ACT.Silu).then_inc(S_("g_ready"), 1)
                act.wait_ge(S_("down_full"), j + 1)
                run(YT, psD[:, :].rearrange("p (m r) -> p m r", r=R), ACT.Copy).then_inc(S_("yT_ready"), 1)
            for t in range(TL):
                act.wait_ge(S_("x2_ready"), t + 1)
                if t:
                    act.wait_ge(S_("x2_ss"), t)
                run(junk2, xr[:, t, :], ACT.Square, accum_out=small[:, 32 + t:33 + t]).then_inc(S_("x2_ss"), 1)
            act.wait_ge(S_("x2_var"), 1)
            run(small[:, 48:48 + TL], small[:, 40:40 + TL], ACT.Sqrt).then_inc(S_("x2_std"), 1)

        @block.vector
        def _(dve):
            v = nc.vector
            n_ = [0]

            def step(ins):
                n_[0] += 1
                ins.then_inc(S_("dve_step"), 1)
                dve.wait_ge(S_("dve_step"), n_[0])

            def ada_sum(s):
                slot, arrived, count = ada_at[s]
                dve.wait_ge(arrived, count)
                acc = ada_acc[:, s - 4, :]
                c = c_("c")
                step(v.tensor_scalar(acc, slot[:, 0, :], c[:, 0:1], None, ALU.mult))
                for k in range(1, KD):
                    ins = v.scalar_tensor_tensor(acc, slot[:, k, :], c[:, 2 * k:2 * k + 1], acc, ALU.mult, ALU.add)
                    if k < KD - 1:
                        step(ins)
                ins.then_inc(S_("ada_summed"), 1)

            def rstd(dst, ss, var, std, n, width, name_ss, cnt, name_var, name_std):
                dve.wait_ge(S_(name_ss), cnt)
                v.tensor_scalar(var, ss, 1.0 / width, EPS, ALU.mult, ALU.add).then_inc(S_(name_var), 1)
                dve.wait_ge(S_(name_std), 1)
                step(v.reciprocal(dst, std))

            for t in range(TT):
                if t < TC:
                    dve.wait_ge(S_("ctx_in"), 16)
                    v.tensor_scalar(xs[:, t, 0:2], xs[:, t, 0:2], 1.0, None, ALU.mult).then_inc(S_("x_pos"), 1)
                else:
                    dve.wait_ge(S_("x_in%d" % (t - TC)), 32)
                    v.tensor_tensor(xs[:, t, :], xs[:, t, :], pos[:, t - TC, :], ALU.add).then_inc(S_("x_pos"), 1)
            rstd(small[:, 24:24 + TT], small[:, 0:TT], small[:, 8:8 + TT], small[:, 16:16 + TT], TT, D,
                 "x_ss", TT, "x_var", "x_std")
            for t in range(TT):
                v.tensor_scalar(xs[:, t, :], xs[:, t, :], small[:, 24 + t:25 + t], None, ALU.mult).then_inc(S_("x_normed"), 1)
            key = ("mod",)
            dve.wait_ge(*is_full(key))
            v.tensor_tensor(mod[:, 0:16, :], bank(key)[:, 0:32].rearrange("p (m j) -> p m j", j=2),
                            c_("ada_b")[:, 0:16].unsqueeze(2).to_broadcast([P, 16, 2]), ALU.add)\
                .then_inc(is_free(key)[0], 1)
            dve.wait_ge(*is_free(key))
            for j in range(2):
                ins = v.scalar_tensor_tensor(modA[:, j, :], mod[:, KD:2 * KD, j], 1.0, c_("norm1"), ALU.add, ALU.mult)
                if j == 0:
                    step(ins)
            ins.then_inc(S_("modA1"), 1)
            phase_end(dve, 1)

            for i in range(2):
                ins = v.memset(raw[i], 0.0)
                if i == 0:
                    step(ins)
            ins.then_inc(S_("raw_zero"), 1)
            v.memset(zeros, 0.0).then_inc(S_("zeros_made"), 1)
            dve.wait_ge(S_("rows_in"), 16)
            dve.wait_ge(*is_full(("dt",)))
            ps = bank(("dt",))
            x_, e_ = tmpd
            v.tensor_tensor(x_, ps[:, 0:TT * 64].rearrange("p (t h) -> p t h", t=TT),
                                 r_("dt_bias").unsqueeze(1).to_broadcast([P, TT, 64]), ALU.add).then_inc(is_free(("dt",))[0], 1)
            dve.wait_ge(*is_free(("dt",)))
            v.scalar_tensor_tensor(e_, x_, -1.0, x_, ALU.mult, ALU.min).then_inc(S_("dt_negabs"), 1)
            dve.wait_ge(S_("dt_exp"), 1)
            step(v.tensor_scalar(dt, e_, 1.0, None, ALU.add))
            v.scalar_tensor_tensor(eacs, dt, -1.0, e_, ALU.add, ALU.subtract).then_inc(S_("dt_w"), 1)
            dve.wait_ge(S_("dt_ln"), 1)
            step(v.tensor_tensor(wend, wend, eacs, ALU.subtract))
            step(v.scalar_tensor_tensor(dt, x_, 0.0, wend, ALU.max, ALU.add))
            dve.wait_ge(S_("nega"), 1)
            v.scalar_tensor_tensor(tmpd[0], dt, -1.0, nega.unsqueeze(1).to_broadcast([P, TT, 64]),
                                          ALU.mult, ALU.mult).then_inc(S_("dta"), 1)
            dve.wait_ge(*is_full(("acs",)))
            ps = bank(("acs",))
            for d in range(2):
                step(v.tensor_copy(acs[:, :, d * SH:(d + 1) * SH],
                                   ps[:, d * 192:(d + 1) * 192].rearrange("p (t h) -> p t h", t=TT)))
            v.tensor_copy(tmpd[1], ps[:, 512:512 + TT * 64].rearrange("p (t h) -> p t h", t=TT)).then_inc(is_free(("acs",))[0], 1)
            dve.wait_ge(*is_free(("acs",)))
            v.tensor_tensor(wend, tmpd[1], acs, ALU.subtract).then_inc(S_("acs_out"), 1)
            lat = acs[:, TC:TT, :].rearrange("p t (d h) -> p t d h", d=2)
            r4 = res.rearrange("p t (d h) -> p t d h", d=2)
            dve.wait_ge(S_("consts_in"), 16 * 2)
            step(v.tensor_copy(identb, ident))
            step(v.tensor_copy(selb[0:3 * SH, :], self_[0:3 * SH, :]))
            step(v.tensor_copy(acs3[:, :, :, 0, :], lat))
            step(v.tensor_tensor(r4, lat, acs3[:, :, :, 0, :], ALU.subtract))
            step(v.tensor_copy(acs3[:, :, :, 1, :], r4))
            step(v.tensor_tensor(r4, r4, acs3[:, :, :, 1, :], ALU.subtract))
            v.tensor_copy(acs3[:, :, :, 2, :], r4).then_inc(S_("acs_split"), 1)
            dve.wait_ge(S_("acs_exps"), 3)
            step(v.tensor_tensor(wend, wend, dt, ALU.mult))

            heads = lambda x: x.rearrange("p (h q) -> p h q", h=HPG)

            def conv(g, kind, m):
                rn = g * 6 + {"x": m, "B": 4, "C": 5}[kind]
                blk = {"x": g * 4 + m, "B": 16 + g, "C": 20 + g}[kind]
                key = ("x", g, m) if kind == "x" else (kind, g)
                dve.wait_ge(*is_free(key))
                if rn:
                    if kind == "x" and m:
                        dve.wait_ge(S_("xc_ready"), g * 4 + m)
                    elif kind == "x":
                        dve.wait_ge(S_("CT_ready"), g)
                    elif kind == "B":
                        dve.wait_ge(S_("xc_ready"), g * 4 + 4)
                    else:
                        dve.wait_ge(S_("BT_ready"), g + 1)
                lo, hi = (0, C + 4 + T) if kind != "C" else (C + 4, C + 4 + T)
                w = c_("conv_w")
                src = raw[rn % 2]
                step(v.tensor_scalar(cacc[:, lo:hi], src[:, lo:hi], w[:, blk * SK:blk * SK + 1], None, ALU.mult))
                for k in range(1, SK):
                    ins = v.scalar_tensor_tensor(cacc[:, lo:hi], src[:, lo + k:hi + k],
                                                 w[:, blk * SK + k:blk * SK + k + 1], cacc[:, lo:hi], ALU.mult, ALU.add)
                    if k < SK - 1:
                        step(ins)
                ins.then_inc(S_("conv_done"), 1)

            for g in range(SG):
                for m in range(4):
                    conv(g, "x", m)
                conv(g, "B", 0)
                conv(g, "C", 0)
                key = ("CB", g)
                dve.wait_ge(*is_full(key))
                ps = bank(key)
                for d in range(2):
                    ins = v.tensor_tensor(cb[d], ps[:, :].rearrange("p (c l) -> p c l", c=TL),
                                          mask[d].unsqueeze(1).to_broadcast([P, TL, P]), ALU.mult)
                    if d == 0:
                        step(ins)
                ins.then_inc(is_free(key)[0], 1)
                dve.wait_ge(*is_free(key))
                for m in range(4):
                    dve.wait_ge(*is_free(("xtok", g, m, 1)))
                if g:
                    dve.wait_ge(*is_full(("yT", g - 1, 3)))
                    dve.wait_ge(S_("yz_squared"), g * 4)
                dsk = r_("ssd_d")[:, g * HPG:(g + 1) * HPG].unsqueeze(2).to_broadcast([P, HPG, SHD])
                for c in range(TL):
                    step(v.tensor_tensor(heads(yacc[:, c, :]), heads(xtok[:, TC + c, :]), dsk, ALU.mult))
                for d in range(2):
                    order = [0, 1, 2, 3, 4, 5] if d == 0 else [1, 0, 5, 4, 3, 2]
                    hs = d * SH + g * HPG
                    per_head = lambda q, t, hs=hs: q[:, t, hs:hs + HPG].unsqueeze(2).to_broadcast([P, HPG, SHD])

                    def make_xw(i, d=d, order=order, per_head=per_head):
                        if i >= 2:
                            dve.wait_ge(*is_full(("kv", g, d, i - 2)))
                        elif g or d:
                            dve.wait_ge(*is_full(("kv", g if d else g - 1, 1 - d, 4)))
                        v.tensor_tensor(heads(xw[i % 2]), heads(xtok[:, order[i], :]), per_head(wend, order[i]),
                                        ALU.mult).then_inc(S_("xw_ready"), 1)

                    if d == 0:
                        make_xw(0)
                        make_xw(1)
                    for i in range(6):
                        if i >= 2:
                            key = ("off", g, d, i)
                            dve.wait_ge(*is_full(key))
                            ps = bank(key)
                            c = order[i] - TC
                            v.tensor_tensor(heads(vtmp), heads(ps[:, :]), per_head(eacs, order[i]), ALU.mult).then_inc(is_free(key)[0], 1)
                            dve.wait_ge(*is_free(key))
                            step(v.tensor_tensor(yacc[:, c, :], yacc[:, c, :], vtmp, ALU.add))
                        if i < 5:
                            key = ("kv", g, d, i)
                            dve.wait_ge(*is_full(key))
                            ps = bank(key)
                            if i == 0:
                                ins = v.tensor_copy(S[0], ps[:, :])
                            else:
                                step(v.tensor_tensor(heads(vtmp), heads(S[(i - 1) % 2]), per_head(eend, order[i]),
                                                     ALU.mult))
                                ins = v.tensor_tensor(S[i % 2], vtmp, ps[:, :], ALU.add)
                            ins.then_inc(is_free(key)[0], 1)
                            dve.wait_ge(*is_free(key))
                            if i + 2 < 5:
                                make_xw(i + 2)
                    if g or d:
                        dve.wait_ge(*is_full(("y", g if d else g - 1, 1 - d)))
                    for c in range(TL):
                        ins = v.tensor_tensor(heads(xdt[:, c, :]), heads(xtok[:, TC + c, :]), per_head(dt, TC + c),
                                              ALU.mult)
                    ins.then_inc(S_("xdt_ready"), 1)

                    def masked(h):
                        n = (g * 2 + d) * HPG + h
                        dve.wait_ge(S_("decay_ready"), n + 1)
                        v.tensor_tensor(mm[n % NM], mm[n % NM], cb[d], ALU.mult).then_inc(S_("M_ready"), 1)

                    for h in range(HPG):
                        n = (g * 2 + d) * HPG + h
                        key = ("R", g, d, h)
                        dve.wait_ge(*is_full(key))
                        ps = bank(key)
                        if n >= NM:
                            o = n - NM
                            if o % HPG == HPG - 1:
                                dve.wait_ge(*is_full(("y", o // HPG // 2, o // HPG % 2)))
                            else:
                                dve.wait_ge(S_("M_used"), o // HPG * (HPG - 1) + o % HPG + 1)
                        for c in range(TL):
                            ins = v.tensor_scalar(mm[n % NM][:, c, :], ps[:, c * P:(c + 1) * P],
                                                  acs[:, TC + c, hs + h:hs + h + 1], 0.0, ALU.subtract, ALU.min)
                        ins.then_inc(is_free(key)[0], 1)
                        if h >= 1:
                            masked(h - 1)
                    masked(HPG - 1)
                    if d == 0:
                        back = lambda q, t: q[:, t, SH + g * HPG:SH + (g + 1) * HPG].unsqueeze(2).to_broadcast([P, HPG, SHD])
                        make_xw(0, 1, [1, 0], back)
                        make_xw(1, 1, [1, 0], back)
                    key = ("y", g, d)
                    dve.wait_ge(*is_full(key))
                    ps = bank(key)
                    for c in range(TL):
                        ins = v.tensor_tensor(yacc[:, c, :], yacc[:, c, :], ps[:, c * 512:(c + 1) * 512], ALU.add)
                        if c < TL - 1:
                            step(ins)
                    ins.then_inc(is_free(key)[0], 1)
                    dve.wait_ge(*is_free(key))
                for t in range(TL):
                    dve.wait_ge(*is_free(("z", g, t)))
                    v.tensor_tensor(yacc[:, t, :], yacc[:, t, :], sz[:, t, :], ALU.mult).then_inc(S_("yz_ready"), 1)
            dve.wait_ge(S_("yz_squared"), SG * TL)
            step(v.tensor_reduce(small[:, 0:TL], ssq, AX.X, ALU.add))
            dve.wait_ge(S_("yz_squared"), SG * TL)
            v.tensor_scalar(small[:, 8:8 + TL], small[:, 0:TL], 1.0 / SI, EPS, ALU.mult, ALU.add).then_inc(S_("ssd_var"), 1)
            dve.wait_ge(S_("ssd_std"), 1)
            v.reciprocal(small[:, 0:TL], small[:, 16:16 + TL]).then_inc(S_("ssd_rstd"), 1)
            dve.wait_ge(*is_free(("rrow",)))
            for m in range(KD):
                dve.wait_ge(*is_free(("gc", m)))
                step(v.tensor_tensor(gateT[:, m, :], gateT[:, m, :], rrow, ALU.mult))
            for m in range(KD):
                key = ("pc", m)
                dve.wait_ge(*is_full(key))
                ps = bank(key)
                v.tensor_tensor(mT[:, m, :], ps[:, :], gateT[:, m, :], ALU.mult).then_inc(is_free(key)[0], 1)
            phase_end(dve, 2)

            step(v.memset(pc[:, :, 0:1], 0.0))
            for h in range(GH):
                for d in range(2):
                    n = h * 2 + d
                    order = [0, 1, 2, 3, 4, 5] if d == 0 else [1, 0, 5, 4, 3, 2]
                    key = ("gz", n)
                    dve.wait_ge(*is_full(key))
                    ps = bank(key)
                    v.tensor_scalar(zb, ps[:, 0:NT], c_("a_b")[:, d * GH + h:d * GH + h + 1], None, ALU.add).then_inc(is_free(key)[0], 1)
                    dve.wait_ge(*is_free(key))
                    v.scalar_tensor_tensor(eb, zb, -1.0, zb, ALU.mult, ALU.min).then_inc(S_("gz_negabs"), 1)
                    dve.wait_ge(S_("gz_exp"), n + 1)
                    step(v.tensor_scalar(wb, eb, 1.0, None, ALU.add))
                    v.scalar_tensor_tensor(lb, wb, -1.0, eb, ALU.add, ALU.subtract).then_inc(S_("gz_w"), 1)
                    dve.wait_ge(S_("gz_ln"), n + 1)
                    step(v.tensor_tensor(wb, wb, lb, ALU.subtract))
                    step(v.scalar_tensor_tensor(zb, zb, 0.0, wb, ALU.min, ALU.subtract))
                    for t in range(TT):
                        step(v.tensor_tensor_scan(pc[:, t, 1:P + 1], ones, zb[:, t * P:(t + 1) * P], 0.0,
                                                  ALU.mult, ALU.add))
                    ref = pc[:, :, P // 2:P // 2 + 1]
                    step(v.tensor_tensor(dd, pc[:, :, 1:P + 1] if d == 0 else pc[:, :, 0:P],
                                         ref.to_broadcast([P, TT, P]), ALU.subtract))
                    v.tensor_tensor(dref, pc[:, :, P], pc[:, :, P // 2], ALU.subtract).then_inc(S_("decay_refd"), 1)
                    dve.wait_ge(S_("gla_exps"), n + 1)
                    if n == 0:
                        for m in range(4):
                            dve.wait_ge(*is_free(("k", m)))
                    step(v.scalar_tensor_tensor(eq.rearrange("p c l -> p (c l)"), eq.rearrange("p c l -> p (c l)"),
                                                float(GDK) ** -0.5, qT[:, h, :], ALU.mult, ALU.mult))
                    v.tensor_tensor(ek.rearrange("p c l -> p (c l)"), ek.rearrange("p c l -> p (c l)"),
                                           kT[:, h, :], ALU.mult).then_inc(S_("qk_ready"), 1)
                    key = ("sc", n)
                    dve.wait_ge(*is_full(key))
                    ps = bank(key)
                    v.tensor_tensor(sc, ps[:, :].rearrange("p (c l) -> p c l", c=TL),
                                         mask[d].unsqueeze(1).to_broadcast([P, TL, P]), ALU.mult).then_inc(is_free(key)[0], 1)
                    start, end = (ea, ebb) if d == 0 else (ebb, ea)
                    for i, t in enumerate(order):
                        if i < 5:
                            key = ("gkv", n, i)
                            dve.wait_ge(*is_full(key))
                            ps = bank(key)
                            src = ps[:, 0:GDV]
                            if i:
                                v.tensor_tensor(sadd, src, st[(i - 1) % 2], ALU.add).then_inc(is_free(key)[0], 1)
                                dve.wait_ge(*is_free(key))
                                src = sadd
                            ins = v.tensor_scalar(st[i % 2], src, end[:, t:t + 1], start[:, order[i + 1]:order[i + 1] + 1],
                                                  ALU.mult, ALU.mult)
                            if i:
                                ins.then_inc(S_("st_ready"), 1)
                                dve.wait_ge(S_("st_ready"), n * 4 + i)
                            else:
                                ins.then_inc(is_free(key)[0], 1)
                                dve.wait_ge(*is_free(key))
                        if i >= 2:
                            key = ("o", n, i)
                            dve.wait_ge(*is_full(key))
                            ps = bank(key)
                            o = otok[:, t - TC, h * GDV:(h + 1) * GDV]
                            if d == 0:
                                v.tensor_copy(o, ps[:, 0:GDV]).then_inc(is_free(key)[0], 1)
                            else:
                                v.tensor_tensor(o, o, ps[:, 0:GDV], ALU.add).then_inc(is_free(key)[0], 1)
                            dve.wait_ge(*is_free(key))
            step(v.tensor_scalar(sadd, sadd, 1.0, None, ALU.mult))
            v.tensor_copy(dref, dref).then_inc(S_("o_all"), 1)
            dve.wait_ge(S_("o_squared"), 1)
            v.tensor_scalar(gss, gss, 1.0 / GDV, EPS, ALU.mult, ALU.add).then_inc(S_("o_var"), 1)
            dve.wait_ge(S_("o_std"), 1)
            step(v.reciprocal(gss, gss))
            for c in range(TL):
                o = otok[:, c, :].rearrange("p (h q) -> p h q", h=GH)
                step(v.tensor_tensor(o, o, gss[:, c, :].unsqueeze(2).to_broadcast([P, GH, GDV]), ALU.mult))
            rbuf = [eb, wb]
            for j in range(2):
                for t in range(TL):
                    i = j * TL + t
                    dve.wait_ge(*is_free(("r", j, t)))
                    o = otok[:, t, j * 512:(j + 1) * 512]
                    v.tensor_tensor(o, o, rbuf[i % 2][:, 0:512], ALU.mult).then_inc(S_("o_gated"), 1)

            def merge(gate_name, name, tmp):
                for m in range(KD):
                    if gate_name == "ga":
                        dve.wait_ge(S_("ga_ready"), m + 1)
                    else:
                        dve.wait_ge(*is_free((gate_name, m)))
                    key = (name, m)
                    dve.wait_ge(*is_full(key))
                    ps = bank(key)
                    v.tensor_tensor(tmp, ps[:, :], gateT[:, m, :], ALU.mult).then_inc(is_free(key)[0], 1)
                    dve.wait_ge(*is_free(key))
                    step(v.tensor_tensor(mT[:, m, :], mT[:, m, :], tmp, ALU.add))

            merge("ga", "pa", zb[:, 0:T])
            phase_end(dve, 3)

            for m in range(KD):
                dve.wait_ge(*is_free(("u", m)))
            H = T // 2
            v.tensor_tensor(ue[:, :, 1:H], uT[:, :, 1:H], uT[:, :, T - 1:H:-1], ALU.add)
            v.tensor_tensor(uo[:, :, 1:H], uT[:, :, 1:H], uT[:, :, T - 1:H:-1], ALU.subtract)
            v.tensor_copy(ue[:, :, 0:1], uT[:, :, 0:1])
            v.memset(uo[:, :, 0:1], 0.0).then_inc(S_("u_folded"), 1)
            for s in range(4, 12):
                ada_sum(s)
            merge("gb", "pb", At[:, 0, 0:T])
            key = ("mod2",)
            dve.wait_ge(*is_full(key))
            v.tensor_tensor(mod[:, 16:48, 0], bank(key)[:, 0:32], c_("ada_b")[:, 16:48], ALU.add)\
                .then_inc(is_free(key)[0], 1)
            dve.wait_ge(*is_free(key))
            step(v.scalar_tensor_tensor(modA[:, 2, :], mod[:, 4 * KD:5 * KD, 0], 1.0, c_("norm2"), ALU.add, ALU.mult))
            phase_end(dve, 4)

            dve.wait_ge(S_("xr_in"), 32)
            step(v.tensor_tensor(xr, xr, pos2, ALU.add))
            for j in range(2):
                dve.wait_ge(*is_free(("g1", j)))
                dve.wait_ge(*is_free(("g2", j)))
            for j in range(2):
                for t in range(TL):
                    key = ("wo", j, t)
                    dve.wait_ge(*is_full(key))
                    ps = bank(key)
                    sl = slice(j * 512, (j + 1) * 512)
                    v.tensor_tensor(yo[:, t, sl], ps[:, :], g1row[:, sl], ALU.mult).then_inc(is_free(key)[0], 1)
                    dve.wait_ge(*is_free(key))
                    v.tensor_tensor(xr[:, t, sl], xr[:, t, sl], yo[:, t, sl], ALU.add).then_inc(S_("x1_ready"), 1)
            rstd(small[:, 24:24 + TL], small[:, 0:TL], small[:, 8:8 + TL], small[:, 16:16 + TL], TL, D,
                 "x1_ss", TL, "x1_var", "x1_std")
            dve.wait_ge(S_("x1_ready"), 2 * TL)
            for t in range(TL):
                v.tensor_scalar(yo[:, t, :], xr[:, t, :], small[:, 24 + t:25 + t], None, ALU.mult).then_inc(S_("x1_normed"), 1)

            dve.wait_ge(*is_free(("route",)))
            step(v.tensor_tensor(sel, score, r_("router_b").unsqueeze(1).to_broadcast([P, TL, NE]), ALU.add))
            G = TL * NG
            q = sel.rearrange("p t (g e) -> p (t g) e", g=NG)
            f = lambda x, i: x.rearrange("p t (i g) -> p i (t g)", i=NG)[:, i, :]
            fl = lambda x, i: x.rearrange("p t e -> p (t e)")[:, i * G:(i + 1) * G]
            for i in range(2):
                step(v.tensor_tensor(fl(ra, i), q[:, :, 2 * i], q[:, :, 2 * i + 1], ALU.max))
                step(v.tensor_tensor(fl(ra, 2 + i), q[:, :, 2 * i], q[:, :, 2 * i + 1], ALU.min))
            step(v.tensor_tensor(fl(rb, 0), fl(ra, 0), fl(ra, 1), ALU.max))
            step(v.tensor_tensor(fl(rb, 1), fl(ra, 0), fl(ra, 1), ALU.min))
            step(v.tensor_tensor(fl(rb, 2), fl(ra, 2), fl(ra, 3), ALU.max))
            step(v.tensor_tensor(fl(rb, 1), fl(rb, 1), fl(rb, 2), ALU.max))
            step(v.tensor_tensor(fl(rb, 0), fl(rb, 0), fl(rb, 1), ALU.add))
            gs = fl(rb, 0).rearrange("p (t g) -> p t g", t=TL)

            def first_max(dst, src, weights, n, red, tmp):
                step(v.tensor_reduce(red, src, AX.X, ALU.max))
                step(v.tensor_tensor(tmp, src, red.unsqueeze(2).to_broadcast([P, TL, n]), ALU.is_equal))
                step(v.tensor_tensor(tmp, tmp, weights.unsqueeze(1).to_broadcast([P, TL, n]), ALU.mult))
                step(v.tensor_reduce(red, tmp, AX.X, ALU.max))
                step(v.tensor_tensor(dst, tmp, red.unsqueeze(2).to_broadcast([P, TL, n]), ALU.is_equal))

            red = small[:, 56:56 + TL]
            bestg = fl(rb, 2).rearrange("p (t g) -> p t g", t=TL)
            tmpg = fl(rb, 3).rearrange("p (t g) -> p t g", t=TL)
            first_max(bestg, gs, r_("first4"), NG, red, tmpg)
            step(v.tensor_scalar(tmpg, bestg, 1.0, BIG, ALU.subtract, ALU.mult))
            step(v.tensor_tensor(ra.rearrange("p t (g e) -> p (t g) e", g=NG), q,
                                 fl(rb, 3).unsqueeze(2).to_broadcast([P, G, EPG]), ALU.add))
            first_max(oh[0], ra, r_("first16"), NE, red, sel)
            step(v.scalar_tensor_tensor(ra, oh[0], -4.0 * BIG, ra, ALU.mult, ALU.add))
            first_max(oh[1], ra, r_("first16"), NE, red, sel)
            v.tensor_tensor(slot_of, oh[0], oh[1], ALU.add).then_inc(S_("picked"), 1)
            for i in range(2):
                step(v.tensor_tensor(ra, oh[i], score, ALU.mult))
                step(v.tensor_reduce(share[:, i, :], ra, AX.X, ALU.add))
            step(v.tensor_tensor(red, share[:, 0, :], share[:, 1, :], ALU.add))
            step(v.reciprocal(small[:, 60:60 + TL], red))
            for i in range(2):
                step(v.tensor_tensor(share[:, i, :], share[:, i, :], small[:, 60:60 + TL], ALU.mult))
            dve.wait_ge(*is_full(("rank",)))
            ps = bank(("rank",))
            step(v.tensor_copy(cnt, ps[:, TL * NE:(TL + 1) * NE]))
            step(v.tensor_tensor(over, cnt.unsqueeze(2).to_broadcast([P, NE, T // ROWS_A_TILE - 1]),
                                 r_("filled_tiles").unsqueeze(1).to_broadcast([P, NE, T // ROWS_A_TILE - 1]), ALU.is_gt))
            step(v.tensor_reduce(ntile, over, AX.X, ALU.add))
            step(v.tensor_scalar(ntile, ntile, 1.0, None, ALU.add))
            step(v.memset(first_tile, 0.0))
            step(v.tensor_tensor_scan(first_tile[:, 1:NE + 1], ones[:, 0:NE], ntile, 0.0, ALU.mult, ALU.add))
            v.tensor_copy(first_tile_i, first_tile).then_inc(S_("tiles_known"), 1)
            step(v.tensor_scalar(cnt, first_tile[:, 0:NE], float(ROWS_A_TILE), -1.0, ALU.mult, ALU.add))
            v.tensor_tensor(slot_of, ps[:, 0:TL * NE].rearrange("p (t e) -> p t e", t=TL),
                            cnt.unsqueeze(1).to_broadcast([P, TL, NE]), ALU.add).then_inc(is_free(("rank",))[0], 1)
            dve.wait_ge(*is_free(("rank",)))
            for i in range(2):
                step(v.tensor_tensor(ra, oh[i], slot_of, ALU.mult))
                step(v.tensor_reduce(small[:, 56:56 + TL], ra, AX.X, ALU.add))
                step(v.tensor_copy(xidx[:, i * TL:(i + 1) * TL], small[:, 56:56 + TL]))
                v.tensor_scalar(yidx[:, i * TL:(i + 1) * TL], small[:, 56:56 + TL], float(ROWS_A_TILE), None,
                                ALU.add).then_inc(S_("slots_known"), 1)
                dve.wait_ge(S_("slots_known"), i + 1)

            R = ROWS_A_TILE
            psU, psX, psY = bank(("U",)), bank(("X",)), bank(("Y",))
            v.memset(YT, 0.0).then_inc(S_("yT_zero"), 1)
            dve.wait_ge(S_("x1_ss"), TL)
            v.memset(ysb, 0.0).then_inc(S_("y_ready"), 1)
            A2 = modA[:, 2, :].unsqueeze(2).to_broadcast([P, KD, R])
            B2 = mod[:, 3 * KD:4 * KD, 0].unsqueeze(2).to_broadcast([P, KD, R])

            def modulate_x(n):
                dve.wait_ge(S_("x_turned"), n)
                v.tensor_tensor(XT, psX[:, :].rearrange("p (k r) -> p k r", r=R), A2, ALU.mult).then_inc(S_("x_scaled"), 1)
                dve.wait_ge(S_("x_scaled"), n)
                v.tensor_tensor(XT, XT, B2, ALU.add).then_inc(S_("x_ready"), 1)

            modulate_x(1)
            n = dve.value_load(first_tile_i[0:1, NE:NE + 1], min_val=1, max_val=XTILES)
            with dve.Fori(0, n) as j:
                dve.wait_ge(S_("g_ready"), j + 1)
                v.tensor_tensor(heT, sg, psU[:, :].rearrange("p (m r) -> p m r", r=R), ALU.mult)\
                    .then_inc(S_("he_ready"), 1)
                modulate_x(j + 2)
                dve.wait_ge(S_("y_turned"), j + 1)
                dve.wait_ge(S_("y_sent"), j * 16 + 16)
                v.tensor_copy(ysb[0:R, :], psY[0:R, :]).then_inc(S_("y_ready"), 1)
            dve.wait_ge(S_("y_turned"), n + 1)
            dve.wait_ge(S_("y_sent"), n * 16 + 16)
            v.tensor_copy(ysb[0:R, :], psY[0:R, :]).then_inc(S_("y_ready"), 1)
            dve.wait_ge(S_("y_back"), 16 * 2 * TL)
            for t in range(TL):
                step(v.tensor_scalar(yo[:, t, :], yback[:, t, :], share[:, 0, t:t + 1], None, ALU.mult))
                step(v.scalar_tensor_tensor(yo[:, t, :], yback[:, TL + t, :], share[:, 1, t:t + 1], yo[:, t, :],
                                            ALU.mult, ALU.add))
            for t in range(TL):
                step(v.tensor_tensor(yo[:, t, :], yo[:, t, :], g2row, ALU.mult))
                v.tensor_tensor(xr[:, t, :], xr[:, t, :], yo[:, t, :], ALU.add).then_inc(S_("x2_ready"), 1)
            rstd(small[:, 24:24 + TL], small[:, 32:32 + TL], small[:, 40:40 + TL], small[:, 48:48 + TL], TL, D,
                 "x2_ss", TL, "x2_var", "x2_std")
            dve.wait_ge(S_("x2_ready"), TL)
            dve.wait_ge(S_("frow_in"), 16)
            for t in range(TL):
                v.scalar_tensor_tensor(yo[:, t, :], xr[:, t, :], small[:, 24 + t:25 + t], frow,
                                              ALU.mult, ALU.mult).then_inc(S_("out_ready"), 1)


        @block.gpsimd
        def _(pool):
            R = ROWS_A_TILE
            pool.wait_ge(S_("zeros_made"), 1)
            pool.dma_start(slots.rearrange("(n p) d -> p n d", p=P),
                           zeros.unsqueeze(1).to_broadcast([P, XTILES * R // P, D])).then_inc(S_("x_zeroed"), 16)
            pool.wait_ge(S_("x_zeroed"), 16)
            pool.wait_ge(S_("slots_known"), 2)
            pool.wait_ge(S_("x1_normed"), TL)
            for i in range(2):
                for t in range(TL):
                    pool.indirect_dma_start(slots[:, :],
                                            bass.IndirectOffsetOnAxis(xidx[:, i * TL + t:i * TL + t + 1], 0),
                                            yo[:, t, :], None).then_inc(S_("x_sent"), 16)
            pool.wait_ge(S_("x_sent"), 16 * 2 * TL)
            pool.wait_ge(S_("x1_ss"), TL)
            pool.dma_start(xrow[0:R, :], slots[0:R, :]).then_inc(S_("xrow_in"), 16)
            pool.wait_ge(S_("y_ready"), 1)
            pool.dma_start(slots[0:R, :], ysb[0:R, :]).then_inc(S_("y_sent"), 16)
            pool.wait_ge(S_("x_turned"), 1)
            pool.dma_start(xrow[0:R, :], slots[R:2 * R, :]).then_inc(S_("xrow_in"), 16)
            n = pool.value_load(first_tile_i[0:1, NE:NE + 1], min_val=1, max_val=XTILES - 2)
            with pool.Fori(0, n) as j:
                pool.wait_ge(S_("x_turned"), j + 2)
                pool.dma_start(xrow[0:R, :], slots[bass.ds(j * R + 2 * R, R), :]).then_inc(S_("xrow_in"), 16)
                pool.wait_ge(S_("y_ready"), j + 2)
                pool.dma_start(slots[bass.ds(j * R, R), :], ysb[0:R, :]).then_inc(S_("y_sent"), 16)
            pool.wait_ge(S_("y_ready"), n + 2)
            pool.dma_start(slots[bass.ds(n * R, R), :], ysb[0:R, :]).then_inc(S_("y_sent"), 16)
            pool.wait_ge(S_("y_sent"), n * 16 + 32)
            pool.sem_inc(S_("pool_passed"), 1)
            for i in range(2):
                for t in range(TL):
                    pool.indirect_dma_start(yback[:, i * TL + t, :], None, slots[:, :],
                                            bass.IndirectOffsetOnAxis(yidx[:, i * TL + t:i * TL + t + 1], 0))\
                        .then_inc(S_("y_back"), 16)
            pool.wait_ge(S_("xrow_in"), n * 16 + 32)


def grid_positions():
    t = np.arange(T)
    quarter = D // 4
    freqs = np.exp(-np.log(10000.0) * np.arange(quarter, dtype=np.float32) / quarter).astype(np.float32)
    ar = (t // GRID_W).astype(np.float32)[:, None] * freqs
    ac = (t % GRID_W).astype(np.float32)[:, None] * freqs
    return np.concatenate([np.sin(ar), np.cos(ar), np.sin(ac), np.cos(ac)], axis=-1).astype(np.float32)


def constants():
    i = np.arange(P)
    squares = np.concatenate([np.eye(P), i[:, None] <= i[None, :], i[:, None] >= i[None, :], np.ones((P, P))], axis=1)
    k = np.arange(T)
    h = np.arange(T // 2)
    time = np.concatenate([np.cos(2 * np.pi * np.outer(h, k) / T), np.sin(2 * np.pi * np.outer(h, k) / T)])
    time[T // 2] = np.cos(np.pi * k)
    ang = 2 * np.pi * np.outer(np.arange(FG), np.arange(FG)) / FG
    unit = 1.0 / np.sqrt(T * FG)
    return {
        "squares": squares.astype(np.float32),
        "sel": np.tile(np.eye(SH), (3, 1)).astype(np.float32),
        "pos": grid_positions(),
        "dft_time": time.astype(np.float32),
        "dft_cos": (unit * np.cos(ang)).astype(np.float32),
        "dft_sin": (-unit * np.sin(ang)).astype(np.float32),
    }


def kernel(**inputs):
    import concourse.bacc as bacc
    from concourse.bass_utils import run_bass_kernel_spmd

    v = {k: np.asarray(x) for k, x in inputs.items()}
    f = np.float32

    def blocks(x):
        return np.ascontiguousarray(x.reshape(-1, P).T)

    both = np.stack([v["c"][0].reshape(KD, P), v["c_ctx"].reshape(KD, P)], axis=1).reshape(2 * KD, P).T
    conv_w = v["ssd_conv_w"][0].T.reshape(SCD // P, P, SK).transpose(1, 0, 2).reshape(P, -1)
    cols = np.concatenate([both, blocks(v["ada_b"][0]), blocks(v["norm1_g"][0]), blocks(v["norm2_g"][0]),
                           blocks(v["gla_a_b"][0].reshape(-1)), blocks(v["gla_norm_g"][0]), conv_w,
                           blocks(v["ssd_conv_b"][0]), blocks(v["ssd_norm_g"][0])], axis=1)
    rows = np.concatenate([v["ssd_dt_bias"][0].reshape(-1), v["ssd_a_log"][0].reshape(-1), v["ssd_d"][0],
                           v["router_b"], np.arange(NE, 0, -1, dtype=f), np.arange(NG, 0, -1, dtype=f),
                           ROWS_A_TILE * np.arange(1, T // ROWS_A_TILE, dtype=f)])
    arrays = {"cols": cols, "rows": np.broadcast_to(rows, (P, NROW)), "final_row": np.broadcast_to(v["final_g"], (P, D))}
    arrays.update(constants())
    for name in ("x", "ctx", "ada_w", "w_in", "gla_a_w", "gla_proj", "fnet_proj", "ssd_proj", "w_out", "router_w",
                 "exp_w1", "exp_w3", "exp_w2"):
        arrays[name] = v[name]
    arrays = {k: np.ascontiguousarray(x) for k, x in arrays.items()}
    nc = bacc.Bacc("TRN2", target_bir_lowering=False, num_devices=1)
    aps = {k: nc.dram_tensor(f"{k}_d", x.shape, mybir.dt.from_np(x.dtype), kind="ExternalInput").ap()
           for k, x in arrays.items()}
    out = nc.dram_tensor("out_d", (1, T, D), F32, kind="ExternalOutput").ap()
    build(nc, aps, out)
    r = run_bass_kernel_spmd(nc, [{f"{k}_d": x for k, x in arrays.items()}], core_ids=[0])
    return r.results[0]["out_d"]
```

```python
from contextlib import ExitStack

import numpy as np

import concourse.bass as bass
from concourse import mybir

F32 = mybir.dt.float32
BF16 = mybir.dt.bfloat16
I32 = mybir.dt.int32
ALU = mybir.AluOpType
ACT = mybir.ActivationFunctionType
AX = mybir.AxisListType

P = 128
D = 1024
T = 512
C = 256
NT = C + T
KD = D // P
TL = T // P
TC = C // P
TT = TL + TC
EPS = 1e-6
N_MOD = 6
GRID_W = 64

GH, GDK, GDV = 4, 128, 256
GQK, GV, GR = GH * GDK, GH * GDV, 16
TAU = 16.0

SI, SHD, SH, SG, SN, SK = 2048, 64, 32, 4, 128, 5
HPG = SH // SG
GW = HPG * SHD
SGN = SG * SN
SCD = SI + 2 * SGN

NE, NG, EPG, FF = 16, 4, 4, 512

SIZES = (GQK, GQK, GV, GV, GR, GR, D, SI, SCD, SH, SH, D, D, D)
OFF = [sum(SIZES[:i]) for i in range(len(SIZES) + 1)]
Q0, K0, V0, R0, LR0, _, U0, Z0, X0, DT0, _, GA0, GB0, GC0, D_IN = OFF
B0, C0 = X0 + SI, X0 + SI + SGN

FG = D // 4
BIG = 1e30

ROWS_A_TILE = 128
XTILES = 2 * T // ROWS_A_TILE + NE + 2


def spans(sizes):
    at, out = 0, {}
    for name, n in sizes:
        out[name] = (at, at + n)
        at += n
    return out, at


COLS, NCOL = spans([("c", 2 * KD), ("ada_b", N_MOD * KD), ("norm1", KD), ("norm2", KD), ("a_b", 2 * GH),
                    ("gla_norm", GDV // P), ("conv_w", SCD // P * SK), ("conv_b", SCD // P), ("ssd_norm", SI // P)])
ROWS, NROW = spans([("dt_bias", 2 * SH), ("a_log", 2 * SH), ("ssd_d", SH), ("router_b", NE),
                    ("first16", NE), ("first4", NG), ("filled_tiles", T // ROWS_A_TILE - 1)])
SQ, NSQ = spans([("ident", P), ("upto", P), ("from", P), ("ones", P)])


def build(nc, a, out):
    with ExitStack() as ctx:
        def sem(name):
            return ctx.enter_context(nc.semaphore(name))

        W = 53100
        arena = ctx.enter_context(nc.sbuf_tensor("arena", [P, W], F32))
        psum = ctx.enter_context(nc.psum_tensor("psum", [P, 8 * 512], F32))
        top = [0]

        def view(off, dims):
            n = int(np.prod(dims))
            v = arena[:, off:off + n]
            if len(dims) == 1:
                return v
            names = "abcde"[:len(dims)]
            return v.rearrange(f"p ({' '.join(names)}) -> p {' '.join(names)}", **dict(zip(names, dims)))

        def alloc(*dims):
            off = top[0]
            top[0] += int(np.prod(dims))
            top[0] += top[0] % 2
            assert top[0] <= W, top[0]
            return view(off, dims)

        NS = 3
        ring = [alloc(8 * 512) for _ in range(NS)]
        col = alloc(NCOL)
        row = alloc(NROW)
        sq = alloc(NSQ)
        identb = alloc(P // 2).bitcast(BF16)
        selb = alloc(SH // 2).bitcast(BF16)
        self_ = alloc(SH)
        wsmall = alloc(KD, 3 * GR + 2 * SH)
        mod = alloc(N_MOD * KD, 2)
        modA = alloc(3, KD)
        small = alloc(64)
        base = top[0]
        hT = alloc(KD, NT)
        phase_base = top[0]

        def c_(name):
            return col[:, COLS[name][0]:COLS[name][1]]

        def r_(name):
            return row[:, ROWS[name][0]:ROWS[name][1]]

        def s_(name):
            return sq[:, SQ[name][0]:SQ[name][1]]

        ident = s_("ident")
        mask = [s_("upto"), s_("from")]
        ones = s_("ones")

        xs = alloc(TT, D)
        pos = alloc(TL, D)
        junk = alloc(D)
        modrow = alloc(4 * 512)
        top[0] = phase_base
        dt = alloc(TT, 2 * SH)
        acs = alloc(TT, 2 * SH)
        eacs = alloc(TT, 2 * SH)
        wend = alloc(TT, 2 * SH)
        eend = alloc(TT, 2 * SH)
        nega = alloc(2 * SH)
        tmpd = [alloc(TT, 2 * SH) for _ in range(2)]
        acs3 = alloc(TL * 2 * 3 * SH // 2).bitcast(BF16).rearrange("p (t d s h) -> p t d s h", t=TL, d=2, s=3)
        rowsT = alloc(2 * T // 2).bitcast(BF16).rearrange("p (d t) -> p d t", d=2)
        RAW = C + T + 8
        LAT = C + 6
        raw = [alloc(RAW) for _ in range(2)]
        cacc = alloc(RAW)
        xcT = alloc(NT)
        BT = alloc(NT)
        CT = alloc(T)
        Btok = alloc(TT, P)
        xtok = alloc(TT, GW)
        xw = [alloc(GW) for _ in range(2)]
        xdt = alloc(TL, GW)
        yacc = alloc(TL, GW)
        cb = [alloc(TL, P) for _ in range(2)]
        NM = 4
        mm = [alloc(TL, P) for _ in range(NM)]
        S = [alloc(GW) for _ in range(2)]
        vtmp = alloc(GW)
        sz = alloc(TL, GW)
        res = sz[:, 0, 0:TL * 2 * SH].rearrange("p (t h) -> p t h", t=TL)
        yT = alloc(SI // P, T)
        ssq = alloc(TL, SG)
        rrow = alloc(T)
        top[0] = phase_base
        gateT = alloc(KD, T)
        mT = alloc(KD, T)
        gate_top = top[0]

        top[0] = gate_top
        qT = alloc(GH, T)
        kT = alloc(GH, NT)
        vtok = alloc(TT, GV)
        otok = alloc(TL, GV)
        lr2 = alloc(NT)
        aw = alloc(GQK)
        zb = alloc(NT)
        eb = alloc(NT)
        wb = alloc(NT)
        lb = alloc(NT)
        pc = alloc(TT, P + 1)
        dd = lb.rearrange("p (t l) -> p t l", t=TT)
        eq = alloc(TL, P)
        ek = alloc(TT, P)
        ekT = ek
        sc = alloc(TL, P)
        st = [alloc(GDV) for _ in range(2)]
        sadd = alloc(GDV)
        ea = alloc(TT)
        ebb = alloc(TT)
        dref = alloc(TT)
        gss = alloc(TL, GH)

        top[0] = gate_top
        uT = alloc(KD, T)
        ue = alloc(KD, T // 2)
        uo = alloc(KD, T // 2)
        At = alloc(TL, D)
        fT = alloc(TL, T)
        fC = alloc(2, FG)
        fS = alloc(2, FG)
        fyT = alloc(KD, T)
        ada_acc = alloc(8, 512)
        top[0] = base
        xr = alloc(TL, D)
        g1row = alloc(D)
        g2row = alloc(D)
        assert top[0] <= phase_base
        pos2 = view(phase_base, (TL, D))
        h2T = view(phase_base, (KD, T))
        top[0] = gate_top
        frow = alloc(D)
        yo = alloc(TL, D)
        rw = alloc(KD, NE)
        score = alloc(TL, NE)
        sel = alloc(TL, NE)
        ra = alloc(TL, NE)
        rb = alloc(TL, NE)
        oh = [alloc(TL, NE) for _ in range(2)]
        slot_of = alloc(TL, NE)
        before = alloc(TL + 1, NE)
        cnt = alloc(NE)
        over = alloc(NE, T // ROWS_A_TILE - 1)
        ntile = alloc(NE)
        first_tile = alloc(NE + 2)
        first_tile_i = alloc(NE + 2).bitcast(I32)
        share = alloc(2, TL)
        xidx = alloc(2 * TL).bitcast(I32)
        xrow = alloc(D)
        XT = alloc(KD, ROWS_A_TILE)
        sg = alloc(FF // P, ROWS_A_TILE)
        heT = alloc(FF // P, ROWS_A_TILE)
        ysb = alloc(D)
        junk2 = xrow
        route_T = xrow[:, 0:T]
        wset0 = top[0]
        wmem = [[alloc(8 * 512) for _ in range(3)], ring]
        yback = view(wset0, (2 * TL, D))
        v_off = gate_top + GH * T + GH * NT
        oT = view(v_off, (KD, T))
        zeros = yT[:, 0:2, :].rearrange("p a b -> p (a b)")
        slots = nc.dram_tensor("slots", [XTILES * ROWS_A_TILE, D], F32).ap()

        full = [sem(f"bank{b}_full") for b in range(8)]
        free = [sem(f"bank{b}_free") for b in range(8)]
        strip_in = [sem(f"strip{s}_in") for s in range(NS)]
        made = {}

        def S_(name):
            if name not in made:
                made[name] = sem(name)
            return made[name]

        turn = [0] * 8
        owner = [None] * 8
        place = {}
        nxt = {}

        def bank(key):
            b, n, _ = place[key]
            return psum[:, b * 512:(b + n) * 512]

        def is_full(key):
            return full[place[key][0]], place[key][2] + 1

        def is_free(key):
            return free[place[key][0]], place[key][2] + 1

        def open_(pe, key, n=1, lo=0, hi=8):
            b = nxt.get((lo, hi), lo)
            if b + n > hi:
                b = lo
            nxt[(lo, hi)] = b + n if b + n < hi else lo
            for o in dict.fromkeys(owner[b:b + n]):
                if o is not None:
                    pe.wait_ge(*is_free(o))
            assert key not in place, key
            place[key] = (b, n, turn[b])
            turn[b] += 1
            owner[b:b + n] = [key] * n
            return bank(key)

        strips = []
        ada_at = {}

        def strip(pe, pieces):
            n = len(strips)
            strips.append([pieces, None])
            pe.wait_ge(strip_in[n % NS], 16 * sum(len(strips[i][0]) for i in range(n % NS, n + 1, NS)))
            return ring[n % NS]

        def strip_used(key):
            strips[-1][1] = key

        def w_cols(w, c0, n=512, r0=0, rows=D):
            return w[r0:r0 + rows, c0:c0 + n].rearrange("(k p) n -> p k n", p=P)

        def full_strip(pe, w, c0, n=512, r0=0, rows=D):
            k = rows // P
            slot = strip(pe, [(lambda s: s[:, 0:k * n].rearrange("p (k n) -> p k n", k=k), w_cols(w, c0, n, r0, rows))])
            return slot[:, 0:k * n].rearrange("p (k n) -> p k n", k=k)

        w_in = a["w_in"][0]
        ada_w = a["ada_w"][0]

        ORDER = ([0, 1, 2, 3, 4, 5], [1, 0, 5, 4, 3, 2])
        Z_FRONT = 11
        Z_STATES = (3, 3, 3, 2, 1, 1)

        side = [("v", 1, t) for t in range(TT)] + [("ga", m) for m in range(KD)]
        SIDE_AHEAD = len(side) * KD // (2 * GH) - TT
        SIDE_TURN = 2

        block = ctx.enter_context(nc.Block())
        ENG = 3

        def phase_end(eng, n):
            eng.drain().then_inc(S_("phase_done"), 1)
            eng.wait_ge(S_("phase_done"), ENG * n)

        def x_turn(pe, g, m, lo=0):
            pe.wait_ge(S_("xc_ready"), g * 4 + m + 1)
            for half in range(2):
                key = ("xtok", g, m, half)
                ps = open_(pe, key, 1, lo, 8)
                for t in range(3):
                    tt = half * 3 + t
                    ins = nc.tensor.transpose(ps[:, t * P:(t + 1) * P], xcT[:, tt * P:(tt + 1) * P], ident)
                ins.then_inc(is_full(key)[0], 1)

        def gla_z(pe, h, d):
            pe.wait_ge(*is_free(("lr",)))
            key = ("gz", h * 2 + d)
            ps = open_(pe, key, 2, 0, 2)
            for c0, c1 in ((0, T), (T, NT)):
                ins = nc.tensor.matmul(ps[:, c0:c1], aw[32 * d:32 * d + GR, h * P:(h + 1) * P], lr2[32 * d:32 * d + GR, c0:c1],
                                       start=True, stop=True)
            ins.then_inc(is_full(key)[0], 1)

        @block.tensor
        def _(pe):
            mmul = nc.tensor.matmul

            def project_T(slot, m, src, key, nctx=False, lo=0, hi=8):
                ps = open_(pe, key, 2 if nctx else 1, lo, hi)
                for k in range(KD):
                    ins = mmul(ps[:, 0:T], slot[:, k, m * P:(m + 1) * P], src[:, k, C:NT],
                               start=(k == 0), stop=(k == KD - 1))
                if nctx:
                    for k in range(KD):
                        ins = mmul(ps[:, T:T + C], slot[:, k, m * P:(m + 1) * P], src[:, k, 0:C],
                                   start=(k == 0), stop=(k == KD - 1))
                ins.then_inc(is_full(key)[0], 1)

            def project_tok(slot, n, src, t, key):
                ps = open_(pe, key)
                for k in range(KD):
                    ins = mmul(ps[:, 0:n], src[:, k, t * P:(t + 1) * P], slot[:, k, 0:n],
                               start=(k == 0), stop=(k == KD - 1))
                ins.then_inc(is_full(key)[0], 1)

            def ada_strip(s):
                n = len(strips)
                pieces = [(lambda q: q.rearrange("p (k n) -> p k n", k=KD), w_cols(ada_w, s * 512))]
                strips.append([pieces, ("sem", "ada_summed", s - 3)])
                ada_at[s] = (ring[n % NS].rearrange("p (k n) -> p k n", k=KD), strip_in[n % NS],
                             16 * sum(len(strips[i][0]) for i in range(n % NS, n + 1, NS)))

            pe.wait_ge(S_("c_act"), 1)
            for s in range(4):
                slot = full_strip(pe, ada_w, s * 512)
                key = ("modrow", s)
                ps = open_(pe, key)
                for k in range(KD):
                    ins = mmul(ps[0:2, :], c_("c")[:, 2 * k:2 * k + 2], slot[:, k, :],
                               start=(k == 0), stop=(k == KD - 1))
                ins.then_inc(is_full(key)[0], 1)
                strip_used(key)
            pe.wait_ge(S_("consts_in"), 16 * 2)
            for k in range(KD):
                pe.wait_ge(S_("x_normed"), TT)
                for key, t0, n in ((("hT", k), TC, TL), (("hTc", k), 0, TC)):
                    ps = open_(pe, key)
                    for t in range(n):
                        ins = nc.tensor.transpose(ps[:, t * P:(t + 1) * P], xs[:, t0 + t, k * P:(k + 1) * P], ident)
                    ins.then_inc(is_full(key)[0], 1)
                if k == 0:
                    for s in range(4):
                        pe.wait_ge(*is_free(("modrow", s)))
                    key = ("mod",)
                    ps = open_(pe, key)
                    for m in range(16):
                        ins = mmul(ps[:, 2 * m:2 * m + 2], modrow[0:2, m * P:(m + 1) * P], ident[0:2, 0:2],
                                   start=True, stop=True)
                    ins.then_inc(is_full(key)[0], 1)
            for k in range(KD):
                pe.wait_ge(*is_free(("hT", k)))
                pe.wait_ge(*is_free(("hTc", k)))
            phase_end(pe, 1)

            pe.wait_ge(S_("small_in"), 32 * 3)
            key = ("dt",)
            ps = open_(pe, key)
            for t in range(TT):
                for k in range(KD):
                    ins = mmul(ps[:, t * 64:(t + 1) * 64], hT[:, k, t * P:(t + 1) * P], wsmall[:, k, 3 * GR:],
                               start=(k == 0), stop=(k == KD - 1))
            ins.then_inc(is_full(key)[0], 1)

            bc = [None]

            def B_part(g, i):
                if i == 0:
                    bc[0] = strip(pe, [(lambda s: s[:, 0:2048].rearrange("p (k n) -> p k n", k=KD)[:, :, 0:P],
                                        w_cols(w_in, B0 + g * SN, SN)),
                                       (lambda s: s[:, 0:2048].rearrange("p (k n) -> p k n", k=KD)[:, :, P:2 * P],
                                        w_cols(w_in, C0 + g * SN, SN))])[:, 0:2048].rearrange("p (k n) -> p k n", k=KD)
                    open_(pe, ("B", g), 2, 2, 4)
                ps = bank(("B", g))
                for q in range(16 * i // 7, 16 * (i + 1) // 7):
                    k, ctx_ = q % KD, q >= KD
                    o, src = (ps[:, T:T + C], hT[:, k, 0:C]) if ctx_ else (ps[:, 0:T], hT[:, k, C:NT])
                    ins = mmul(o, bc[0][:, k, 0:P], src, start=(k == 0), stop=(k == KD - 1))
                if i == 6:
                    ins.then_inc(is_full(("B", g))[0], 1)

            gc = [None]

            def next_part(g, i):
                if g < SG:
                    B_part(g, i)
                    return
                if i == 0:
                    gc[0] = full_strip(pe, w_in, GC0)
                    open_(pe, ("gc", 0), 1, 2, 4)
                for k in range(KD * i // 7, KD * (i + 1) // 7):
                    ins = mmul(bank(("gc", 0))[:, :], gc[0][:, k, 0:P], hT[:, k, C:NT],
                               start=(k == 0), stop=(k == KD - 1))
                if i == 6:
                    ins.then_inc(is_full(("gc", 0))[0], 1)

            def project_C(g):
                project_T(bc[0], 1, hT, ("C", g), lo=0, hi=2)
                strip_used(("C", g))
                if g:
                    y_turn(g - 1)

            for i in range(7):
                B_part(0, i)
            project_C(0)
            pe.wait_ge(S_("dta"), 1)
            key = ("acs",)
            ps = open_(pe, key, 2)
            dta = tmpd[0]
            for d in range(2):
                ins = mmul(ps[:, d * 192:(d + 1) * 192], mask[d], dta[:, :, d * SH:(d + 1) * SH], start=True, stop=True)
            ins = mmul(ps[:, 512:512 + TT * 64], ones, dta[:, :, :].rearrange("p t h -> p (t h)"), start=True, stop=True)
            ins.then_inc(is_full(key)[0], 1)
            pe.wait_ge(S_("acs_split"), 1)
            for d in range(2):
                key = ("acsT", d)
                ps = open_(pe, key).bitcast(BF16)
                for t in range(TL):
                    ins = nc.tensor.transpose(ps[0:3 * SH, t * P:(t + 1) * P],
                                              acs3[:, t, d, :, :].rearrange("p s h -> p (s h)"), identb)
                ins.then_inc(is_full(key)[0], 1)

            def y_turn(g):
                pe.wait_ge(S_("yz_ready"), (g + 1) * TL)
                for m in range(4):
                    key = ("yT", g, m)
                    ps = open_(pe, key)
                    for c in range(TL):
                        ins = nc.tensor.transpose(ps[:, c * P:(c + 1) * P], yacc[:, c, m * P:(m + 1) * P], ident)
                    ins.then_inc(is_full(key)[0], 1)

            for g in range(SG):
                if g:
                    project_C(g)
                slot = full_strip(pe, w_in, X0 + g * GW)
                for m in range(4):
                    project_T(slot, m, hT, ("x", g, m), nctx=True)
                    strip_used(("x", g, m))
                    if m == 0:
                        pe.wait_ge(S_("BT_ready"), g + 1)
                        for half in range(2):
                            key = ("Btok", g, half)
                            ps = open_(pe, key)
                            for t in range(3):
                                tt = half * 3 + t
                                ins = nc.tensor.transpose(ps[:, t * P:(t + 1) * P], BT[:, tt * P:(tt + 1) * P], ident)
                            ins.then_inc(is_full(key)[0], 1)
                    if m == 1:
                        pe.wait_ge(S_("CT_ready"), g + 1)
                        key = ("CB", g)
                        ps = open_(pe, key)
                        for c in range(TL):
                            ins = mmul(ps[:, c * P:(c + 1) * P], BT[:, C + c * P:C + (c + 1) * P],
                                       CT[:, c * P:(c + 1) * P], start=True, stop=True)
                        ins.then_inc(is_full(key)[0], 1)
                    if m >= 1:
                        x_turn(pe, g, m - 1)
                slot = full_strip(pe, w_in, Z0 + g * GW)
                z_done = [0]

                def z_part(n):
                    for q in range(z_done[0], z_done[0] + n):
                        t, k = q // KD, q % KD
                        key = ("z", g, t)
                        if k == 0:
                            open_(pe, key, 1, 3 if t == TL - 1 else 2, 4)
                        ins = mmul(bank(key)[:, :], hT[:, k, (TC + t) * P:(TC + t + 1) * P], slot[:, k, :],
                                   start=(k == 0), stop=(k == KD - 1))
                        if k == KD - 1:
                            ins.then_inc(is_full(key)[0], 1)
                    z_done[0] += n

                z_part(Z_FRONT)
                x_turn(pe, g, 3, 4)
                pe.wait_ge(*is_free(("Btok", g, 1)))

                def rows_of(d, h):
                    key = ("R", g, d, h)
                    ps = open_(pe, key, 1, 0, 2)
                    hh = g * HPG + h
                    pe.wait_ge(*is_free(("acsT", d)))
                    ins = mmul(ps[:, :], selb[0:3 * SH, hh:hh + 1].to_broadcast([3 * SH, P]),
                               rowsT[0:3 * SH, d, :], start=True, stop=True)
                    ins.then_inc(is_full(key)[0], 1)

                def state_step(d, i, lo, hi):
                    t = ORDER[d][i]
                    if i >= 2:
                        key = ("off", g, d, i)
                        ps = open_(pe, key, 1, lo, hi)
                        pe.wait_ge(*is_free(("kv", g, d, i - 1)))
                        ins = mmul(ps[:, :], CT[:, (t - TC) * P:(t - TC + 1) * P], S[(i - 1) % 2][:, :],
                                   start=True, stop=True)
                        ins.then_inc(is_full(key)[0], 1)
                    if i < 5:
                        key = ("kv", g, d, i)
                        pe.wait_ge(S_("xw_ready"), (g * 2 + d) * 5 + i + 1)
                        ps = open_(pe, key, 1, lo, hi)
                        ins = mmul(ps[:, :], Btok[:, t, :], xw[i % 2][:, :], start=True, stop=True)
                        ins.then_inc(is_full(key)[0], 1)

                for i in range(6):
                    state_step(0, i, 4, 8)
                    z_part(Z_STATES[i])
                for d in range(2):
                    rows_of(d, 0)
                    rows_of(d, 1)
                    if d:
                        for i in range(2):
                            next_part(g + 1, i)
                    pe.wait_ge(S_("xdt_ready"), g * 2 + d + 1)
                    yb = open_(pe, ("y", g, d), 4, 4, 8)
                    for h in range(HPG):
                        n = (g * 2 + d) * HPG + h
                        if h + 2 < HPG:
                            rows_of(d, h + 2)
                        if d == 0 and h < 6:
                            state_step(1, h, 2, 3)
                        pe.wait_ge(S_("M_ready"), n + 1)
                        for c in range(TL):
                            ins = mmul(yb[:, c * 512 + h * SHD:c * 512 + (h + 1) * SHD], mm[n % NM][:, c, :],
                                       xdt[:, c, h * SHD:(h + 1) * SHD], start=True, stop=True)
                        if h < HPG - 1:
                            ins.then_inc(S_("M_used"), 1)
                            if d == 0:
                                z_part(2 if h == 0 else 1)
                            elif h + 2 < 7:
                                next_part(g + 1, h + 2)
                    ins.then_inc(is_full(("y", g, d))[0], 1)
                    if d == 0:
                        strip_used(("z", g, TL - 1))
            for m in range(1, 4):
                project_T(gc[0], m, hT, ("gc", m))
            strip_used(("gc", 3))
            y_turn(SG - 1)

            pe.wait_ge(S_("ssd_rstd"), 1)
            key = ("rrow",)
            ps = open_(pe, key)
            for c in range(TL):
                ins = mmul(ps[:, c * P:(c + 1) * P], small[:, c:c + 1].to_broadcast([P, P]), ident,
                           start=True, stop=True)
            ins.then_inc(is_full(key)[0], 1)

            def gate_T(c0, name, ada=(None, None)):
                for j in range(2):
                    slot = full_strip(pe, w_in, c0 + j * 512)
                    for m in range(4):
                        project_T(slot, m, hT, (name, j * 4 + m))
                        strip_used((name, j * 4 + m))
                    if ada[j]:
                        ada_strip(ada[j])

            slot = full_strip(pe, w_in, GC0 + 512)
            for m in range(4):
                project_T(slot, m, hT, ("gc", 4 + m))
            strip_used(("gc", 7))
            pe.wait_ge(*is_free(("yT", SG - 1, 3)))
            for j in range(2):
                keys = [("pc", j * 4 + m) for m in range(4)]
                for kh in range(2):
                    slot = full_strip(pe, a["ssd_proj"][0], j * 512, 512, kh * D, D)
                    if kh == 0:
                        pss = [open_(pe, k) for k in keys]
                    for m in range(4):
                        for k in range(KD):
                            ins = mmul(pss[m][:, :], slot[:, k, m * P:(m + 1) * P], yT[:, kh * KD + k, :],
                                       start=(kh == 0 and k == 0), stop=(kh == 1 and k == KD - 1))
                        if kh == 1:
                            ins.then_inc(is_full(keys[m])[0], 1)
                        elif m == 3:
                            ins.then_inc(S_("pc_half"), 1)
                    strip_used(keys[3] if kh else ("sem", "pc_half", j + 1))
            phase_end(pe, 2)

            key = ("lr",)
            ps = open_(pe, key, 2)
            for c0, c1, o in ((C, NT, 0), (0, C, T)):
                for k in range(KD):
                    ins = mmul(ps[0:3 * GR, o:o + c1 - c0], wsmall[:, k, 0:3 * GR], hT[:, k, c0:c1],
                               start=(k == 0), stop=(k == KD - 1))
            ins.then_inc(is_full(key)[0], 1)
            slot = full_strip(pe, w_in, Q0)
            for m in range(4):
                project_T(slot, m, hT, ("q", m))
            strip_used(("q", 3))
            pe.wait_ge(S_("aw_in"), 16 * 2)
            gla_z(pe, 0, 0)
            slot = full_strip(pe, w_in, K0)
            for m in range(4):
                project_T(slot, m, hT, ("k", m), nctx=True)
            strip_used(("k", 3))
            slot = full_strip(pe, w_in, V0)
            for t in range(TT):
                project_tok(slot, 512, hT, t, ("v", 0, t))
            strip_used(("v", 0, TT - 1))
            side_done = [0]
            side_slot = [None]

            def side_part(n):
                for q in range(side_done[0], side_done[0] + n):
                    i, k = q // KD, q % KD
                    key = side[i]
                    if k == 0:
                        if i == 0:
                            side_slot[0] = full_strip(pe, w_in, V0 + 512)
                        elif i in (TT, TT + 4):
                            side_slot[0] = full_strip(pe, w_in, GA0 + (i - TT) // 4 * 512)
                        open_(pe, key, 1, 2, 4)
                    slot = side_slot[0]
                    if key[0] == "v":
                        ins = mmul(bank(key)[:, :], hT[:, k, key[2] * P:(key[2] + 1) * P], slot[:, k, :],
                                   start=(k == 0), stop=(k == KD - 1))
                    else:
                        ins = mmul(bank(key)[:, :], slot[:, k, key[1] % 4 * P:(key[1] % 4 + 1) * P], hT[:, k, C:NT],
                                   start=(k == 0), stop=(k == KD - 1))
                    if k == KD - 1:
                        ins.then_inc(is_full(key)[0], 1)
                        if i in (TT - 1, TT + 3, TT + 7):
                            strip_used(key)
                side_done[0] += n

            for h in range(GH):
                for d in range(2):
                    n = h * 2 + d
                    pe.wait_ge(*is_free(("lr",)))
                    order = [0, 1, 2, 3, 4, 5] if d == 0 else [1, 0, 5, 4, 3, 2]
                    side_part(SIDE_AHEAD - SIDE_TURN)
                    pe.wait_ge(S_("qk_ready"), n + 1)
                    key = ("sc", n)
                    ps = open_(pe, key, 1, 4, 8)
                    for c in range(TL):
                        ins = mmul(ps[:, c * P:(c + 1) * P], ek[:, TC + c, :], eq[:, c, :], start=True, stop=True)
                    ins.then_inc(is_full(key)[0], 1)
                    for half in range(2):
                        key = ("ekT", n, half)
                        ps = open_(pe, key, 1, 4, 8)
                        for t in range(3):
                            ins = nc.tensor.transpose(ps[:, t * P:(t + 1) * P], ek[:, half * 3 + t, :], ident)
                        ins.then_inc(is_full(key)[0], 1)
                    if n + 1 < 8:
                        gla_z(pe, (n + 1) // 2, (n + 1) % 2)
                    side_part(SIDE_TURN)
                    pe.wait_ge(*is_free(("v", h // 2, TT - 1)))
                    for i, t in enumerate(order):
                        if i < 5:
                            pe.wait_ge(*is_free(("ekT", n, t // 3)))
                            key = ("gkv", n, i)
                            ps = open_(pe, key, 1, 4, 8)
                            ins = mmul(ps[:, 0:GDV], ekT[:, t, :], vtok[:, t, h * GDV:(h + 1) * GDV],
                                       start=True, stop=True)
                            ins.then_inc(is_full(key)[0], 1)
                        if i >= 2:
                            pe.wait_ge(*is_free(("sc", n)))
                            key = ("o", n, i)
                            ps = open_(pe, key, 1, 4, 8)
                            mmul(ps[:, 0:GDV], sc[:, t - TC, :], vtok[:, t, h * GDV:(h + 1) * GDV],
                                 start=True, stop=False)
                            pe.wait_ge(S_("st_ready"), n * 4 + i - 1)
                            ins = mmul(ps[:, 0:GDV], eq[:, t - TC, :], st[(i - 1) % 2][:, :], start=False, stop=True)
                            ins.then_inc(is_full(key)[0], 1)
                        side_part(1)
            for j in range(2):
                slot = full_strip(pe, w_in, R0 + j * 512)
                for t in range(TL):
                    project_tok(slot, 512, hT, TC + t, ("r", j, t))
                strip_used(("r", j, TL - 1))
            pe.wait_ge(S_("o_gated"), 2 * TL)
            for m in range(KD):
                key = ("oT", m)
                ps = open_(pe, key)
                for c in range(TL):
                    ins = nc.tensor.transpose(ps[:, c * P:(c + 1) * P], otok[:, c, m * P:(m + 1) * P], ident)
                ins.then_inc(is_full(key)[0], 1)

            def branch(w, src, name, ada=(None, None)):
                for j in range(2):
                    slot = full_strip(pe, w, j * 512)
                    for m in range(4):
                        key = (name, j * 4 + m)
                        ps = open_(pe, key)
                        for k in range(KD):
                            ins = mmul(ps[:, :], slot[:, k, m * P:(m + 1) * P], src[:, k, :],
                                       start=(k == 0), stop=(k == KD - 1))
                        ins.then_inc(is_full(key)[0], 1)
                    strip_used((name, j * 4 + 3))
                    if ada[j]:
                        ada_strip(ada[j])

            for m in range(KD):
                pe.wait_ge(*is_free(("oT", m)))
            branch(a["gla_proj"][0], oT, "pa")
            phase_end(pe, 3)

            for j in range(2):
                slot = full_strip(pe, w_in, U0 + j * 512)
                for m in range(4):
                    project_T(slot, m, hT, ("u", j * 4 + m))
                strip_used(("u", j * 4 + 3))
            ada_strip(4)
            gate_T(GB0, "gb", (5, 6))
            for s in (7, 8, 9, 10):
                ada_strip(s)
            pe.wait_ge(S_("fconst_in"), 16 * 3)
            pe.wait_ge(S_("u_folded"), 1)
            for r in range(TL):
                src, f = (ue, fC) if r < 2 else (uo, fS)
                key = ("A", r)
                ps = open_(pe, key, 2)
                for g in range(4):
                    o = ps[:, g * FG:(g + 1) * FG]
                    for k in range(2):
                        ins = mmul(o, src[:, 2 * g + k, (r % 2) * P:(r % 2 + 1) * P], f[:, k, :],
                                   start=(k == 0), stop=(k == 1))
                        if r == 2 and k == 0:
                            for q in range(2):
                                mmul(ps[0:1, g * FG:(g + 1) * FG], uT[:, 2 * g + q, T // 2:T // 2 + 1], fC[:, q, :],
                                     start=False, stop=False, skip_group_check=True)
                ins.then_inc(is_full(key)[0], 1)
            for r in range(TL):
                pe.wait_ge(*is_free(("A", r)))
            for m in range(KD):
                key = ("fy", m)
                ps = open_(pe, key)
                for r in range(TL):
                    ins = mmul(ps[:, :], At[:, r, m * P:(m + 1) * P], fT[:, r, :], start=(r == 0), stop=(r == TL - 1))
                ins.then_inc(is_full(key)[0], 1)
            for m in range(KD):
                pe.wait_ge(*is_free(("fy", m)))
            branch(a["fnet_proj"][0], fyT, "pb", (11, None))
            key = ("mod2",)
            pe.wait_ge(S_("ada_summed"), 8)
            ps = open_(pe, key)
            for m in range(2 * KD):
                ins = mmul(ps[:, m:m + 1], ada_acc[:, 2 + m // 4, m % 4 * P:(m % 4 + 1) * P], ones[:, 0:1],
                           start=True, stop=True)
            ins.then_inc(is_full(key)[0], 1)
            for name, s in (("g1", 0), ("g2", 6)):
                for j in range(2):
                    key = (name, j)
                    ps = open_(pe, key)
                    mmul(ps[:, :], ones, ada_acc[:, s + j, :], start=True, stop=True).then_inc(is_full(key)[0], 1)
            phase_end(pe, 4)

            for j in range(2):
                slot = full_strip(pe, a["w_out"][0], j * 512)
                for t in range(TL):
                    project_tok(slot, 512, mT, t, ("wo", j, t))
                strip_used(("wo", j, TL - 1))
            for k in range(KD):
                pe.wait_ge(S_("x1_normed"), TL)
                key = ("h2T", k)
                ps = open_(pe, key)
                for t in range(TL):
                    ins = nc.tensor.transpose(ps[:, t * P:(t + 1) * P], yo[:, t, k * P:(k + 1) * P], ident)
                ins.then_inc(is_full(key)[0], 1)
            key = ("routeT",)
            pe.wait_ge(S_("rw_in"), 16)
            ps = open_(pe, key)
            for k in range(KD):
                pe.wait_ge(*is_free(("h2T", k)))
                ins = mmul(ps[0:NE, :], rw[:, k, :], h2T[:, k, :], start=(k == 0), stop=(k == KD - 1))
            ins.then_inc(is_full(key)[0], 1)
            pe.wait_ge(*is_free(key))
            key = ("route",)
            ps = open_(pe, key)
            for t in range(TL):
                ins = mmul(ps[:, t * NE:(t + 1) * NE], route_T[0:NE, t * P:(t + 1) * P], ident[0:NE, 0:NE],
                           start=True, stop=True)
            ins.then_inc(is_full(key)[0], 1)

            pe.wait_ge(S_("picked"), 1)
            ps = open_(pe, ("rank",))
            picks = slot_of.rearrange("p t e -> p (t e)")
            mmul(ps[:, 0:TL * NE], mask[0], picks, start=True, stop=True)
            ins = mmul(ps[:, TL * NE:2 * TL * NE], ones, picks, start=True, stop=True)
            ins.then_inc(is_full(("rank",))[0], 1)

            R = ROWS_A_TILE
            psG = [open_(pe, ("G", i), 1, b, b + 1) for i, b in enumerate((0, 6))]
            psU = [open_(pe, ("U", i), 1, b, b + 1) for i, b in enumerate((1, 7))]
            psX = open_(pe, ("X",), 2, 2, 4)
            psD = open_(pe, ("D",), 2, 4, 6)

            def turn_x():
                for k in range(KD):
                    ins = nc.tensor.transpose(psX[:, k * R:(k + 1) * R], xrow[0:R, k * P:(k + 1) * P],
                                              ident[0:R, 0:R])
                ins.then_inc(S_("x_turned"), 1)

            pe.wait_ge(S_("xrow_in"), 16)
            turn_x()
            pe.wait_ge(S_("tiles_known"), 1)
            with pe.Fori(0, NE // 2) as pair:
                for par in range(2):
                    w1, w3, w2 = (w.rearrange("p (k n) -> p k n", k=k) for w, k in zip(wmem[par], (KD, KD, FF // P)))
                    e = pair * 2 + par
                    lo = pe.value_load(first_tile_i[0:1, bass.ds(e, 1)], min_val=0, max_val=XTILES)
                    hi = pe.value_load(first_tile_i[0:1, bass.ds(e + 1, 1)], min_val=0, max_val=XTILES)
                    pe.wait_ge(S_("w_in%d" % par), pair * 48 + 48)
                    pe.sem_inc(S_("pe_passed"), 1)
                    with pe.Fori(lo, hi) as j:
                        pe.wait_ge(S_("x_ready"), j + 1)
                        for m in range(FF // P):
                            for w, ps in ((w1, psG), (w3, psU)):
                                for k in range(KD):
                                    ins = mmul(ps[m // 2][:, m % 2 * R:(m % 2 + 1) * R], w[:, k, m * P:(m + 1) * P], XT[:, k, :],
                                               start=(k == 0), stop=(k == KD - 1))
                            if m % 2:
                                ins.then_inc(S_("up_full"), 1)
                        pe.wait_ge(S_("xrow_in"), j * 16 + 32)
                        pe.sem_inc(S_("pe_passed"), 1)
                        turn_x()
                        pe.wait_ge(S_("he_ready"), j * 2 + 2)
                        pe.wait_ge(S_("y_ready"), j + 1)
                        pe.sem_inc(S_("pe_passed"), 1)
                        for half in range(2):
                            for k in range(FF // P):
                                ins = mmul(psD[:, half * 512:(half + 1) * 512], heT[:, k, :],
                                           w2[:, k, half * 512:(half + 1) * 512],
                                           start=(k == 0), stop=(k == FF // P - 1))
                        ins.then_inc(S_("down_full"), 1)

        @block.sync
        def _(sp):
            sp.dma_start(col, a["cols"]).then_inc(S_("cols_in"), 16)
            for n, (pieces, _) in enumerate(strips):
                if n >= NS:
                    key = strips[n - NS][1]
                    if key[0] == "sem":
                        sp.wait_ge(S_(key[1]), key[2])
                    else:
                        sp.wait_ge(*is_full(key))
                for dst, src in pieces:
                    sp.dma_start(dst(ring[n % NS]), src).then_inc(strip_in[n % NS], 16)
                if n == 0:
                    sp.dma_start(row, a["rows"]).then_inc(S_("rows_in"), 16)
            sp.wait_ge(S_("phase_done"), ENG * 4)

            def weights(e, par, names, slots):
                for name, i in zip(names, slots):
                    src = a[name][0, e] if isinstance(e, int) else a[name][0, bass.ds(e, 1), :, :].rearrange("o r n -> (o r) n")
                    k = FF // P if name == "exp_w2" else KD
                    sp.dma_start(wmem[par][i].rearrange("p (k n) -> p k n", k=k),
                                 src.rearrange("(k p) n -> p k n", p=P)).then_inc(S_("w_in%d" % par), 16)

            weights(0, 0, ("exp_w1", "exp_w3", "exp_w2"), (0, 1, 2))
            for n in range(len(strips) - NS, len(strips)):
                sp.wait_ge(*is_full(strips[n][1]))
            weights(1, 1, ("exp_w1", "exp_w3", "exp_w2"), (0, 1, 2))
            sp.wait_ge(S_("tiles_known"), 1)
            with sp.Fori(1, NE // 2) as pair:
                for par in range(2):
                    e = pair * 2 + par
                    used = sp.value_load(first_tile_i[0:1, bass.ds(e - 1, 1)], min_val=1, max_val=XTILES)
                    sp.wait_ge(S_("up_full"), used * 2)
                    weights(e, par, ("exp_w1", "exp_w3"), (0, 1))
                    sp.wait_ge(S_("down_full"), used)
                    weights(e, par, ("exp_w2",), (2,))
            for i in range(TL // 2):
                for t, name in ((i, "out_ready"), (TL // 2 + i, "out_ready_act")):
                    sp.wait_ge(S_(name), i + 1)
                    sp.dma_start(out[0, t * P:(t + 1) * P, :], yo[:, t, :]).then_inc(S_("out_sent"), 16)
            sp.wait_ge(S_("out_sent"), 16 * TL)

        @block.scalar
        def _(act):
            run = nc.scalar.activation
            n_ = [0]

            def step(ins):
                n_[0] += 1
                ins.then_inc(S_("act_step"), 1)
                act.wait_ge(S_("act_step"), n_[0])

            act.dma_start(xs[:, 0:TC, :], a["ctx"][0].rearrange("(t p) d -> p t d", p=P)).then_inc(S_("ctx_in"), 16)
            for t in range(TL):
                act.dma_start(xs[:, TC + t, :], a["x"][0, t * P:(t + 1) * P, :]).then_inc(S_("x_in%d" % t), 16)
                act.dma_start(pos[:, t, :], a["pos"][t * P:(t + 1) * P, :]).then_inc(S_("x_in%d" % t), 16)
            act.dma_start(sq, a["squares"]).then_inc(S_("consts_in"), 16)
            act.dma_start(self_[0:3 * SH, :], a["sel"]).then_inc(S_("consts_in"), 16)
            for d0, c0, n in ((0, LR0, GR), (GR, LR0, 2 * GR), (3 * GR, DT0, 2 * SH)):
                act.dma_start(wsmall[:, :, d0:d0 + n], w_cols(w_in, c0, n),
                              allow_slow_non_contiguous=True).then_inc(S_("small_in"), 32)

            act.wait_ge(S_("cols_in"), 16)
            run(c_("c"), c_("c"), ACT.Silu).then_inc(S_("c_act"), 1)
            for t in range(TT):
                if t < TC:
                    act.wait_ge(S_("ctx_in"), 16)
                else:
                    act.wait_ge(S_("x_pos"), t - TC + 1)
                if t:
                    act.wait_ge(S_("x_ss"), t)
                ins = run(junk, xs[:, t, :], ACT.Square, accum_out=small[:, t:t + 1])
                ins.then_inc(S_("x_ss"), 1)
            act.wait_ge(S_("x_var"), 1)
            run(small[:, 16:16 + TT], small[:, 8:8 + TT], ACT.Sqrt).then_inc(S_("x_std"), 1)
            for s in range(4):
                key = ("modrow", s)
                act.wait_ge(*is_full(key))
                run(modrow[0:2, s * 512:(s + 1) * 512], bank(key)[0:2, :], ACT.Copy).then_inc(is_free(key)[0], 1)
            act.wait_ge(S_("modA1"), 1)
            for k in range(KD):
                for key, j, lo, n in ((("hT", k), 0, C, T), (("hTc", k), 1, 0, C)):
                    act.wait_ge(*is_full(key))
                    ps = bank(key)
                    run(hT[:, k, lo:lo + n], ps[:, 0:n], ACT.Identity, scale=modA[:, j, k:k + 1],
                             bias=mod[:, k, j:j + 1]).then_inc(is_free(key)[0], 1)
            phase_end(act, 1)

            run(nega, r_("a_log"), ACT.Exp).then_inc(S_("nega"), 1)
            act.wait_ge(S_("dt_negabs"), 1)
            run(tmpd[1], tmpd[1], ACT.Exp).then_inc(S_("dt_exp"), 1)
            act.wait_ge(S_("dt_w"), 1)
            run(wend, dt, ACT.Ln).then_inc(S_("dt_ln"), 1)

            def raw_evac(key, rn):
                if rn >= 2:
                    act.wait_ge(S_("conv_done"), rn - 1)
                act.wait_ge(*is_full(key))
                ps = bank(key)
                dst = raw[rn % 2]
                if key[0] != "C":
                    step(run(dst[:, 2:2 + C], ps[:, T:T + C], ACT.Copy))
                run(dst[:, LAT:LAT + T], ps[:, 0:T], ACT.Copy).then_inc(is_free(key)[0], 1)

            act.wait_ge(S_("raw_zero"), 1)
            raw_evac(("B", 0), 0)
            raw_evac(("C", 0), 1)
            act.wait_ge(S_("acs_out"), 1)
            run(wend, wend, ACT.Exp).then_inc(S_("acs_exps"), 1)
            run(eend, tmpd[1], ACT.Exp).then_inc(S_("acs_exps"), 1)
            run(eacs, acs, ACT.Exp).then_inc(S_("acs_exps"), 1)
            for d in range(2):
                act.wait_ge(*is_full(("acsT", d)))
                ps = bank(("acsT", d))
                ps = ps.bitcast(BF16)
                run(rowsT[0:3 * SH, d, :], ps[0:3 * SH, 0:T], ACT.Copy).then_inc(is_free(("acsT", d))[0], 1)
            def yT_evac(g):
                if g == 0:
                    act.wait_ge(S_("x_zeroed"), 16)
                for m in range(4):
                    key = ("yT", g, m)
                    act.wait_ge(*is_full(key))
                    blk = g * 4 + m
                    run(yT[:, blk, :], bank(key)[:, :], ACT.Identity, scale=c_("ssd_norm")[:, blk:blk + 1],
                        bias=0.0).then_inc(is_free(key)[0], 1)

            for g in range(SG):
                def silu_conv(kind, m, rn):
                    act.wait_ge(S_("conv_done"), rn + 1)
                    if kind == "x":
                        blk = g * 4 + m
                        bias = c_("conv_b")[:, blk:blk + 1]
                        prev = ("xtok", g, m - 1, 1) if m else (("xtok", g - 1, 3, 1) if g else None)
                        if prev:
                            act.wait_ge(*is_full(prev))
                        run(xcT[:, 0:C], cacc[:, 0:C], ACT.Silu, bias=bias)
                        run(xcT[:, C:NT], cacc[:, C + 4:C + 4 + T], ACT.Silu, bias=bias).then_inc(S_("xc_ready"), 1)
                    elif kind == "B":
                        bias = c_("conv_b")[:, 16 + g:17 + g]
                        if g:
                            act.wait_ge(*is_full(("CB", g - 1)))
                        run(BT[:, 0:C], cacc[:, 0:C], ACT.Silu, bias=bias)
                        run(BT[:, C:NT], cacc[:, C + 4:C + 4 + T], ACT.Silu, bias=bias).then_inc(S_("BT_ready"), 1)
                    else:
                        if g:
                            act.wait_ge(*is_full(("off", g - 1, 1, 5)))
                        run(CT, cacc[:, C + 4:C + 4 + T], ACT.Silu, bias=c_("conv_b")[:, 20 + g:21 + g]).then_inc(S_("CT_ready"), 1)

                def xtok_evac(m):
                    if g:
                        act.wait_ge(S_("xw_ready"), g * 10)
                        act.wait_ge(S_("xdt_ready"), g * 2)
                        act.wait_ge(S_("y_started"), g)
                    for half in range(2):
                        key = ("xtok", g, m, half)
                        act.wait_ge(*is_full(key))
                        ps = bank(key)
                        run(xtok[:, half * 3:half * 3 + 3, m * P:(m + 1) * P],
                                 ps[:, 0:3 * P].rearrange("p (t n) -> p t n", t=3), ACT.Copy).then_inc(is_free(key)[0], 1)

                if g:
                    raw_evac(("B", g), g * 6)
                silu_conv("B", 0, g * 6)
                if g:
                    raw_evac(("C", g), g * 6 + 1)
                    yT_evac(g - 1)
                silu_conv("C", 0, g * 6 + 1)
                for m in range(4):
                    raw_evac(("x", g, m), g * 6 + 2 + m)
                    if m == 0:
                        for half in range(2):
                            key = ("Btok", g, half)
                            act.wait_ge(*is_full(key))
                            if g:
                                act.wait_ge(*is_full(("kv", g - 1, 1, 4)))
                            run(Btok[:, half * 3:half * 3 + 3, :], bank(key)[:, 0:3 * P].rearrange("p (t n) -> p t n", t=3),
                                ACT.Copy).then_inc(is_free(key)[0], 1)
                    else:
                        xtok_evac(m - 1)
                    silu_conv("x", m, g * 6 + 2 + m)

                def z_silu(t):
                    key = ("z", g, t)
                    act.wait_ge(*is_full(key))
                    if g:
                        act.wait_ge(S_("yz_squared"), g * 4)
                    run(sz[:, t, :], bank(key)[:, :], ACT.Silu).then_inc(is_free(key)[0], 1)

                z_silu(0)
                xtok_evac(3)
                for d in range(2):
                    if d == 0:
                        z_silu(1)
                        z_silu(2)
                    for h in range(HPG):
                        n = (g * 2 + d) * HPG + h
                        act.wait_ge(*is_free(("R", g, d, h)))
                        run(mm[n % NM], mm[n % NM], ACT.Exp).then_inc(S_("decay_ready"), 1)
                    if d == 0:
                        z_silu(3)
                for t in range(TL):
                    act.wait_ge(S_("yz_ready"), g * 4 + t + 1)
                    run(sz[:, t, :], yacc[:, t, :], ACT.Square, accum_out=ssq[:, t, g:g + 1]).then_inc(S_("yz_squared"), 1)
            act.wait_ge(S_("ssd_var"), 1)
            run(small[:, 16:16 + TL], small[:, 8:8 + TL], ACT.Sqrt).then_inc(S_("ssd_std"), 1)

            def gates(name, m0=0, m1=KD):
                for m in range(m0, m1):
                    act.wait_ge(*is_full((name, m)))
                    ps = bank((name, m))
                    run(gateT[:, m, :], ps[:, :], ACT.Sigmoid).then_inc(is_free((name, m))[0], 1)

            gates("gc", 0, 4)
            yT_evac(SG - 1)
            act.wait_ge(*is_full(("rrow",)))
            ps = bank(("rrow",))
            run(rrow, ps[:, :], ACT.Copy).then_inc(is_free(("rrow",))[0], 1)

            gates("gc", 4)
            phase_end(act, 2)

            for d in range(2):
                act.dma_start(aw[32 * d:32 * d + GR, :], a["gla_a_w"][0, d]).then_inc(S_("aw_in"), 16)
            act.wait_ge(*is_full(("lr",)))
            ps = bank(("lr",))
            run(lr2[0:3 * GR, 0:C], ps[0:3 * GR, T:NT], ACT.Copy)
            run(lr2[0:3 * GR, C:NT], ps[0:3 * GR, 0:T], ACT.Copy).then_inc(is_free(("lr",))[0], 1)
            for m in range(4):
                act.wait_ge(*is_full(("q", m)))
                ps = bank(("q", m))
                run(qT[:, m, :], ps[:, :], ACT.Copy).then_inc(is_free(("q", m))[0], 1)
            for m in range(4):
                act.wait_ge(*is_full(("k", m)))
                ps = bank(("k", m))
                run(kT[:, m, 0:C], ps[:, T:NT], ACT.Copy)
                run(kT[:, m, C:NT], ps[:, 0:T], ACT.Copy).then_inc(is_free(("k", m))[0], 1)

            def side_evac(key):
                act.wait_ge(*is_full(key))
                dst = vtok[:, key[2], key[1] * 512:(key[1] + 1) * 512] if key[0] == "v" else gateT[:, key[1], :]
                run(dst, bank(key)[:, :], ACT.Copy).then_inc(is_free(key)[0], 1)

            def log_sigmoid(n):
                act.wait_ge(S_("gz_negabs"), n + 1)
                run(eb, eb, ACT.Exp).then_inc(S_("gz_exp"), 1)
                act.wait_ge(S_("gz_w"), n + 1)
                run(wb, wb, ACT.Ln).then_inc(S_("gz_ln"), 1)

            log_sigmoid(0)
            for t in range(TT):
                side_evac(("v", 0, t))
            for n in range(8):
                act.wait_ge(S_("decay_refd"), n + 1)
                sgn = 1.0 if n % 2 == 0 else -1.0
                if n:
                    act.wait_ge(*is_full(("o", n - 1, 5)))
                run(eq, dd[:, TC:TT, :], ACT.Exp, scale=sgn / TAU)
                run(ek, dd, ACT.Exp, scale=-sgn / TAU)
                run(ea, pc[:, :, P // 2], ACT.Exp, scale=1.0 / TAU)
                run(ebb, dref, ACT.Exp, scale=1.0 / TAU).then_inc(S_("gla_exps"), 1)
                for half in range(2):
                    key = ("ekT", n, half)
                    act.wait_ge(*is_full(key))
                    ps = bank(key)
                    run(ekT[:, half * 3:half * 3 + 3, :], ps[:, 0:3 * P].rearrange("p (t n) -> p t n", t=3),
                             ACT.Copy).then_inc(is_free(key)[0], 1)
                if n < 7:
                    log_sigmoid(n + 1)
                a_n = (SIDE_AHEAD + TT)
                for i in range(n * a_n // KD, (n + 1) * a_n // KD):
                    side_evac(side[i])
            for m in range(KD):
                act.wait_ge(*is_free(("ga", m)))
                run(gateT[:, m, :], gateT[:, m, :], ACT.Sigmoid).then_inc(S_("ga_ready"), 1)
            act.wait_ge(S_("o_all"), 1)
            for c in range(TL):
                for h in range(GH):
                    if h or c:
                        step(ins)
                    ins = run(zb[:, 0:GDV], otok[:, c, h * GDV:(h + 1) * GDV], ACT.Square,
                              accum_out=gss[:, c, h:h + 1])
            ins.then_inc(S_("o_squared"), 1)
            act.wait_ge(S_("o_var"), 1)
            run(gss, gss, ACT.Sqrt).then_inc(S_("o_std"), 1)
            rbuf = [eb, wb]
            for j in range(2):
                for t in range(TL):
                    i = j * TL + t
                    act.wait_ge(*is_full(("r", j, t)))
                    ps = bank(("r", j, t))
                    if i >= 2:
                        act.wait_ge(S_("o_gated"), i - 1)
                    run(rbuf[i % 2][:, 0:512], ps[:, :], ACT.Silu).then_inc(is_free(("r", j, t))[0], 1)
            for m in range(KD):
                act.wait_ge(*is_full(("oT", m)))
                ps = bank(("oT", m))
                run(oT[:, m, :], ps[:, :], ACT.Identity, scale=c_("gla_norm")[:, m % 2:m % 2 + 1], bias=0.0).then_inc(is_free(("oT", m))[0], 1)
            phase_end(act, 3)

            act.dma_start(fT, a["dft_time"].rearrange("(r p) k -> p r k", p=P)).then_inc(S_("fconst_in"), 16)
            act.dma_start(fC, a["dft_cos"].rearrange("(r p) k -> p r k", p=P)).then_inc(S_("fconst_in"), 16)
            act.dma_start(fS, a["dft_sin"].rearrange("(r p) k -> p r k", p=P)).then_inc(S_("fconst_in"), 16)
            for m in range(KD):
                act.wait_ge(*is_full(("u", m)))
                ps = bank(("u", m))
                run(uT[:, m, :], ps[:, :], ACT.Copy).then_inc(is_free(("u", m))[0], 1)
            gates("gb")
            for r in range(TL):
                act.wait_ge(*is_full(("A", r)))
                ps = bank(("A", r))
                run(At[:, r, :], ps[:, :], ACT.Copy).then_inc(is_free(("A", r))[0], 1)
            for m in range(KD):
                act.wait_ge(*is_full(("fy", m)))
                ps = bank(("fy", m))
                run(fyT[:, m, :], ps[:, :], ACT.Copy).then_inc(is_free(("fy", m))[0], 1)
            phase_end(act, 4)

            act.dma_start(g1row, a["gate_rows"][:, 0:D]).then_inc(S_("gates_in"), 16)
            act.dma_start(g2row, a["gate_rows"][:, D:2 * D]).then_inc(S_("gates_in"), 16)
            act.dma_start(xr, a["x"][0].rearrange("(t p) d -> p t d", p=P)).then_inc(S_("xr_in"), 16)
            act.dma_start(pos2, a["pos"].rearrange("(t p) d -> p t d", p=P)).then_inc(S_("xr_in"), 16)
            act.dma_start(rw, a["router_w"].rearrange("(k p) e -> p k e", p=P)).then_inc(S_("rw_in"), 16)
            act.dma_start(frow, a["final_row"]).then_inc(S_("frow_in"), 16)
            for t in range(TL):
                act.wait_ge(S_("x1_ready"), TL + t + 1)
                if t:
                    act.wait_ge(S_("x1_ss"), t)
                ins = run(junk2, xr[:, t, :], ACT.Square, accum_out=small[:, t:t + 1])
                ins.then_inc(S_("x1_ss"), 1)
            act.wait_ge(S_("x1_var"), 1)
            run(small[:, 16:16 + TL], small[:, 8:8 + TL], ACT.Sqrt).then_inc(S_("x1_std"), 1)
            for k in range(KD):
                act.wait_ge(*is_full(("h2T", k)))
                ps = bank(("h2T", k))
                run(h2T[:, k, :], ps[:, :], ACT.Identity, scale=modA[:, 2, k:k + 1],
                         bias=mod[:, 3 * KD + k, 0:1]).then_inc(is_free(("h2T", k))[0], 1)
            act.wait_ge(*is_full(("routeT",)))
            run(route_T[0:NE, :], bank(("routeT",))[0:NE, :], ACT.Copy).then_inc(is_free(("routeT",))[0], 1)
            act.wait_ge(*is_full(("route",)))
            ps = bank(("route",))
            run(score, ps[:, 0:TL * NE].rearrange("p (t e) -> p t e", t=TL), ACT.Sigmoid).then_inc(is_free(("route",))[0], 1)
            R = ROWS_A_TILE
            psG = [bank(("G", half)) for half in range(2)]
            act.wait_ge(S_("tiles_known"), 1)
            n = act.value_load(first_tile_i[0:1, NE:NE + 1], min_val=1, max_val=XTILES)
            with act.Fori(0, n) as j:
                for half in range(2):
                    act.wait_ge(S_("up_full"), j * 2 + (half + 1))
                    run(sg[:, 2 * half:2 * half + 2, :],
                        psG[half][:, 0:2 * R].rearrange("p (m r) -> p m r", r=R),
                        ACT.Silu).then_inc(S_("g_ready"), 1)
            for t in range(TL):
                act.wait_ge(S_("x2_ready"), t + 1)
                if t:
                    act.wait_ge(S_("x2_ss"), t)
                run(junk2, xr[:, t, :], ACT.Square, accum_out=small[:, 32 + t:33 + t]).then_inc(S_("x2_ss"), 1)
            act.wait_ge(S_("x2_var"), 1)
            run(small[:, 48:48 + TL], small[:, 40:40 + TL], ACT.Sqrt).then_inc(S_("x2_std"), 1)
            act.wait_ge(S_("x2_rstd"), 1)
            act.wait_ge(S_("x2_rowed"), TL)
            for t in range(TL // 2, TL):
                run(yo[:, t, :], yo[:, t, :], ACT.Copy, scale=small[:, 24 + t:25 + t]).then_inc(S_("out_ready_act"), 1)

        @block.vector
        def _(dve):
            v = nc.vector
            n_ = [0]

            def step(ins):
                n_[0] += 1
                ins.then_inc(S_("dve_step"), 1)
                dve.wait_ge(S_("dve_step"), n_[0])

            def ada_sum(s):
                slot, arrived, count = ada_at[s]
                dve.wait_ge(arrived, count)
                acc = ada_acc[:, s - 4, :]
                c = c_("c")
                step(v.tensor_scalar(acc, slot[:, 0, :], c[:, 0:1], None, ALU.mult))
                for k in range(1, KD):
                    ins = v.scalar_tensor_tensor(acc, slot[:, k, :], c[:, 2 * k:2 * k + 1], acc, ALU.mult, ALU.add)
                    if k < KD - 1:
                        step(ins)
                ins.then_inc(S_("ada_summed"), 1)

            def rstd(dst, ss, var, std, n, width, name_ss, cnt, name_var, name_std):
                dve.wait_ge(S_(name_ss), cnt)
                v.tensor_scalar(var, ss, 1.0 / width, EPS, ALU.mult, ALU.add).then_inc(S_(name_var), 1)
                dve.wait_ge(S_(name_std), 1)
                v.reciprocal(dst, std).then_inc(S_(name_std.replace("std", "rstd")), 1)
                dve.wait_ge(S_(name_std.replace("std", "rstd")), 1)

            for t in range(TT):
                if t >= TC:
                    dve.wait_ge(S_("x_in%d" % (t - TC)), 32)
                    v.tensor_tensor(xs[:, t, :], xs[:, t, :], pos[:, t - TC, :], ALU.add).then_inc(S_("x_pos"), 1)
            rstd(small[:, 24:24 + TT], small[:, 0:TT], small[:, 8:8 + TT], small[:, 16:16 + TT], TT, D,
                 "x_ss", TT, "x_var", "x_std")
            for t in range(TT):
                v.tensor_scalar(xs[:, t, :], xs[:, t, :], small[:, 24 + t:25 + t], None, ALU.mult).then_inc(S_("x_normed"), 1)
            key = ("mod",)
            dve.wait_ge(*is_full(key))
            v.tensor_tensor(mod[:, 0:16, :], bank(key)[:, 0:32].rearrange("p (m j) -> p m j", j=2),
                            c_("ada_b")[:, 0:16].unsqueeze(2).to_broadcast([P, 16, 2]), ALU.add)\
                .then_inc(is_free(key)[0], 1)
            dve.wait_ge(*is_free(key))
            for j in range(2):
                ins = v.scalar_tensor_tensor(modA[:, j, :], mod[:, KD:2 * KD, j], 1.0, c_("norm1"), ALU.add, ALU.mult)
                if j == 0:
                    step(ins)
            ins.then_inc(S_("modA1"), 1)
            phase_end(dve, 1)

            for i in range(2):
                ins = v.memset(raw[i], 0.0)
                if i == 0:
                    step(ins)
            ins.then_inc(S_("raw_zero"), 1)
            v.memset(zeros, 0.0).then_inc(S_("zeros_made"), 1)
            dve.wait_ge(S_("rows_in"), 16)
            dve.wait_ge(*is_full(("dt",)))
            ps = bank(("dt",))
            x_, e_ = tmpd
            v.tensor_tensor(x_, ps[:, 0:TT * 64].rearrange("p (t h) -> p t h", t=TT),
                                 r_("dt_bias").unsqueeze(1).to_broadcast([P, TT, 64]), ALU.add).then_inc(is_free(("dt",))[0], 1)
            dve.wait_ge(*is_free(("dt",)))
            v.scalar_tensor_tensor(e_, x_, -1.0, x_, ALU.mult, ALU.min).then_inc(S_("dt_negabs"), 1)
            dve.wait_ge(S_("dt_exp"), 1)
            step(v.tensor_scalar(dt, e_, 1.0, None, ALU.add))
            v.scalar_tensor_tensor(eacs, dt, -1.0, e_, ALU.add, ALU.subtract).then_inc(S_("dt_w"), 1)
            dve.wait_ge(S_("dt_ln"), 1)
            step(v.tensor_tensor(wend, wend, eacs, ALU.subtract))
            step(v.scalar_tensor_tensor(dt, x_, 0.0, wend, ALU.max, ALU.add))
            dve.wait_ge(S_("nega"), 1)
            v.scalar_tensor_tensor(tmpd[0], dt, -1.0, nega.unsqueeze(1).to_broadcast([P, TT, 64]),
                                          ALU.mult, ALU.mult).then_inc(S_("dta"), 1)
            dve.wait_ge(*is_full(("acs",)))
            ps = bank(("acs",))
            for d in range(2):
                step(v.tensor_copy(acs[:, :, d * SH:(d + 1) * SH],
                                   ps[:, d * 192:(d + 1) * 192].rearrange("p (t h) -> p t h", t=TT)))
            v.tensor_copy(tmpd[1], ps[:, 512:512 + TT * 64].rearrange("p (t h) -> p t h", t=TT)).then_inc(is_free(("acs",))[0], 1)
            dve.wait_ge(*is_free(("acs",)))
            v.tensor_tensor(wend, tmpd[1], acs, ALU.subtract).then_inc(S_("acs_out"), 1)
            lat = acs[:, TC:TT, :].rearrange("p t (d h) -> p t d h", d=2)
            r4 = res.rearrange("p t (d h) -> p t d h", d=2)
            dve.wait_ge(S_("consts_in"), 16 * 2)
            step(v.tensor_copy(identb, ident))
            step(v.tensor_copy(selb[0:3 * SH, :], self_[0:3 * SH, :]))
            step(v.tensor_copy(acs3[:, :, :, 0, :], lat))
            step(v.tensor_tensor(r4, lat, acs3[:, :, :, 0, :], ALU.subtract))
            step(v.tensor_copy(acs3[:, :, :, 1, :], r4))
            step(v.tensor_tensor(r4, r4, acs3[:, :, :, 1, :], ALU.subtract))
            v.tensor_copy(acs3[:, :, :, 2, :], r4).then_inc(S_("acs_split"), 1)
            dve.wait_ge(S_("acs_exps"), 3)
            v.tensor_tensor(wend, wend, dt, ALU.mult).then_inc(S_("steps_ready"), 1)

            heads = lambda x: x.rearrange("p (h q) -> p h q", h=HPG)

            def conv(g, kind, m):
                rn = g * 6 + {"B": 0, "C": 1, "x": 2 + m}[kind]
                blk = {"x": g * 4 + m, "B": 16 + g, "C": 20 + g}[kind]
                key = ("x", g, m) if kind == "x" else (kind, g)
                dve.wait_ge(*is_free(key))
                if rn:
                    if kind == "x" and m:
                        dve.wait_ge(S_("xc_ready"), g * 4 + m)
                    elif kind == "x":
                        dve.wait_ge(S_("CT_ready"), g + 1)
                    elif kind == "B":
                        dve.wait_ge(S_("xc_ready"), g * 4)
                    else:
                        dve.wait_ge(S_("BT_ready"), g + 1)
                lo, hi = (0, C + 4 + T) if kind != "C" else (C + 4, C + 4 + T)
                w = c_("conv_w")
                src = raw[rn % 2]
                step(v.tensor_scalar(cacc[:, lo:hi], src[:, lo:hi], w[:, blk * SK:blk * SK + 1], None, ALU.mult))
                for k in range(1, SK):
                    ins = v.scalar_tensor_tensor(cacc[:, lo:hi], src[:, lo + k:hi + k],
                                                 w[:, blk * SK + k:blk * SK + k + 1], cacc[:, lo:hi], ALU.mult, ALU.add)
                    if k < SK - 1:
                        step(ins)
                ins.then_inc(S_("conv_done"), 1)

            for g in range(SG):
                conv(g, "B", 0)
                conv(g, "C", 0)
                conv(g, "x", 0)
                conv(g, "x", 1)
                key = ("CB", g)
                dve.wait_ge(*is_full(key))
                if g:
                    dve.wait_ge(S_("M_ready"), g * 2 * HPG)
                for d in range(2):
                    ins = v.tensor_tensor(cb[d], bank(key)[:, :].rearrange("p (c l) -> p c l", c=TL),
                                          mask[d].unsqueeze(1).to_broadcast([P, TL, P]), ALU.mult)
                    if d == 0:
                        step(ins)
                ins.then_inc(is_free(key)[0], 1)
                conv(g, "x", 2)
                conv(g, "x", 3)
                dve.wait_ge(S_("y_started"), g + 1)

                def state_step(d, i):
                    t = ORDER[d][i]
                    hs = d * SH + g * HPG
                    per_head = lambda q: q[:, t, hs:hs + HPG].unsqueeze(2).to_broadcast([P, HPG, SHD])
                    if i >= 2:
                        key = ("off", g, d, i)
                        dve.wait_ge(*is_full(key))
                        c = t - TC
                        v.tensor_tensor(heads(vtmp), heads(bank(key)[:, :]), per_head(eacs), ALU.mult)\
                            .then_inc(is_free(key)[0], 1)
                        dve.wait_ge(*is_free(key))
                        step(v.tensor_tensor(yacc[:, c, :], yacc[:, c, :], vtmp, ALU.add))
                    if i < 5:
                        key = ("kv", g, d, i)
                        dve.wait_ge(*is_full(key))
                        if i == 0:
                            ins = v.tensor_copy(S[0], bank(key)[:, :])
                        else:
                            step(v.tensor_tensor(heads(vtmp), heads(S[(i - 1) % 2]), per_head(eend), ALU.mult))
                            ins = v.tensor_tensor(S[i % 2], vtmp, bank(key)[:, :], ALU.add)
                        ins.then_inc(is_free(key)[0], 1)
                        dve.wait_ge(*is_free(key))

                def exponents(d, h):
                    n = (g * 2 + d) * HPG + h
                    at = d * SH + g * HPG + h
                    key = ("R", g, d, h)
                    dve.wait_ge(*is_full(key))
                    if n >= NM:
                        o = n - NM
                        if o % HPG == HPG - 1:
                            dve.wait_ge(*is_full(("y", o // HPG // 2, o // HPG % 2)))
                        else:
                            dve.wait_ge(S_("M_used"), o // HPG * (HPG - 1) + o % HPG + 1)
                    for c in range(TL):
                        ins = v.tensor_scalar(mm[n % NM][:, c, :], bank(key)[:, c * P:(c + 1) * P],
                                              acs[:, TC + c, at:at + 1], 0.0, ALU.subtract, ALU.min)
                    ins.then_inc(is_free(key)[0], 1)

                for i in range(6):
                    state_step(0, i)
                for d in range(2):
                    exponents(d, 0)
                    for h in range(HPG):
                        if h + 1 < HPG:
                            exponents(d, h + 1)
                        if d == 0 and h < 6:
                            state_step(1, h)
                    key = ("y", g, d)
                    dve.wait_ge(*is_full(key))
                    for c in range(TL):
                        ins = v.tensor_tensor(yacc[:, c, :], yacc[:, c, :], bank(key)[:, c * 512:(c + 1) * 512], ALU.add)
                        if c < TL - 1:
                            step(ins)
                    ins.then_inc(is_free(key)[0], 1)
                    dve.wait_ge(*is_free(key))
                for t in range(TL):
                    dve.wait_ge(*is_free(("z", g, t)))
                    v.tensor_tensor(yacc[:, t, :], yacc[:, t, :], sz[:, t, :], ALU.mult).then_inc(S_("yz_ready"), 1)
            dve.wait_ge(S_("yz_squared"), SG * TL)
            step(v.tensor_reduce(small[:, 0:TL], ssq, AX.X, ALU.add))
            dve.wait_ge(S_("yz_squared"), SG * TL)
            v.tensor_scalar(small[:, 8:8 + TL], small[:, 0:TL], 1.0 / SI, EPS, ALU.mult, ALU.add).then_inc(S_("ssd_var"), 1)
            dve.wait_ge(S_("ssd_std"), 1)
            v.reciprocal(small[:, 0:TL], small[:, 16:16 + TL]).then_inc(S_("ssd_rstd"), 1)
            dve.wait_ge(*is_free(("rrow",)))
            for m in range(KD):
                dve.wait_ge(*is_free(("gc", m)))
                step(v.tensor_tensor(gateT[:, m, :], gateT[:, m, :], rrow, ALU.mult))
            for m in range(KD):
                key = ("pc", m)
                dve.wait_ge(*is_full(key))
                ps = bank(key)
                v.tensor_tensor(mT[:, m, :], ps[:, :], gateT[:, m, :], ALU.mult).then_inc(is_free(key)[0], 1)
            phase_end(dve, 2)

            step(v.memset(pc[:, :, 0:1], 0.0))

            def decays(n, i):
                h, d = n // 2, n % 2
                if i == 0:
                    key = ("gz", n)
                    dve.wait_ge(*is_full(key))
                    v.tensor_scalar(zb, bank(key)[:, 0:NT], c_("a_b")[:, d * GH + h:d * GH + h + 1], None, ALU.add)\
                        .then_inc(is_free(key)[0], 1)
                    dve.wait_ge(*is_free(key))
                    v.scalar_tensor_tensor(eb, zb, -1.0, zb, ALU.mult, ALU.min).then_inc(S_("gz_negabs"), 1)
                elif i == 1:
                    dve.wait_ge(S_("gz_exp"), n + 1)
                    step(v.tensor_scalar(wb, eb, 1.0, None, ALU.add))
                    v.scalar_tensor_tensor(lb, wb, -1.0, eb, ALU.add, ALU.subtract).then_inc(S_("gz_w"), 1)
                elif i == 2:
                    dve.wait_ge(S_("gz_ln"), n + 1)
                    step(v.tensor_tensor(wb, wb, lb, ALU.subtract))
                    step(v.scalar_tensor_tensor(zb, zb, 0.0, wb, ALU.min, ALU.subtract))
                elif i < 5:
                    for t in range(3 * (i - 3), 3 * (i - 2)):
                        step(v.tensor_tensor_scan(pc[:, t, 1:P + 1], ones, zb[:, t * P:(t + 1) * P], 0.0,
                                                  ALU.mult, ALU.add))
                else:
                    ref = pc[:, :, P // 2:P // 2 + 1]
                    step(v.tensor_tensor(dd, pc[:, :, 1:P + 1] if d == 0 else pc[:, :, 0:P],
                                         ref.to_broadcast([P, TT, P]), ALU.subtract))
                    v.tensor_tensor(dref, pc[:, :, P], pc[:, :, P // 2], ALU.subtract).then_inc(S_("decay_refd"), 1)

            for i in range(6):
                decays(0, i)
            for h in range(GH):
                for d in range(2):
                    n = h * 2 + d
                    order = [0, 1, 2, 3, 4, 5] if d == 0 else [1, 0, 5, 4, 3, 2]
                    dve.wait_ge(S_("gla_exps"), n + 1)
                    if n == 0:
                        for m in range(4):
                            dve.wait_ge(*is_free(("k", m)))
                    step(v.scalar_tensor_tensor(eq.rearrange("p c l -> p (c l)"), eq.rearrange("p c l -> p (c l)"),
                                                float(GDK) ** -0.5, qT[:, h, :], ALU.mult, ALU.mult))
                    v.tensor_tensor(ek.rearrange("p c l -> p (c l)"), ek.rearrange("p c l -> p (c l)"),
                                           kT[:, h, :], ALU.mult).then_inc(S_("qk_ready"), 1)
                    key = ("sc", n)
                    dve.wait_ge(*is_full(key))
                    ps = bank(key)
                    v.tensor_tensor(sc, ps[:, :].rearrange("p (c l) -> p c l", c=TL),
                                         mask[d].unsqueeze(1).to_broadcast([P, TL, P]), ALU.mult).then_inc(is_free(key)[0], 1)
                    start, end = (ea, ebb) if d == 0 else (ebb, ea)
                    for i, t in enumerate(order):
                        if n < 7:
                            decays(n + 1, i)
                        if i < 5:
                            key = ("gkv", n, i)
                            dve.wait_ge(*is_full(key))
                            ps = bank(key)
                            src = ps[:, 0:GDV]
                            if i:
                                v.tensor_tensor(sadd, src, st[(i - 1) % 2], ALU.add).then_inc(is_free(key)[0], 1)
                                dve.wait_ge(*is_free(key))
                                src = sadd
                            ins = v.tensor_scalar(st[i % 2], src, end[:, t:t + 1], start[:, order[i + 1]:order[i + 1] + 1],
                                                  ALU.mult, ALU.mult)
                            if i:
                                ins.then_inc(S_("st_ready"), 1)
                                dve.wait_ge(S_("st_ready"), n * 4 + i)
                            else:
                                ins.then_inc(is_free(key)[0], 1)
                                dve.wait_ge(*is_free(key))
                        if i >= 2:
                            key = ("o", n, i)
                            dve.wait_ge(*is_full(key))
                            ps = bank(key)
                            o = otok[:, t - TC, h * GDV:(h + 1) * GDV]
                            if d == 0:
                                v.tensor_copy(o, ps[:, 0:GDV]).then_inc(is_free(key)[0], 1)
                            else:
                                v.tensor_tensor(o, o, ps[:, 0:GDV], ALU.add).then_inc(is_free(key)[0], 1)
                            dve.wait_ge(*is_free(key))
            dve.drain().then_inc(S_("o_all"), 1)
            dve.wait_ge(S_("o_squared"), 1)
            v.tensor_scalar(gss, gss, 1.0 / GDV, EPS, ALU.mult, ALU.add).then_inc(S_("o_var"), 1)
            dve.wait_ge(S_("o_std"), 1)
            step(v.reciprocal(gss, gss))
            for c in range(TL):
                o = otok[:, c, :].rearrange("p (h q) -> p h q", h=GH)
                step(v.tensor_tensor(o, o, gss[:, c, :].unsqueeze(2).to_broadcast([P, GH, GDV]), ALU.mult))
            rbuf = [eb, wb]
            for j in range(2):
                for t in range(TL):
                    i = j * TL + t
                    dve.wait_ge(*is_free(("r", j, t)))
                    o = otok[:, t, j * 512:(j + 1) * 512]
                    v.tensor_tensor(o, o, rbuf[i % 2][:, 0:512], ALU.mult).then_inc(S_("o_gated"), 1)

            def merge(gate_name, name, tmp):
                for m in range(KD):
                    if gate_name == "ga":
                        dve.wait_ge(S_("ga_ready"), m + 1)
                    else:
                        dve.wait_ge(*is_free((gate_name, m)))
                    key = (name, m)
                    dve.wait_ge(*is_full(key))
                    ps = bank(key)
                    v.tensor_tensor(tmp, ps[:, :], gateT[:, m, :], ALU.mult).then_inc(is_free(key)[0], 1)
                    dve.wait_ge(*is_free(key))
                    step(v.tensor_tensor(mT[:, m, :], mT[:, m, :], tmp, ALU.add))

            merge("ga", "pa", zb[:, 0:T])
            phase_end(dve, 3)

            for m in range(KD):
                dve.wait_ge(*is_free(("u", m)))
            H = T // 2
            v.tensor_tensor(ue[:, :, 1:H], uT[:, :, 1:H], uT[:, :, T - 1:H:-1], ALU.add)
            v.tensor_tensor(uo[:, :, 1:H], uT[:, :, 1:H], uT[:, :, T - 1:H:-1], ALU.subtract)
            v.tensor_copy(ue[:, :, 0:1], uT[:, :, 0:1])
            v.memset(uo[:, :, 0:1], 0.0).then_inc(S_("u_folded"), 1)
            for s in range(4, 12):
                ada_sum(s)
            merge("gb", "pb", At[:, 0, 0:T])
            key = ("mod2",)
            dve.wait_ge(*is_full(key))
            v.tensor_tensor(mod[:, 3 * KD:5 * KD, 0], bank(key)[:, 0:2 * KD], c_("ada_b")[:, 3 * KD:5 * KD], ALU.add)\
                .then_inc(is_free(key)[0], 1)
            dve.wait_ge(*is_free(key))
            step(v.scalar_tensor_tensor(modA[:, 2, :], mod[:, 4 * KD:5 * KD, 0], 1.0, c_("norm2"), ALU.add, ALU.mult))
            phase_end(dve, 4)

            dve.wait_ge(S_("gates_in"), 16 * 2)
            for name, dst in (("g1", g1row), ("g2", g2row)):
                for j in range(2):
                    dve.wait_ge(*is_full((name, j)))
                    sl = slice(j * 512, (j + 1) * 512)
                    v.tensor_tensor(dst[:, sl], dst[:, sl], bank((name, j))[:, :], ALU.add)\
                        .then_inc(is_free((name, j))[0], 1)
            for j in range(2):
                dve.wait_ge(*is_free(("g1", j)))
                dve.wait_ge(*is_free(("g2", j)))
            dve.wait_ge(S_("xr_in"), 32)
            step(v.tensor_tensor(xr, xr, pos2, ALU.add))
            for j in range(2):
                for t in range(TL):
                    key = ("wo", j, t)
                    dve.wait_ge(*is_full(key))
                    ps = bank(key)
                    sl = slice(j * 512, (j + 1) * 512)
                    v.tensor_tensor(yo[:, t, sl], ps[:, :], g1row[:, sl], ALU.mult).then_inc(is_free(key)[0], 1)
                    dve.wait_ge(*is_free(key))
                    v.tensor_tensor(xr[:, t, sl], xr[:, t, sl], yo[:, t, sl], ALU.add).then_inc(S_("x1_ready"), 1)
            rstd(small[:, 24:24 + TL], small[:, 0:TL], small[:, 8:8 + TL], small[:, 16:16 + TL], TL, D,
                 "x1_ss", TL, "x1_var", "x1_std")
            dve.wait_ge(S_("x1_ready"), 2 * TL)
            for t in range(TL):
                v.tensor_scalar(yo[:, t, :], xr[:, t, :], small[:, 24 + t:25 + t], None, ALU.mult).then_inc(S_("x1_normed"), 1)

            dve.wait_ge(*is_free(("route",)))
            step(v.tensor_tensor(sel, score, r_("router_b").unsqueeze(1).to_broadcast([P, TL, NE]), ALU.add))
            G = TL * NG
            q = sel.rearrange("p t (g e) -> p (t g) e", g=NG)
            f = lambda x, i: x.rearrange("p t (i g) -> p i (t g)", i=NG)[:, i, :]
            fl = lambda x, i: x.rearrange("p t e -> p (t e)")[:, i * G:(i + 1) * G]
            for i in range(2):
                step(v.tensor_tensor(fl(ra, i), q[:, :, 2 * i], q[:, :, 2 * i + 1], ALU.max))
                step(v.tensor_tensor(fl(ra, 2 + i), q[:, :, 2 * i], q[:, :, 2 * i + 1], ALU.min))
            step(v.tensor_tensor(fl(rb, 0), fl(ra, 0), fl(ra, 1), ALU.max))
            step(v.tensor_tensor(fl(rb, 1), fl(ra, 0), fl(ra, 1), ALU.min))
            step(v.tensor_tensor(fl(rb, 2), fl(ra, 2), fl(ra, 3), ALU.max))
            step(v.tensor_tensor(fl(rb, 1), fl(rb, 1), fl(rb, 2), ALU.max))
            step(v.tensor_tensor(fl(rb, 0), fl(rb, 0), fl(rb, 1), ALU.add))
            gs = fl(rb, 0).rearrange("p (t g) -> p t g", t=TL)

            def first_max(dst, src, weights, n, red, tmp):
                step(v.tensor_reduce(red, src, AX.X, ALU.max))
                step(v.tensor_tensor(tmp, src, red.unsqueeze(2).to_broadcast([P, TL, n]), ALU.is_equal))
                step(v.tensor_tensor(tmp, tmp, weights.unsqueeze(1).to_broadcast([P, TL, n]), ALU.mult))
                step(v.tensor_reduce(red, tmp, AX.X, ALU.max))
                step(v.tensor_tensor(dst, tmp, red.unsqueeze(2).to_broadcast([P, TL, n]), ALU.is_equal))

            red = small[:, 56:56 + TL]
            bestg = fl(rb, 2).rearrange("p (t g) -> p t g", t=TL)
            tmpg = fl(rb, 3).rearrange("p (t g) -> p t g", t=TL)
            first_max(bestg, gs, r_("first4"), NG, red, tmpg)
            step(v.tensor_scalar(tmpg, bestg, 1.0, BIG, ALU.subtract, ALU.mult))
            step(v.tensor_tensor(ra.rearrange("p t (g e) -> p (t g) e", g=NG), q,
                                 fl(rb, 3).unsqueeze(2).to_broadcast([P, G, EPG]), ALU.add))
            first_max(oh[0], ra, r_("first16"), NE, red, sel)
            step(v.scalar_tensor_tensor(ra, oh[0], -4.0 * BIG, ra, ALU.mult, ALU.add))
            first_max(oh[1], ra, r_("first16"), NE, red, sel)
            v.tensor_tensor(slot_of, oh[0], oh[1], ALU.add).then_inc(S_("picked"), 1)
            for i in range(2):
                step(v.tensor_tensor(ra, oh[i], score, ALU.mult))
                step(v.tensor_reduce(share[:, i, :], ra, AX.X, ALU.add))
            step(v.tensor_tensor(red, share[:, 0, :], share[:, 1, :], ALU.add))
            step(v.reciprocal(small[:, 60:60 + TL], red))
            for i in range(2):
                step(v.tensor_tensor(share[:, i, :], share[:, i, :], small[:, 60:60 + TL], ALU.mult))
            dve.wait_ge(*is_full(("rank",)))
            ps = bank(("rank",))
            step(v.memset(before[:, 0, :], 0.0))
            for t in range(TL):
                step(v.tensor_tensor(before[:, t + 1, :], before[:, t, :], ps[:, (TL + t) * NE:(TL + t + 1) * NE],
                                     ALU.add))
            step(v.tensor_tensor(over, before[:, TL, :].unsqueeze(2).to_broadcast([P, NE, T // ROWS_A_TILE - 1]),
                                 r_("filled_tiles").unsqueeze(1).to_broadcast([P, NE, T // ROWS_A_TILE - 1]), ALU.is_gt))
            step(v.tensor_reduce(ntile, over, AX.X, ALU.add))
            step(v.tensor_scalar(ntile, ntile, 1.0, None, ALU.add))
            step(v.memset(first_tile, 0.0))
            step(v.tensor_tensor_scan(first_tile[:, 1:NE + 1], ones[:, 0:NE], ntile, 0.0, ALU.mult, ALU.add))
            v.tensor_copy(first_tile_i, first_tile).then_inc(S_("tiles_known"), 1)
            step(v.tensor_scalar(cnt, first_tile[:, 0:NE], float(ROWS_A_TILE), -1.0, ALU.mult, ALU.add))
            v.tensor_tensor(slot_of, ps[:, 0:TL * NE].rearrange("p (t e) -> p t e", t=TL), before[:, 0:TL, :],
                            ALU.add).then_inc(is_free(("rank",))[0], 1)
            dve.wait_ge(*is_free(("rank",)))
            step(v.tensor_tensor(slot_of, slot_of, cnt.unsqueeze(1).to_broadcast([P, TL, NE]), ALU.add))
            for i in range(2):
                step(v.tensor_tensor(ra, oh[i], slot_of, ALU.mult))
                step(v.tensor_reduce(small[:, 56:56 + TL], ra, AX.X, ALU.add))
                v.tensor_copy(xidx[:, i * TL:(i + 1) * TL], small[:, 56:56 + TL]).then_inc(S_("slots_known"), 1)
                dve.wait_ge(S_("slots_known"), i + 1)

            R = ROWS_A_TILE
            psU = [bank(("U", half)) for half in range(2)]
            psX, psD = bank(("X",)), bank(("D",))
            dve.wait_ge(S_("x1_ss"), TL)
            v.memset(ysb, 0.0).then_inc(S_("y_ready"), 1)
            A2 = modA[:, 2, :].unsqueeze(2).to_broadcast([P, KD, R])
            B2 = mod[:, 3 * KD:4 * KD, 0].unsqueeze(2).to_broadcast([P, KD, R])

            def modulate_x(n):
                dve.wait_ge(S_("x_turned"), n)
                v.tensor_tensor(XT, psX[:, :].rearrange("p (k r) -> p k r", r=R), A2, ALU.mult).then_inc(S_("x_scaled"), 1)
                dve.wait_ge(S_("x_scaled"), n)
                v.tensor_tensor(XT, XT, B2, ALU.add).then_inc(S_("x_ready"), 1)

            modulate_x(1)
            n = dve.value_load(first_tile_i[0:1, NE:NE + 1], min_val=1, max_val=XTILES)
            with dve.Fori(0, n) as j:
                for half in range(2):
                    dve.wait_ge(S_("g_ready"), j * 2 + (half + 1))
                    v.tensor_tensor(heT[:, 2 * half:2 * half + 2, :], sg[:, 2 * half:2 * half + 2, :],
                                    psU[half][:, 0:2 * R].rearrange("p (m r) -> p m r", r=R),
                                    ALU.mult).then_inc(S_("he_ready"), 1)
                modulate_x(j + 2)
                dve.wait_ge(S_("down_full"), j + 1)
                dve.wait_ge(S_("y_sent"), j * 16 + 16)
                v.tensor_tensor(ysb[0:R, :], psD[:, :], g2row, ALU.mult).then_inc(S_("y_ready"), 1)
            for t in range(TL):
                dve.wait_ge(S_("y_back%d" % t), 32)
                step(v.scalar_tensor_tensor(xr[:, t, :], yback[:, t, :], share[:, 0, t:t + 1], xr[:, t, :],
                                            ALU.mult, ALU.add))
                v.scalar_tensor_tensor(xr[:, t, :], yback[:, TL + t, :], share[:, 1, t:t + 1], xr[:, t, :],
                                       ALU.mult, ALU.add).then_inc(S_("x2_ready"), 1)
            rstd(small[:, 24:24 + TL], small[:, 32:32 + TL], small[:, 40:40 + TL], small[:, 48:48 + TL], TL, D,
                 "x2_ss", TL, "x2_var", "x2_std")
            dve.wait_ge(S_("x2_rowed"), 2)
            v.tensor_scalar(yo[:, 0, :], yo[:, 0, :], small[:, 24:25], None, ALU.mult).then_inc(S_("out_ready"), 1)
            v.tensor_scalar(yo[:, 1, :], yo[:, 1, :], small[:, 25:26], None, ALU.mult).then_inc(S_("out_ready"), 1)

        @block.gpsimd
        def _(pool):
            R = ROWS_A_TILE
            pool.wait_ge(S_("zeros_made"), 1)
            pool.dma_start(slots.rearrange("(n p) d -> p n d", p=P),
                           zeros.unsqueeze(1).to_broadcast([P, XTILES * R // P, D])).then_inc(S_("x_zeroed"), 16)
            g_ = nc.gpsimd
            heads = lambda x: x.rearrange("p (h q) -> p h q", h=HPG)
            pool.wait_ge(S_("rows_in"), 16)
            pool.wait_ge(S_("steps_ready"), 1)
            for g in range(SG):
                for m in range(4):
                    pool.wait_ge(*is_free(("xtok", g, m, 1)))
                dsk = r_("ssd_d")[:, g * HPG:(g + 1) * HPG].unsqueeze(2).to_broadcast([P, HPG, SHD])

                def make_xw(d, i):
                    if i >= 2:
                        pool.wait_ge(*is_full(("kv", g, d, i - 2)))
                    elif g or d:
                        pool.wait_ge(*is_full(("kv", g if d else g - 1, 1 - d, 4)))
                    t = ORDER[d][i]
                    hs = d * SH + g * HPG
                    g_.tensor_tensor(heads(xw[i % 2]), heads(xtok[:, t, :]),
                                     wend[:, t, hs:hs + HPG].unsqueeze(2).to_broadcast([P, HPG, SHD]),
                                     ALU.mult).then_inc(S_("xw_ready"), 1)

                def make_xdt(d):
                    if g or d:
                        pool.wait_ge(*is_full(("y", g if d else g - 1, 1 - d)))
                    hs = d * SH + g * HPG
                    for c in range(TL):
                        ins = g_.tensor_tensor(heads(xdt[:, c, :]), heads(xtok[:, TC + c, :]),
                                               dt[:, TC + c, hs:hs + HPG].unsqueeze(2).to_broadcast([P, HPG, SHD]),
                                               ALU.mult)
                    ins.then_inc(S_("xdt_ready"), 1)

                make_xw(0, 0)
                make_xw(0, 1)
                if g:
                    pool.wait_ge(*is_full(("yT", g - 1, 3)))
                    pool.wait_ge(S_("yz_squared"), g * 4)
                for c in range(TL):
                    ins = g_.tensor_tensor(heads(yacc[:, c, :]), heads(xtok[:, TC + c, :]), dsk, ALU.mult)
                ins.then_inc(S_("y_started"), 1)
                for i in range(2, 5):
                    make_xw(0, i)
                make_xdt(0)
                make_xw(1, 0)
                make_xw(1, 1)
                pool.wait_ge(*is_free(("CB", g)))
                for d in range(2):
                    if d:
                        make_xdt(1)
                    for h in range(HPG):
                        n = (g * 2 + d) * HPG + h
                        pool.wait_ge(S_("decay_ready"), n + 1)
                        g_.tensor_tensor(mm[n % NM], mm[n % NM], cb[d], ALU.mult).then_inc(S_("M_ready"), 1)
                        if d == 0 and h + 2 < 5:
                            make_xw(1, h + 2)
            pool.wait_ge(S_("x_zeroed"), 16)
            pool.wait_ge(S_("slots_known"), 2)
            pool.wait_ge(S_("x1_normed"), TL)
            for i in range(2):
                for t in range(TL):
                    pool.indirect_dma_start(slots[:, :],
                                            bass.IndirectOffsetOnAxis(xidx[:, i * TL + t:i * TL + t + 1], 0),
                                            yo[:, t, :], None).then_inc(S_("x_sent"), 16)
            pool.wait_ge(S_("x_sent"), 16 * 2 * TL)
            pool.wait_ge(S_("x1_ss"), TL)
            pool.dma_start(xrow[0:R, :], slots[0:R, :]).then_inc(S_("xrow_in"), 16)
            pool.wait_ge(S_("y_ready"), 1)
            pool.dma_start(slots[0:R, :], ysb[0:R, :]).then_inc(S_("y_sent"), 16)
            pool.wait_ge(S_("x_turned"), 1)
            pool.dma_start(xrow[0:R, :], slots[R:2 * R, :]).then_inc(S_("xrow_in"), 16)
            n = pool.value_load(first_tile_i[0:1, NE:NE + 1], min_val=1, max_val=XTILES - 2)
            with pool.Fori(0, n) as j:
                pool.wait_ge(S_("x_turned"), j + 2)
                pool.dma_start(xrow[0:R, :], slots[bass.ds(j * R + 2 * R, R), :]).then_inc(S_("xrow_in"), 16)
                pool.wait_ge(S_("y_ready"), j + 2)
                pool.dma_start(slots[bass.ds(j * R, R), :], ysb[0:R, :]).then_inc(S_("y_sent"), 16)
            pool.wait_ge(S_("y_sent"), n * 16 + 16)
            pool.sem_inc(S_("pool_passed"), 1)
            for t in range(TL):
                for i in range(2):
                    pool.indirect_dma_start(yback[:, i * TL + t, :], None, slots[:, :],
                                            bass.IndirectOffsetOnAxis(xidx[:, i * TL + t:i * TL + t + 1], 0))\
                        .then_inc(S_("y_back%d" % t), 16)
            pool.wait_ge(S_("frow_in"), 16)
            for t in range(TL):
                pool.wait_ge(S_("x2_ready"), t + 1)
                g_.tensor_tensor(yo[:, t, :], xr[:, t, :], frow, ALU.mult).then_inc(S_("x2_rowed"), 1)
            pool.wait_ge(S_("xrow_in"), n * 16 + 32)


def grid_positions():
    t = np.arange(T)
    quarter = D // 4
    freqs = np.exp(-np.log(10000.0) * np.arange(quarter, dtype=np.float32) / quarter).astype(np.float32)
    ar = (t // GRID_W).astype(np.float32)[:, None] * freqs
    ac = (t % GRID_W).astype(np.float32)[:, None] * freqs
    return np.concatenate([np.sin(ar), np.cos(ar), np.sin(ac), np.cos(ac)], axis=-1).astype(np.float32)


def constants():
    i = np.arange(P)
    squares = np.concatenate([np.eye(P), i[:, None] <= i[None, :], i[:, None] >= i[None, :], np.ones((P, P))], axis=1)
    k = np.arange(T)
    h = np.arange(T // 2)
    time = np.concatenate([np.cos(2 * np.pi * np.outer(h, k) / T), np.sin(2 * np.pi * np.outer(h, k) / T)])
    time[T // 2] = np.cos(np.pi * k)
    ang = 2 * np.pi * np.outer(np.arange(FG), np.arange(FG)) / FG
    unit = 1.0 / np.sqrt(T * FG)
    return {
        "squares": squares.astype(np.float32),
        "sel": np.tile(np.eye(SH), (3, 1)).astype(np.float32),
        "pos": grid_positions(),
        "dft_time": time.astype(np.float32),
        "dft_cos": (unit * np.cos(ang)).astype(np.float32),
        "dft_sin": (-unit * np.sin(ang)).astype(np.float32),
    }


def kernel(**inputs):
    import concourse.bacc as bacc
    from concourse.bass_utils import run_bass_kernel_spmd

    v = {k: np.asarray(x) for k, x in inputs.items()}
    f = np.float32

    def blocks(x):
        return np.ascontiguousarray(x.reshape(-1, P).T)

    both = np.stack([v["c"][0].reshape(KD, P), v["c_ctx"].reshape(KD, P)], axis=1).reshape(2 * KD, P).T
    conv_w = v["ssd_conv_w"][0].T.reshape(SCD // P, P, SK).transpose(1, 0, 2).reshape(P, -1)
    cols = np.concatenate([both, blocks(v["ada_b"][0]), blocks(v["norm1_g"][0]), blocks(v["norm2_g"][0]),
                           blocks(v["gla_a_b"][0].reshape(-1)), blocks(v["gla_norm_g"][0]), conv_w,
                           blocks(v["ssd_conv_b"][0]), blocks(v["ssd_norm_g"][0])], axis=1)
    rows = np.concatenate([v["ssd_dt_bias"][0].reshape(-1), v["ssd_a_log"][0].reshape(-1), v["ssd_d"][0],
                           v["router_b"], np.arange(NE, 0, -1, dtype=f), np.arange(NG, 0, -1, dtype=f),
                           ROWS_A_TILE * np.arange(1, T // ROWS_A_TILE, dtype=f)])
    arrays = {"cols": cols, "rows": np.broadcast_to(rows, (P, NROW)), "final_row": np.broadcast_to(v["final_g"], (P, D))}
    gate_rows = np.concatenate([v["ada_b"][0][2 * D:3 * D], v["ada_b"][0][5 * D:6 * D]])
    arrays["gate_rows"] = np.broadcast_to(gate_rows, (P, 2 * D))
    arrays.update(constants())
    for name in ("x", "ctx", "ada_w", "w_in", "gla_a_w", "gla_proj", "fnet_proj", "ssd_proj", "w_out", "router_w",
                 "exp_w1", "exp_w3", "exp_w2"):
        arrays[name] = v[name]
    arrays = {k: np.ascontiguousarray(x) for k, x in arrays.items()}
    nc = bacc.Bacc("TRN2", target_bir_lowering=False, num_devices=1)
    aps = {k: nc.dram_tensor(f"{k}_d", x.shape, mybir.dt.from_np(x.dtype), kind="ExternalInput").ap()
           for k, x in arrays.items()}
    out = nc.dram_tensor("out_d", (1, T, D), F32, kind="ExternalOutput").ap()
    build(nc, aps, out)
    r = run_bass_kernel_spmd(nc, [{f"{k}_d": x for k, x in arrays.items()}], core_ids=[0])
    return r.results[0]["out_d"]
```
